# Optimizing a Trainium2 kernel written in Bass

```python
import math
import jax, jax.numpy as jnp
from jax import lax
import numpy as np

D_MODEL = 1024
BATCH = 1
SEQ = 4096
DEPTH = 1
DEC_BATCH = 8
DEC_SEQ = 8
PAST_LEN = 2048
PAGE_SIZE = 128

D_MIX = D_MODEL
D_LRU = 3 * D_MODEL // 8
LRU_BLOCKS = 6
LRU_BLOCK = D_LRU // LRU_BLOCKS
CONV_W = 4
RG_C = 8.0
D_SSM = D_MODEL // 4
SSM_GROUP = 16
SSM_GROUPS = D_SSM // SSM_GROUP
SSM_STATE = 64
D_ATT = D_MIX - D_LRU - D_SSM
HEAD_DIM = 64
N_HEADS = D_ATT // HEAD_DIM
DILATED = ((128, 1), (512, 4), (2048, 16))
WINDOW_MAX = 2048
D_IN = 2 * D_LRU + 2 * D_SSM + 4 * D_ATT
SPLITS = (D_LRU, 2 * D_LRU, 2 * D_LRU + D_SSM, 2 * D_LRU + 2 * D_SSM,
          2 * D_LRU + 2 * D_SSM + D_ATT, 2 * D_LRU + 2 * D_SSM + 2 * D_ATT,
          2 * D_LRU + 2 * D_SSM + 3 * D_ATT)
EPS = 1e-6
NEG_INF = -1e30

kernel_name = 'hymba_style_rglru_s5_dilated_decoder_step'

def rms_norm(x, g):
    xf = x.astype(jnp.float32)
    y = xf * lax.rsqrt(jnp.mean(xf * xf, axis=-1, keepdims=True) + EPS)
    return (y * g.astype(jnp.float32)).astype(x.dtype)

def alibi_slopes():
    h = jnp.arange(1, N_HEADS + 1, dtype=jnp.float32)
    return jnp.exp2(-8.0 * h / N_HEADS)

def causal_conv(xa, buf, w, b):
    xp = jnp.concatenate([buf.astype(xa.dtype), xa], axis=1)
    y = lax.conv_general_dilated(xp, w[:, None, :].astype(xa.dtype), window_strides=(1,),
                                 padding='VALID', dimension_numbers=('NWC', 'WIO', 'NWC'),
                                 feature_group_count=xa.shape[-1])
    return y + b.astype(xa.dtype), xp[:, -(CONV_W - 1):]

def rg_lru(xc, h0, w_r, b_r, w_i, b_i, lam, seq_start):
    f32 = jnp.float32
    n, t, c = xc.shape
    xf = xc.astype(f32)
    xb = xf.reshape(n, t, LRU_BLOCKS, LRU_BLOCK)
    r = jax.nn.sigmoid(jnp.einsum('ntki,kij->ntkj', xb, w_r.astype(f32)).reshape(n, t, c) + b_r.astype(f32))
    i = jax.nn.sigmoid(jnp.einsum('ntki,kij->ntkj', xb, w_i.astype(f32)).reshape(n, t, c) + b_i.astype(f32))
    log_a = -RG_C * r * jax.nn.softplus(-lam.astype(f32))
    a = jnp.exp(log_a)
    mult = jnp.sqrt(-jnp.expm1(2.0 * log_a))
    if seq_start:
        mult = mult.at[:, 0].set(1.0)
    bx = mult * i * xf
    bx = bx.at[:, 0].add(a[:, 0] * h0.astype(f32))

    def comb(lhs, rhs):
        a1, b1 = lhs
        a2, b2 = rhs
        return a1 * a2, a2 * b1 + b2

    _, h = lax.associative_scan(comb, (a, bx), axis=1)
    return h, h[:, -1]

def s5_ssm(u, s0_re, s0_im, lam_re, lam_im, log_dt, b_re, b_im, c_re, c_im, d):
    f32 = jnp.float32
    n, t, _ = u.shape
    uf = u.astype(f32).reshape(n, t, SSM_GROUPS, SSM_GROUP)
    dt = jnp.exp(log_dt.astype(f32))
    lr, li = lam_re.astype(f32), lam_im.astype(f32)
    mag = jnp.exp(lr * dt)
    ang = li * dt
    ab_re, ab_im = mag * jnp.cos(ang), mag * jnp.sin(ang)
    den = lr * lr + li * li
    xr, yi = ab_re - 1.0, ab_im
    coef_re = (xr * lr + yi * li) / den
    coef_im = (yi * lr - xr * li) / den
    br, bi = b_re.astype(f32), b_im.astype(f32)
    bb_re = coef_re[..., None] * br - coef_im[..., None] * bi
    bb_im = coef_re[..., None] * bi + coef_im[..., None] * br
    bu_re = jnp.einsum('ntgc,gpc->ntgp', uf, bb_re)
    bu_im = jnp.einsum('ntgc,gpc->ntgp', uf, bb_im)
    s0r, s0i = s0_re.astype(f32), s0_im.astype(f32)
    bu_re = bu_re.at[:, 0].add(ab_re * s0r - ab_im * s0i)
    bu_im = bu_im.at[:, 0].add(ab_re * s0i + ab_im * s0r)
    a_re = jnp.broadcast_to(ab_re, bu_re.shape)
    a_im = jnp.broadcast_to(ab_im, bu_im.shape)

    def comb(lhs, rhs):
        ar1, ai1, br1, bi1 = lhs
        ar2, ai2, br2, bi2 = rhs
        return (ar2 * ar1 - ai2 * ai1, ar2 * ai1 + ai2 * ar1,
                ar2 * br1 - ai2 * bi1 + br2, ar2 * bi1 + ai2 * br1 + bi2)

    _, _, x_re, x_im = lax.associative_scan(comb, (a_re, a_im, bu_re, bu_im), axis=1)
    y = (jnp.einsum('ntgp,gcp->ntgc', x_re, c_re.astype(f32))
         - jnp.einsum('ntgp,gcp->ntgc', x_im, c_im.astype(f32)))
    y = y + d.astype(f32).reshape(SSM_GROUPS, SSM_GROUP) * uf
    return y.reshape(n, t, D_SSM), x_re[:, -1], x_im[:, -1]

def dilated_attn_prompt(q, k, v, window, dil, slopes):
    f32 = jnp.float32
    bsz, s, h, dh = q.shape
    jw = window // dil
    ln = s // dil
    nb = -(-ln // jw)
    lp = nb * jw

    def blocks(z):
        z = z.reshape(bsz, ln, dil, h, dh)
        z = jnp.pad(z, ((0, 0), (0, lp - ln), (0, 0), (0, 0), (0, 0)))
        return z.reshape(bsz, nb, jw, dil, h, dh)

    def with_prev(z):
        prev = jnp.pad(z[:, :-1], ((0, 0), (1, 0), (0, 0), (0, 0), (0, 0), (0, 0)))
        return jnp.concatenate([prev, z], axis=2)

    qb = blocks(q)
    kk, vv = with_prev(blocks(k)), with_prev(blocks(v))
    sc = jnp.einsum('bnqchd,bnkchd->bnchqk', qb, kk, preferred_element_type=f32)
    iq = jnp.arange(jw)[:, None]
    jk = jnp.arange(2 * jw)[None, :]
    delta = iq - jk + jw
    nblk = jnp.arange(nb)[:, None, None]
    valid = (delta >= 0) & (delta <= jw) & (nblk * jw - jw + jk >= 0)
    sc = sc - slopes[:, None, None] * (delta * dil).astype(f32)
    sc = jnp.where(valid[None, :, None, None], sc, NEG_INF)
    m = jnp.max(sc, axis=-1, keepdims=True)
    p = jnp.exp(sc - m)
    den = jnp.sum(p, axis=-1, keepdims=True)
    lse = (m + jnp.log(den))[..., 0]
    o = jnp.einsum('bnchqk,bnkchd->bnqchd', (p / den).astype(v.dtype), vv,
                   preferred_element_type=f32)
    o = o.reshape(bsz, lp, dil, h, dh)[:, :ln].reshape(bsz, s, h, dh)
    lse = jnp.transpose(lse, (0, 1, 4, 2, 3)).reshape(bsz, lp, dil, h)[:, :ln].reshape(bsz, s, h)
    return o, lse

def dilated_attn_sample(q, k_all, v_all, n_past, window, dil, slopes):
    f32 = jnp.float32
    t = q.shape[1]
    jw = window // dil
    dist = dil * jnp.arange(jw + 1)
    idx = n_past + jnp.arange(t)[:, None] - dist[None, :]
    valid = idx >= 0
    idx_c = jnp.maximum(idx, 0)
    kg = k_all[:, idx_c]
    vg = v_all[:, idx_c]
    sc = jnp.einsum('nthd,ntjhd->nthj', q, kg, preferred_element_type=f32)
    sc = sc - slopes[:, None] * dist.astype(f32)[None, :]
    sc = jnp.where(valid[None, :, None, :], sc, NEG_INF)
    m = jnp.max(sc, axis=-1, keepdims=True)
    p = jnp.exp(sc - m)
    den = jnp.sum(p, axis=-1, keepdims=True)
    lse = (m + jnp.log(den))[..., 0]
    o = jnp.einsum('nthj,ntjhd->nthd', (p / den).astype(vg.dtype), vg, preferred_element_type=f32)
    return o, lse

def combine_dilations(outs):
    w = jax.nn.softmax(jnp.stack([l for _, l in outs], axis=0), axis=0)
    o = w[0][..., None] * outs[0][0]
    for i in range(1, len(outs)):
        o = o + w[i][..., None] * outs[i][0]
    return o

def mixer_layer(x, p, seq_start, conv_buf, h0, s0_re, s0_im, k_past, v_past):
    n, t, _ = x.shape
    hN = rms_norm(x, p['norm_g'])
    z = hN @ p['w_in']
    xa, ga, u, gb, q, k, v, gc = jnp.split(z, SPLITS, axis=-1)
    xc, conv_new = causal_conv(xa, conv_buf, p['conv_w'], p['conv_b'])
    ha, h_last = rg_lru(xc, h0, p['w_r'], p['b_r'], p['w_i'], p['b_i'], p['lru_lambda'], seq_start)
    ya = ha.astype(x.dtype) * jax.nn.silu(ga)
    yb, s_re, s_im = s5_ssm(u, s0_re, s0_im, p['lam_re'], p['lam_im'], p['log_dt'],
                            p['b_re'], p['b_im'], p['c_re'], p['c_im'], p['d'])
    yb = jax.nn.gelu(yb)
    yb = yb * jax.nn.sigmoid(yb @ p['glu_w'].astype(jnp.float32) + p['glu_b'].astype(jnp.float32))
    yb = yb.astype(x.dtype) * jax.nn.silu(gb)
    q = rms_norm(q.reshape(n, t, N_HEADS, HEAD_DIM), p['q_g']) * (HEAD_DIM ** -0.5)
    k = rms_norm(k.reshape(n, t, N_HEADS, HEAD_DIM), p['k_g'])
    v = v.reshape(n, t, N_HEADS, HEAD_DIM)
    slopes = alibi_slopes()
    if k_past is None:
        outs = [dilated_attn_prompt(q, k, v, w, dl, slopes) for w, dl in DILATED]
        keep = min(WINDOW_MAX, t)
        k_rows, v_rows = k[:, -keep:], v[:, -keep:]
    else:
        n_past = k_past.shape[1]
        k_all = jnp.concatenate([k_past.astype(k.dtype), k], axis=1)
        v_all = jnp.concatenate([v_past.astype(v.dtype), v], axis=1)
        outs = [dilated_attn_sample(q, k_all, v_all, n_past, w, dl, slopes) for w, dl in DILATED]
        k_rows, v_rows = k, v
    yc = combine_dilations(outs).reshape(n, t, D_ATT).astype(x.dtype) * jax.nn.silu(gc)
    og = p['out_g']
    y = jnp.concatenate([rms_norm(ya, og[:D_LRU]),
                         rms_norm(yb, og[D_LRU:D_LRU + D_SSM]),
                         rms_norm(yc, og[D_LRU + D_SSM:])], axis=-1)
    x = x + y @ p['w_out']
    return x, (conv_new, h_last, s_re, s_im, k_rows, v_rows)

def setup_inputs(seed: int = 0) -> dict:
    key = jax.random.key(seed)
    ks = jax.random.split(key, 32)
    f32 = jnp.float32
    n_buf = min(WINDOW_MAX, PAST_LEN)

    def nrm(k, shape, s):
        return s * jax.random.normal(k, shape, f32)

    u_a = jax.random.uniform(ks[16], (DEPTH, D_LRU), f32, 0.9, 0.999)
    sig = u_a ** (1.0 / RG_C)
    lru_lambda = jnp.log(sig) - jnp.log1p(-sig)
    n_idx = jnp.arange(SSM_STATE, dtype=f32)
    lam_re = -0.5 * jnp.exp(nrm(ks[17], (DEPTH, SSM_GROUPS, SSM_STATE), 0.05))
    lam_im = math.pi * n_idx + nrm(ks[18], (DEPTH, SSM_GROUPS, SSM_STATE), 0.05)
    log_dt = jax.random.uniform(ks[19], (DEPTH, SSM_GROUPS, SSM_STATE), f32,
                                math.log(1e-3), math.log(1e-1))
    return {
        'x_prompt': nrm(ks[0], (BATCH, SEQ, D_MODEL), 1.0),
        'x_sample': nrm(ks[1], (DEC_BATCH, DEC_SEQ, D_MODEL), 1.0),
        'state_conv': nrm(ks[2], (DEPTH, DEC_BATCH, CONV_W - 1, D_LRU), 1.0),
        'state_lru': nrm(ks[3], (DEPTH, DEC_BATCH, D_LRU), 0.5),
        'state_ssm_re': nrm(ks[4], (DEPTH, DEC_BATCH, SSM_GROUPS, SSM_STATE), 0.1),
        'state_ssm_im': nrm(ks[5], (DEPTH, DEC_BATCH, SSM_GROUPS, SSM_STATE), 0.1),
        'cache_k': nrm(ks[6], (DEPTH, DEC_BATCH, n_buf, N_HEADS, HEAD_DIM), 1.0),
        'cache_v': nrm(ks[7], (DEPTH, DEC_BATCH, n_buf, N_HEADS, HEAD_DIM), 1.0),
        'norm_g': 1.0 + nrm(ks[8], (DEPTH, D_MODEL), 0.05),
        'w_in': nrm(ks[9], (DEPTH, D_MODEL, D_IN), D_MODEL ** -0.5),
        'conv_w': nrm(ks[10], (DEPTH, CONV_W, D_LRU), CONV_W ** -0.5),
        'conv_b': nrm(ks[11], (DEPTH, D_LRU), 0.02),
        'w_r': nrm(ks[12], (DEPTH, LRU_BLOCKS, LRU_BLOCK, LRU_BLOCK), LRU_BLOCK ** -0.5),
        'b_r': nrm(ks[13], (DEPTH, D_LRU), 0.02),
        'w_i': nrm(ks[14], (DEPTH, LRU_BLOCKS, LRU_BLOCK, LRU_BLOCK), LRU_BLOCK ** -0.5),
        'b_i': nrm(ks[15], (DEPTH, D_LRU), 0.02),
        'lru_lambda': lru_lambda,
        'ssm_lambda_re': lam_re,
        'ssm_lambda_im': lam_im,
        'ssm_log_dt': log_dt,
        'ssm_b_re': nrm(ks[20], (DEPTH, SSM_GROUPS, SSM_STATE, SSM_GROUP), (2 * SSM_GROUP) ** -0.5),
        'ssm_b_im': nrm(ks[21], (DEPTH, SSM_GROUPS, SSM_STATE, SSM_GROUP), (2 * SSM_GROUP) ** -0.5),
        'ssm_c_re': nrm(ks[22], (DEPTH, SSM_GROUPS, SSM_GROUP, SSM_STATE), SSM_STATE ** -0.5),
        'ssm_c_im': nrm(ks[23], (DEPTH, SSM_GROUPS, SSM_GROUP, SSM_STATE), SSM_STATE ** -0.5),
        'ssm_d': nrm(ks[24], (DEPTH, D_SSM), 1.0),
        'glu_w': nrm(ks[25], (DEPTH, D_SSM, D_SSM), D_SSM ** -0.5),
        'glu_b': nrm(ks[26], (DEPTH, D_SSM), 0.02),
        'q_norm_g': 1.0 + nrm(ks[27], (DEPTH, HEAD_DIM), 0.05),
        'k_norm_g': 1.0 + nrm(ks[28], (DEPTH, HEAD_DIM), 0.05),
        'out_norm_g': 1.0 + nrm(ks[29], (DEPTH, D_MIX), 0.05),
        'w_out': nrm(ks[30], (DEPTH, D_MIX, D_MODEL), 0.5 * D_MIX ** -0.5),
    }

def reference(x_prompt, x_sample, state_conv, state_lru, state_ssm_re, state_ssm_im, cache_k, cache_v,
              norm_g, w_in, conv_w, conv_b, w_r, b_r, w_i, b_i, lru_lambda,
              ssm_lambda_re, ssm_lambda_im, ssm_log_dt, ssm_b_re, ssm_b_im, ssm_c_re, ssm_c_im,
              ssm_d, glu_w, glu_b, q_norm_g, k_norm_g, out_norm_g, w_out):
    xp, xs = x_prompt, x_sample
    bp = xp.shape[0]
    zero_conv = jnp.zeros((bp, CONV_W - 1, D_LRU), xp.dtype)
    zero_h = jnp.zeros((bp, D_LRU), jnp.float32)
    zero_s = jnp.zeros((bp, SSM_GROUPS, SSM_STATE), jnp.float32)
    sp_list, ss_list = [], []
    for l in range(DEPTH):
        p = dict(norm_g=norm_g[l], w_in=w_in[l], conv_w=conv_w[l], conv_b=conv_b[l],
                 w_r=w_r[l], b_r=b_r[l], w_i=w_i[l], b_i=b_i[l], lru_lambda=lru_lambda[l],
                 lam_re=ssm_lambda_re[l], lam_im=ssm_lambda_im[l], log_dt=ssm_log_dt[l],
                 b_re=ssm_b_re[l], b_im=ssm_b_im[l], c_re=ssm_c_re[l], c_im=ssm_c_im[l],
                 d=ssm_d[l], glu_w=glu_w[l], glu_b=glu_b[l], q_g=q_norm_g[l], k_g=k_norm_g[l],
                 out_g=out_norm_g[l], w_out=w_out[l])
        xp, sp = mixer_layer(xp, p, True, zero_conv, zero_h, zero_s, zero_s, None, None)
        xs, ss = mixer_layer(xs, p, False, state_conv[l], state_lru[l], state_ssm_re[l],
                             state_ssm_im[l], cache_k[l], cache_v[l])
        sp_list.append(sp)
        ss_list.append(ss)
    conv_p = jnp.stack([s[0] for s in sp_list], axis=0)
    lru_p = jnp.stack([s[1] for s in sp_list], axis=0)
    ssm_re_p = jnp.stack([s[2] for s in sp_list], axis=0)
    ssm_im_p = jnp.stack([s[3] for s in sp_list], axis=0)
    k_p = jnp.stack([s[4] for s in sp_list], axis=0)
    v_p = jnp.stack([s[5] for s in sp_list], axis=0)
    conv_s = jnp.stack([s[0] for s in ss_list], axis=0)
    lru_s = jnp.stack([s[1] for s in ss_list], axis=0)
    ssm_re_s = jnp.stack([s[2] for s in ss_list], axis=0)
    ssm_im_s = jnp.stack([s[3] for s in ss_list], axis=0)
    k_s = jnp.stack([s[4] for s in ss_list], axis=0)
    v_s = jnp.stack([s[5] for s in ss_list], axis=0)
    return (xp, xs, conv_p, lru_p, ssm_re_p, ssm_im_p, k_p, v_p,
            conv_s, lru_s, ssm_re_s, ssm_im_s, k_s, v_s)


_drawn_inputs = setup_inputs


def setup_inputs(seed=0):
    import zlib

    import numpy as np

    out = dict(_drawn_inputs(seed))
    spreads = {}
    factors = {'b_r': 8.0, 'b_i': 8.0, 'glu_b': 33.946, 'q_norm_g': 5.557}
    for name, (base, spread) in spreads.items():
        noise = np.random.default_rng([zlib.crc32(name.encode()), seed]).standard_normal(out[name].shape)
        drawn = base * np.exp(spread * noise) if base else spread * noise
        out[name] = __import__('jax').numpy.asarray(drawn.astype(out[name].dtype))
    for name, factor in factors.items():
        out[name] = (out[name] * factor).astype(out[name].dtype)
    return out
```

```python
from contextlib import ExitStack

import numpy as np

import concourse.bass as bass
from concourse import mybir

F32 = mybir.dt.float32
F32R = mybir.dt.float32r
ALU = mybir.AluOpType
ACT = mybir.ActivationFunctionType
AX = mybir.AxisListType
ds = bass.ds

P = 128
D = 1024
KT = D // P
SEQ = 4096
NS, TS = 8, 8
SMP = NS * TS
PAST = 2048
D_LRU, D_SSM, D_ATT = 384, 256, 384
HEADS, DH = 6, 64
PAIRS = HEADS // 2
LT = D_LRU // P
CONV_W = 4
GROUPS, GC, STATE = 16, 16, 64
CH = 8
EPS = 1e-6
NEG = -1e30
LEVELS = ((128, 1), (512, 4), (2048, 16))
KEEP = 2048
D_A = 4 * D_ATT
D_R = 2 * D_LRU + 2 * D_SSM
RG_C = 8.0


def peeled(eng, n, body, lead=1, tail=1):
    for i in range(lead):
        body(i, i == 0, False)
    with eng.Fori(lead, n - tail, 1) as i:
        body(i, False, False)
    for i in range(n - tail, n):
        body(i, False, i == n - 1)


def hold(eng, keep, sem, value):
    if not isinstance(value, int):
        value = eng.to_reg(value)
        eng.wait_ge(keep["loaded"], 16)
    eng.wait_ge(sem, value)


class Frame:

    def __init__(self, nc, ctx):
        self.nc, self.ctx, self.sems = nc, ctx, []
        ctx.callback(self.release)

    def release(self):
        self.nc.clear_and_free_semaphores(self.sems)
        self.nc.all_engine_barrier()

    def sb(self, name, shape, dt=F32):
        return self.ctx.enter_context(self.nc.sbuf_tensor(name, shape, dt))

    def ps(self, name, shape, dt=F32):
        return self.ctx.enter_context(self.nc.psum_tensor(name, shape, dt))

    def sem(self, name):
        self.sems.append(self.nc.alloc_semaphore(name))
        return self.sems[-1]


TB = 256
NB = SEQ // TB
SUB = TB // P


def project_attention(nc, top, t, keep):
    with ExitStack() as ctx:
        f = Frame(nc, ctx)
        w_hi = f.sb("wa_hi", [P, KT, D_A], F32R)
        w_lo = f.sb("wa_lo", [P, KT, D_A], F32R)
        w_raw = f.sb("wa_raw", [P, 2, D_A])
        gain = f.sb("wa_gain", [P, KT])
        x_raw = f.sb("xa_raw", [P, 2, KT, TB])
        x_hi = f.sb("xa_hi", [P, 2, KT, TB], F32R)
        x_lo = f.sb("xa_lo", [P, 2, KT, TB], F32R)
        x_tok = f.sb("x_tok", [P, SUB, D])
        sq_sum = f.sb("sq_sum", [P, 2, SUB])
        rs = f.sb("rs_a", [P, 2, SUB])
        z = f.sb("z_a", [P, 2, D_A])
        qk_n = f.sb("qk_n", [P, 2, 2 * D_ATT])
        ss = f.sb("qk_ss", [P, 2, 2 * HEADS])
        qkT = f.sb("qkT_stage", [P, 2, 2 * PAIRS, P])
        z_ps = f.ps("z_ps", [P, 2, 3, 512])
        t_ps = f.ps("t_ps", [P, 2, 512])
        gains = keep["qk_gain"]

        gain_loaded, tok_loaded = f.sem("gain_loaded"), f.sem("tok_loaded")
        w_loaded = [f.sem(f"wa_loaded{j}") for j in range(2)]
        x_loaded = [f.sem(f"xa_loaded{j}") for j in range(2)]
        w_scaled, w_hi_done, w_split = f.sem("wa_scaled"), f.sem("wa_hi_done"), f.sem("wa_split")
        x_hi_done, x_split = f.sem("xa_hi_done"), f.sem("xa_split")
        squared, rs_done, rs_root = f.sem("squared"), f.sem("rs_done"), f.sem("rs_root")
        z_done, z_out = f.sem("z_done"), f.sem("z_out")
        qk_ss_done, qk_root, qk_normed = f.sem("qk_ss_done"), f.sem("qk_root"), f.sem("qk_normed")
        turned, turned_out = f.sem("turned"), f.sem("turned_out")
        vg_stored = [f.sem(f"vg_stored{j}") for j in range(2)]
        kn_stored = [f.sem(f"kn_stored{j}") for j in range(2)]
        qkT_stored = [f.sem(f"qkT_stored{j}") for j in range(2)]
        outs_copied = f.sem("outs_copied")
        dve, rs_ready = f.sem("dve_a"), f.sem("rs_ready")
        rs_keep = keep["rs"]
        block = ctx.enter_context(nc.Block())
        NT = SEQ // P

        @block.sync
        def _(sp):
            sp.dma_start(gain[:], t["norm_g"]).then_inc(gain_loaded, 16)
            for k in range(KT):
                if k >= 2:
                    hold(sp, keep, w_hi_done, k - 1)
                    hold(sp, keep, w_split, k - 1)
                sp.dma_start(w_raw[:, k % 2], t["w_att"][:, k]).then_inc(w_loaded[k % 2], 16)

            def store(tile, s, at, rows):
                hold(sp, keep, z_out, tile + 1)
                sp.dma_start(t["v_all"][at, :], z[0:rows, s, 2 * D_ATT:3 * D_ATT]).then_inc(vg_stored[s], 16)
                sp.dma_start(t["gc_all"][at, :], z[0:rows, s, 3 * D_ATT:]).then_inc(vg_stored[s], 16)
                hold(sp, keep, qk_normed, tile + 1)
                sp.dma_start(t["k_all"][at, :], qk_n[0:rows, s, D_ATT:]).then_inc(kn_stored[s], 16)

            def store_turned(tile, b, at, rows):
                hold(sp, keep, turned_out, tile + 1)
                sp.dma_start(t["qkT_all"][:, :, at], qkT[:, b, :, 0:rows]).then_inc(qkT_stored[b], 16)

            def stores(blk, first):
                for s in range(SUB):
                    tile = blk * SUB + s
                    store(tile, s, ds(tile * P, P), P)
                    if not (first and s == 0):
                        store_turned(tile - 1, (s + 1) % 2, ds((tile - 1) * P, P), P)

            def body(i, first, last):
                for j in range(2):
                    if not first:
                        hold(sp, keep, x_split, 2 * i + j - 1)
                        hold(sp, keep, x_hi_done, 2 * i + j - 1)
                    sp.dma_start(x_raw[:, j], t["xT_p"][:, :, ds((2 * i + j) * TB, TB)]).then_inc(x_loaded[j], 16)
                    if not (first and j == 0):
                        hold(sp, keep, squared, SUB * (2 * i + j))
                    src = t["x_p"].rearrange("(n p) d -> p n d", p=P)
                    sp.dma_start(x_tok[:], src[:, ds((2 * i + j) * SUB, SUB)]).then_inc(tok_loaded, 16)
                    if not (first and j == 0):
                        stores(2 * i + j - 1, first)
            peeled(sp, NB // 2, body)
            hold(sp, keep, x_split, NB - 1)
            sp.dma_start(x_raw[:, 0, :, 0:SMP], t["xT_s"]).then_inc(x_loaded[0], 16)
            hold(sp, keep, squared, SUB * NB)
            sp.dma_start(x_tok[0:SMP, 0], t["x_s"]).then_inc(tok_loaded, 16)
            stores(NB - 1, False)
            store(NT, 0, slice(SEQ, SEQ + SMP), SMP)
            store_turned(NT - 1, 1, slice(SEQ - P, SEQ), P)
            store_turned(NT, 0, slice(SEQ, SEQ + SMP), SMP)
            for s, n in ((0, NT // 2 + 1), (1, NT // 2)):
                sp.wait_ge(vg_stored[s], 32 * n)
                sp.wait_ge(kn_stored[s], 16 * n)
                sp.wait_ge(qkT_stored[s], 16 * n)
            sp.dma_start(t["k_p"], t["k_all"][SEQ - KEEP:SEQ, :]).then_inc(outs_copied, 16)
            sp.dma_start(t["v_p"], t["v_all"][SEQ - KEEP:SEQ, :]).then_inc(outs_copied, 16)
            sp.dma_start(t["k_s"], t["k_all"][SEQ:SEQ + SMP, :]).then_inc(outs_copied, 16)
            sp.dma_start(t["v_s"], t["v_all"][SEQ:SEQ + SMP, :]).then_inc(outs_copied, 16)
            sp.wait_ge(outs_copied, 64)

        @block.tensor
        def _(pe):
            def products(tile, j, s, rows, free_count):
                b = s % 2
                if free_count is not None:
                    pe.wait_ge(z_out, free_count)
                for c in range(3):
                    for k in range(KT):
                        xh = x_hi[:, j, k, s * P:s * P + rows]
                        xl = x_lo[:, j, k, s * P:s * P + rows]
                        out = z_ps[0:rows, b, c]
                        cols = slice(c * 512, c * 512 + 512)
                        pe.matmul(out, xh, w_hi[:, k, cols], start=(k == 0), stop=False)
                        pe.matmul(out, xh, w_lo[:, k, cols], start=False, stop=False)
                        last = pe.matmul(out, xl, w_hi[:, k, cols], start=False, stop=(k == KT - 1))
                last.then_inc(z_done, 1)

            def turn(tile, b, rows, free_count):
                pe.wait_ge(qk_normed, tile + 1)
                if free_count is not None:
                    pe.wait_ge(turned_out, free_count)
                for c in range(2 * PAIRS):
                    last = pe.transpose(t_ps[:, c // 3, (c % 3) * P:(c % 3) * P + rows],
                                        qk_n[0:rows, b, c * P:(c + 1) * P], keep["ident"][0:rows, 0:rows])
                last.then_inc(turned, 1)

            pe.wait_ge(w_split, KT)

            def body(i, first, last):
                for j in range(2):
                    pe.wait_ge(x_split, 2 * i + j + 1)
                    for s in range(SUB):
                        tile = (2 * i + j) * SUB + s
                        early = first and j == 0
                        products(tile, j, s, P, None if early else tile - 1)
                        if not (early and s == 0):
                            turn(tile - 1, (s + 1) % 2, P, None if (early and s == 1) else tile - 1)
            peeled(pe, NB // 2, body)
            pe.wait_ge(x_split, NB + 1)
            products(NT, 0, 0, SMP, NT - 1)
            turn(NT - 1, 1, P, NT - 1)
            turn(NT, 0, SMP, NT)

        @block.scalar
        def _(act):
            for k in range(KT):
                act.wait_ge(w_scaled, k + 1)
                act.activation(w_hi[:, k], w_raw[:, k % 2], ACT.Copy).then_inc(w_hi_done, 1)

            def split(nth, j, n):
                act.wait_ge(x_loaded[j], (nth + 1) * 16)
                act.activation(x_hi[:, j, :, 0:n], x_raw[:, j, :, 0:n], ACT.Copy).then_inc(x_hi_done, 1)

            def squares(blk, j, tiles, rows):
                act.wait_ge(tok_loaded, (blk + 1) * 16)
                for s in range(tiles):
                    act.activation(x_tok[0:rows, s], x_tok[0:rows, s], ACT.Square,
                                   accum_out=sq_sum[0:rows, j, s:s + 1]).then_inc(squared, 1)

            def copy_out(tile, j, s, rows):
                act.wait_ge(z_done, tile + 1)
                for c in range(3):
                    last = act.activation(z[0:rows, s, c * 512:c * 512 + 512], z_ps[0:rows, s, c], ACT.Copy,
                                          scale=rs[0:rows, j, s:s + 1])
                last.then_inc(z_out, 1)

            def qk_sqrt(tile, s, rows):
                act.wait_ge(qk_ss_done, tile + 1)
                act.activation(ss[0:rows, s], ss[0:rows, s], ACT.Sqrt).then_inc(qk_root, 1)

            def sqrt_rs(blk, j, rows, tiles):
                act.wait_ge(rs_done, blk + 1)
                act.activation(sq_sum[0:rows, j, 0:tiles], sq_sum[0:rows, j, 0:tiles], ACT.Sqrt).then_inc(rs_root, 1)

            def body(i, first, last):
                for j in range(2):
                    blk = 2 * i + j
                    early = first and j == 0
                    squares(blk, j, SUB, P)
                    sqrt_rs(blk, j, P, SUB)
                    act.wait_ge(rs_ready, blk + 1)
                    for s in range(SUB):
                        tile = blk * SUB + s
                        if not early:
                            act.wait_ge(vg_stored[s], 32 * blk)
                            act.wait_ge(qk_normed, tile - 1)
                        if s == 0:
                            if not early:
                                act.wait_ge(z_done, blk * SUB)
                            split(i + j, (j + 1) % 2, SMP if last and j else TB)
                        copy_out(tile, j, s, P)
                        qk_sqrt(tile, s, P)

            split(0, 0, TB)
            peeled(act, NB // 2, body)
            squares(NB, 0, 1, SMP)
            sqrt_rs(NB, 0, SMP, 1)
            act.wait_ge(rs_ready, NB + 1)
            act.wait_ge(vg_stored[0], 32 * NB)
            act.wait_ge(qk_normed, NT - 1)
            copy_out(NT, 0, 0, SMP)
            qk_sqrt(NT, 0, SMP)

        @block.vector
        def _(v):
            v.wait_ge(gain_loaded, 16)
            for k in range(KT):
                v.wait_ge(w_loaded[k % 2], 16 * (k // 2 + 1))
                v.tensor_scalar(w_raw[:, k % 2], w_raw[:, k % 2], gain[:, k:k + 1], None, ALU.mult).then_inc(w_scaled, 1)
                v.wait_ge(w_hi_done, k + 1)
                v.tensor_tensor(w_lo[:, k], w_raw[:, k % 2], w_hi[:, k].bitcast(F32), ALU.subtract).then_inc(w_split, 1)

            def lows(blk, j, n):
                v.wait_ge(x_hi_done, blk + 1)
                v.tensor_tensor(x_lo[:, j, :, 0:n], x_raw[:, j, :, 0:n], x_hi[:, j, :, 0:n].bitcast(F32),
                                ALU.subtract).then_inc(x_split, 1)

            def inv_rms(blk, j, rows, tiles, col):
                v.wait_ge(squared, blk * SUB + tiles)
                v.tensor_scalar(sq_sum[0:rows, j, 0:tiles], sq_sum[0:rows, j, 0:tiles], 1.0 / D, EPS,
                                ALU.mult, ALU.add).then_inc(rs_done, 1)
                v.wait_ge(rs_root, blk + 1)
                v.reciprocal(rs[0:rows, j, 0:tiles], sq_sum[0:rows, j, 0:tiles]).then_inc(rs_ready, 1)
                v.wait_ge(rs_ready, blk + 1)
                v.tensor_copy(rs_keep[0:rows, col], rs[0:rows, j, 0:tiles])

            def qk_norm(tile, s, rows, n):
                v.wait_ge(z_out, tile + 1)
                if n is not None:
                    v.wait_ge(turned, tile - 1)
                    v.wait_ge(kn_stored[s], 16 * n)
                qk = z[0:rows, s, 0:2 * D_ATT]
                out = qk_n[0:rows, s]
                v.tensor_tensor(out, qk, qk, ALU.mult).then_inc(dve, 1)
                v.wait_ge(dve, 4 * tile + 1)
                v.tensor_reduce(ss[0:rows, s], out.rearrange("p (h d) -> p h d", d=DH), AX.X, ALU.add).then_inc(dve, 1)
                v.wait_ge(dve, 4 * tile + 2)
                v.tensor_scalar(ss[0:rows, s], ss[0:rows, s], 1.0 / DH, EPS, ALU.mult, ALU.add).then_inc(qk_ss_done, 1)
                v.wait_ge(qk_root, tile + 1)
                v.reciprocal(ss[0:rows, s], ss[0:rows, s]).then_inc(dve, 1)
                v.wait_ge(dve, 4 * tile + 3)
                r = ss[0:rows, s].rearrange("p (h o) -> p h o", o=1).broadcast_to([rows, 2 * HEADS, DH])
                v.tensor_tensor(out.rearrange("p (h d) -> p h d", d=DH), qk.rearrange("p (h d) -> p h d", d=DH), r,
                                ALU.mult).then_inc(dve, 1)
                v.wait_ge(dve, 4 * tile + 4)
                v.tensor_tensor(out, out, gains[0:rows], ALU.mult).then_inc(qk_normed, 1)

            def turned_copy(tile, b, rows, n):
                v.wait_ge(turned, tile + 1)
                if n is not None:
                    v.wait_ge(qkT_stored[b], 16 * n)
                for c in range(2):
                    last = v.tensor_copy(qkT[:, b, 3 * c:3 * c + 3, 0:rows],
                                         t_ps[:, c, 0:3 * P].rearrange("p (c t) -> p c t", c=3)[:, :, 0:rows])
                last.then_inc(turned_out, 1)

            def body(i, first, last):
                for j in range(2):
                    blk = 2 * i + j
                    early = first and j == 0
                    inv_rms(blk, j, P, SUB, ds(blk * SUB, SUB))
                    for s in range(SUB):
                        tile = blk * SUB + s
                        if s == 0:
                            if not early:
                                v.wait_ge(z_done, blk * SUB)
                            lows(blk + 1, (j + 1) % 2, SMP if last and j else TB)
                        qk_norm(tile, s, P, None if early else blk)
                        if not (early and s == 0):
                            turned_copy(tile - 1, (s + 1) % 2, P, None if early or (first and s == 0) else blk - 1 + s)
            lows(0, 0, TB)
            peeled(v, NB // 2, body)
            inv_rms(NB, 0, SMP, 1, slice(NT, NT + 1))
            qk_norm(NT, 0, SMP, NB)
            turned_copy(NT - 1, 1, P, NB - 1)
            turned_copy(NT, 0, SMP, NB)



def project_recurrent(nc, top, t, keep):
    with ExitStack() as ctx:
        f = Frame(nc, ctx)
        w_hi = f.sb("wr_hi", [P, KT, D_R], F32R)
        w_lo = f.sb("wr_lo", [P, KT, D_R], F32R)
        gain = f.sb("wr_gain", [P, KT])
        x_raw = f.sb("xr_raw", [P, 2, KT * TB])
        x_hi = f.sb("xr_hi", [P, 2, KT, TB], F32R)
        x_lo = f.sb("xr_lo", [P, 2, KT, TB], F32R)
        ones = f.sb("ones_r", [P, P])
        rs_wide = f.sb("rs_wide", [P, SUB, P])
        rs_row = f.sb("rs_row", [P, 2, TB])
        xa = f.sb("xa", [P, 2, LT, CONV_W - 1 + TB])
        xc = f.sb("xc", [P, 2, LT, TB])
        g = f.sb("ga", [P, 2, LT, TB])
        sg = f.sb("sg", [P, 2, LT, TB])
        r = f.sb("r", [P, LT, TB])
        ig = f.sb("ig", [P, LT, TB])
        q = f.sb("q", [P, LT, TB])
        y = f.sb("ya", [P, 2, LT, TB])
        inv = f.sb("inv_a", [P, TB])
        ug = f.sb("ug", [P, SUB, 2 * D_SSM])
        cw = f.sb("cw", [P, LT, CONV_W])
        vec = f.sb("lru_vec", [P, 5, LT])
        wg = f.sb("wg", [P, 2, LT, P])
        lam = f.sb("lam", [P, 3, LT])
        carry = f.sb("h_carry", [P, LT])
        eps = f.sb("eps_r", [P, 1])
        conv_s = f.sb("conv_s_in", [P, LT, NS, 3])
        h_s = f.sb("h_s_in", [P, LT, NS])
        xs = f.sb("xa_s", [P, LT, NS, 3 + TS])

        ch_ps = f.ps("ch_ps", [P, LT, 512])
        tok_ps = f.ps("tok_ps", [P, SUB, 512])
        gate_ps = f.ps("gate_ps", [P, 2, 512])
        row_ps = f.ps("row_ps", [P, 512])

        gain_loaded = f.sem("gainr_loaded")
        w_loaded = [f.sem(f"wr_loaded{j}") for j in range(2)]
        x_loaded = [f.sem(f"xr_loaded{j}") for j in range(2)]
        w_scaled, w_hi_done, w_split = f.sem("wr_scaled"), f.sem("wr_hi_done"), f.sem("wr_split")
        x_scaled, x_hi_done, x_split = f.sem("xr_scaled"), f.sem("xr_hi_done"), f.sem("xr_split")
        rs_spread, rs_turned, rs_copied = f.sem("rs_spread"), f.sem("rs_turned"), f.sem("rs_copied")
        ch_done, xa_out, ga_out = f.sem("ch_done"), f.sem("xa_out"), f.sem("ga_out")
        tok_done, tok_out = f.sem("tok_done"), f.sem("tok_out")
        ug_stored = [f.sem(f"ug_stored{j}") for j in range(SUB)]
        y_stored = [f.sem(f"ya_stored{j}") for j in range(2)]
        silu_sig, conv_done, gates_done, gates_out = f.sem("silu_sig"), f.sem("conv_done"), f.sem("gates_done"), f.sem("gates_out")
        tanh_done, root_done, squared = f.sem("tanh_done"), f.sem("root_done"), f.sem("ya_squared")
        ss_done, ss_root, y_done = f.sem("ss_done"), f.sem("ss_root"), f.sem("ya_done")
        lru, conv, setup, setup_act = f.sem("lru_step"), f.sem("conv_step"), f.sem("lru_setup"), f.sem("lru_setup_act")
        ini, state_out = f.sem("lru_inputs"), f.sem("state_out")
        samp, samp2, inv_done, carried = f.sem("r_out"), f.sem("once_step"), f.sem("inv_done"), f.sem("carried")
        block = ctx.enter_context(nc.Block())
        x_raw4 = x_raw.rearrange("p j (k n) -> p j k n", k=KT)
        NLRU = 9 * LT
        L_ADD, L_REC, L_MUL, L_A, L_I, L_X, L_SCAN, L_G, L_Y = range(9)

        def lru_count(b, step, ch):
            return NLRU * b + LT * step + ch + 1

        @block.sync
        def _(sp):
            sp.dma_start(gain[:], t["norm_g"]).then_inc(gain_loaded, 16)
            for k in range(KT):
                if k >= 2:
                    sp.wait_ge(w_hi_done, k - 1)
                    sp.wait_ge(w_split, k - 1)
                sp.dma_start(x_raw[:, k % 2, 0:D_R], t["w_rec"][:, k]).then_inc(w_loaded[k % 2], 16)
                if k == 0:
                    sp.dma_start(cw[:], t["conv_w"]).then_inc(ini, 16)
                    sp.dma_start(vec[:], t["lru_vec"]).then_inc(ini, 16)
                    sp.dma_start(conv_s[:], t["state_conv"]).then_inc(ini, 16)
                    sp.dma_start(h_s[:], t["state_lru"]).then_inc(ini, 16)
                    sp.wait_ge(setup, 1)
                    for n, name in enumerate(("w_r", "w_i")):
                        for b in range(6):
                            o = 64 * (b % 2)
                            sp.dma_start(wg[o:o + 64, n, b // 2, o:o + 64], t[name][b]).then_inc(ini, 16)

            def load(nth, j, at):
                if not (isinstance(nth, int) and nth == 0):
                    hold(sp, keep, x_split, 2 * nth + j - 1)
                sp.dma_start(x_raw4[:, j], t["xT_p"][:, :, ds(at, TB)]).then_inc(x_loaded[j], 16)

            def store_tokens(blk, s, at, rows):
                hold(sp, keep, tok_out, SUB * blk + s + 1)
                sp.dma_start(t["ug_all"][at, :], ug[0:rows, s]).then_inc(ug_stored[s], 16)

            def store_y(blk, j, at, n):
                hold(sp, keep, y_done, LT * (blk + 1))
                sp.dma_start(t["yaT_all"][:, :, at], y[:, j, :, 0:n]).then_inc(y_stored[j], 16)

            sp.wait_ge(w_split, KT)
            load(0, 0, 0)
            load(0, 1, TB)

            def body(i, first, last):
                for j in range(2):
                    b = 2 * i + j
                    if not last:
                        load(i + 1, j, (b + 2) * TB)
                    elif j == 0:
                        sp.wait_ge(x_split, NB - 1)
                        sp.dma_start(x_raw4[:, 0, :, 0:SMP], t["xT_s"]).then_inc(x_loaded[0], 16)
                    for s in range(SUB):
                        store_tokens(b, s, ds(b * TB + s * P, P), P)
                    if not first:
                        store_y(b - 2, j, ds((b - 2) * TB, TB), TB)
            peeled(sp, NB // 2, body, 2)
            store_tokens(NB, 0, slice(SEQ, SEQ + SMP), SMP)
            store_y(NB - 2, 0, ds((NB - 2) * TB, TB), TB)
            store_y(NB - 1, 1, ds((NB - 1) * TB, TB), TB)
            sp.dma_start(t["conv_p"], xa[:, 1, :, TB:]).then_inc(state_out, 16)
            sp.dma_start(t["lru_p"], carry[:]).then_inc(state_out, 16)
            store_y(NB, 0, slice(SEQ, SEQ + SMP), SMP)
            sp.wait_ge(samp2, 5)
            sp.dma_start(t["lru_s"], h_s[:]).then_inc(state_out, 16)
            for c in range(LT):
                sp.dma_start(t["conv_s"][:, c], xs[:, c, :, TS:]).then_inc(state_out, 16)
            sp.wait_ge(state_out, 48 + 16 * LT)
            sp.wait_ge(ug_stored[0], 16 * (NB + 1))
            sp.wait_ge(ug_stored[1], 16 * NB)
            sp.wait_ge(y_stored[0], 16 * (NB // 2 + 1))
            sp.wait_ge(y_stored[1], 16 * (NB // 2))

        @block.gpsimd
        def _(pool):
            nc.gpsimd.memset(wg[:], 0.0).then_inc(setup, 1)
            nc.gpsimd.memset(ones[:], 1.0).then_inc(setup, 1)
            nc.gpsimd.memset(eps[:], EPS).then_inc(setup, 1)

            def scale(b, nth, j, n):
                pool.wait_ge(x_loaded[j], 16 * (nth + 1))
                pool.wait_ge(rs_copied, b + 1)
                for k in range(KT):
                    last = nc.gpsimd.tensor_tensor(x_raw4[:, j, k, 0:n], x_raw4[:, j, k, 0:n], rs_row[:, j, 0:n], ALU.mult)
                last.then_inc(x_scaled, 1)
            scale(0, 0, 0, TB)

            def body(i, first, last):
                for j in range(2):
                    b = 2 * i + j
                    scale(b + 1, i + j, (j + 1) % 2, SMP if last and j else TB)
            peeled(pool, NB // 2, body, 2)

        @block.tensor
        def _(pe):
            def spread_rows(b, j, n):
                pe.wait_ge(rs_spread, b + 1)
                for s in range(-(-n // P)):
                    rows = min(P, n - s * P)
                    last = pe.matmul(row_ps[:, s * P:s * P + rows], rs_wide[0:rows, s, :],
                                     keep["ident"][0:rows, 0:rows], start=(s == 0), stop=True, skip_group_check=True)
                last.then_inc(rs_turned, 1)

            def channels(b, j, c, n):
                for k in range(KT):
                    out = ch_ps[:, c % LT, 0:n]
                    cols = slice(c * P, c * P + P)
                    pe.matmul(out, w_hi[:, k, cols], x_hi[:, j, k, 0:n], start=(k == 0), stop=False)
                    pe.matmul(out, w_hi[:, k, cols], x_lo[:, j, k, 0:n], start=False, stop=False)
                    last = pe.matmul(out, w_lo[:, k, cols], x_hi[:, j, k, 0:n], start=False, stop=(k == KT - 1))
                last.then_inc(ch_done, 1)

            def tokens(j, s, rows):
                for k in range(KT):
                    xh = x_hi[:, j, k, s * P:s * P + rows]
                    out = tok_ps[0:rows, s]
                    cols = slice(2 * D_LRU, D_R)
                    pe.matmul(out, xh, w_hi[:, k, cols], start=(k == 0), stop=False)
                    pe.matmul(out, xh, w_lo[:, k, cols], start=False, stop=False)
                    last = pe.matmul(out, x_lo[:, j, k, s * P:s * P + rows], w_hi[:, k, cols], start=False, stop=(k == KT - 1))
                last.then_inc(tok_done, 1)

            def gates(b, j, n):
                for c in range(LT):
                    pe.wait_ge(conv_done, LT * b + c + 1)
                    if not (isinstance(b, int) and b == 0 and c < 2):
                        pe.wait_ge(gates_out, LT * b + max(c - 1, 0))
                    for m in range(2):
                        last = pe.matmul(gate_ps[:, c % 2, m * TB:m * TB + n],
                                         wg[:, m, c], xc[:, j, c, 0:n], start=True, stop=True)
                    last.then_inc(gates_done, 1)

            def sum_squares(b, j, n):
                pe.wait_ge(squared, LT * (b + 1))
                for c in range(LT):
                    last = pe.matmul(row_ps[:, TB:TB + n], ones[:], sg[:, j, c, 0:n], start=(c == 0), stop=(c == LT - 1))
                last.then_inc(ss_done, 1)

            pe.wait_ge(setup, 3)
            pe.wait_ge(ini, 16 * 16)
            spread_rows(0, 0, TB)

            def main(b, j, n, first, last, is_first_block, tail):
                early = isinstance(b, int)
                pe.wait_ge(x_split, b + 1)
                for c in range(LT):
                    if not is_first_block:
                        pe.wait_ge(ga_out, LT * (b - 1) + c + 1)
                    channels(b, j, c, n)
                    if c == 0 and not tail:
                        if not (early and b < 3):
                            pe.wait_ge(ss_root, b - 2)
                        pe.wait_ge(rs_copied, b + 1)
                        spread_rows(b + 1, (j + 1) % 2, SMP if (last and j) else TB)
                if not (early and b < 2):
                    pe.wait_ge(rs_copied, min(b + 2, NB + 1) if early else b + 2)
                    sum_squares(b - 2, j, TB)
                if not is_first_block:
                    gates(b - 1, (j + 1) % 2, TB)
                for c in range(LT):
                    pe.wait_ge(xa_out, LT * b + c + 1)
                    channels(b, j, LT + c, n)
                for s in range(-(-n // P)):
                    if not is_first_block:
                        pe.wait_ge(tok_out, SUB * (b - 1) + s + 1)
                    tokens(j, s, min(P, n))

            def body(i, first, last):
                for j in range(2):
                    main(2 * i + j, j, TB, first, last, first and j == 0, False)
            peeled(pe, NB // 2, body, 2)
            main(NB, 0, SMP, False, True, False, True)
            pe.wait_ge(ss_root, NB - 1)
            sum_squares(NB - 1, 1, TB)
            gates(NB, 0, SMP)
            pe.wait_ge(ss_root, NB)
            sum_squares(NB, 0, SMP)

        @block.scalar
        def _(act):
            for k in range(KT):
                act.wait_ge(w_scaled, k + 1)
                act.activation(w_hi[:, k], x_raw[:, k % 2, 0:D_R], ACT.Copy).then_inc(w_hi_done, 1)
            act.wait_ge(ini, 16 * 16)
            act.activation(lam[:, 0], vec[:, 3], ACT.Abs).then_inc(setup_act, 1)
            act.wait_ge(setup_act, 1)
            act.activation(lam[:, 0], lam[:, 0], ACT.Exp, scale=-1.0).then_inc(setup_act, 1)
            act.wait_ge(setup_act, 2)
            act.activation(lam[:, 0], lam[:, 0], ACT.Ln, bias=1.0).then_inc(setup_act, 1)
            act.wait_ge(setup_act, 4)

            def copy_rows(b, j, n):
                act.wait_ge(rs_turned, b + 1)
                act.activation(rs_row[:, j, 0:n], row_ps[:, 0:n], ACT.Copy).then_inc(rs_copied, 1)

            def split(b, j, n):
                act.wait_ge(x_scaled, b + 1)
                act.activation(x_hi[:, j, :, 0:n], x_raw4[:, j, :, 0:n], ACT.Copy).then_inc(x_hi_done, 1)

            def gate_functions(b, j, n):
                for c in range(LT):
                    act.wait_ge(gates_done, LT * b + c + 1)
                    if not (isinstance(b, int) and b == 0):
                        act.wait_ge(lru, lru_count(b - 1, L_SCAN, c))
                    act.activation(r[:, c, 0:n], gate_ps[:, c % 2, 0:n], ACT.Sigmoid, bias=vec[:, 1, c:c + 1]).then_inc(samp, 1)
                    act.activation(ig[:, c, 0:n], gate_ps[:, c % 2, TB:TB + n], ACT.Sigmoid, bias=vec[:, 2, c:c + 1]).then_inc(gates_out, 1)
                for c in range(LT):
                    act.wait_ge(samp, LT * b + c + 1)
                    act.activation(r[:, c, 0:n], r[:, c, 0:n], ACT.Tanh, scale=lam[:, 1, c:c + 1]).then_inc(tanh_done, 1)

            def roots(b, j, n):
                for c in range(LT):
                    act.wait_ge(lru, lru_count(b, L_ADD, c))
                    act.activation(r[:, c, 0:n], r[:, c, 0:n], ACT.Sqrt).then_inc(root_done, 1)

            def squares(b, j, n):
                for c in range(LT):
                    act.wait_ge(lru, lru_count(b, L_Y, c))
                    act.activation(sg[:, j, c, 0:n], g[:, j, c, 0:n], ACT.Square).then_inc(squared, 1)

            def norm_root(b, n):
                act.wait_ge(ss_done, b + 1)
                if not (isinstance(b, int) and b == 0):
                    act.wait_ge(y_done, LT * b)
                act.activation(inv[:, 0:n], row_ps[:, TB:TB + n], ACT.Sqrt, scale=1.0 / D_LRU, bias=eps[:]).then_inc(ss_root, 1)

            copy_rows(0, 0, TB)
            split(0, 0, TB)

            def main(b, nth, j, n, is_first, second, last, tail):
                for c in range(LT):
                    act.wait_ge(ch_done, 2 * LT * b + c + 1)
                    if not (is_first or second):
                        act.wait_ge(conv_done, LT * (b - 1) + 1)
                    dst = xs[:, c, :, 3:] if tail else xa[:, j, c, CONV_W - 1:]
                    src = ch_ps[:, c, 0:n]
                    act.activation(dst, src.rearrange("p (n k) -> p n k", k=TS) if tail else src, ACT.Copy).then_inc(xa_out, 1)
                    if c == 0 and not tail:
                        copy_rows(b + 1, (j + 1) % 2, SMP if last and j else TB)
                if not (is_first or second):
                    squares(b - 2, j, TB)
                    norm_root(b - 2, TB)
                if not is_first:
                    gate_functions(b - 1, (j + 1) % 2, TB)
                if not tail:
                    if not is_first:
                        act.wait_ge(tok_done, SUB * b)
                    split(b + 1, (j + 1) % 2, SMP if last and j else TB)
                for c in range(LT):
                    act.wait_ge(ch_done, 2 * LT * b + LT + c + 1)
                    if not (is_first or second):
                        act.wait_ge(y_done, LT * (b - 2) + c + 1)
                    act.activation(g[:, j, c, 0:n], ch_ps[:, c, 0:n], ACT.Copy).then_inc(ga_out, 1)
                for c in range(LT):
                    act.wait_ge(ga_out, LT * b + c + 1)
                    if not (is_first or second):
                        act.wait_ge(ss_done, b - 1)
                    act.activation(sg[:, j, c, 0:n], g[:, j, c, 0:n], ACT.Sigmoid).then_inc(silu_sig, 1)
                if not is_first:
                    roots(b - 1, (j + 1) % 2, TB)
                for s in range(-(-n // P)):
                    rows = min(P, n)
                    act.wait_ge(tok_done, SUB * b + s + 1)
                    if not is_first:
                        act.wait_ge(ug_stored[s], 16 * b)
                    act.activation(ug[0:rows, s], tok_ps[0:rows, s], ACT.Copy).then_inc(tok_out, 1)

            def body(i, first, last):
                for j in range(2):
                    main(2 * i + j, i, j, TB, first and j == 0, first and j == 1, last, False)
            peeled(act, NB // 2, body, 2)
            main(NB, NB // 2, 0, SMP, False, False, True, True)
            squares(NB - 1, 1, TB)
            norm_root(NB - 1, TB)
            gate_functions(NB, 0, SMP)
            roots(NB, 0, SMP)
            squares(NB, 0, SMP)
            norm_root(NB, SMP)

        @block.vector
        def _(v):
            v.wait_ge(gain_loaded, 16)
            for k in range(KT):
                v.wait_ge(w_loaded[k % 2], 16 * (k // 2 + 1))
                stage = x_raw[:, k % 2, 0:D_R]
                v.tensor_scalar(stage, stage, gain[:, k:k + 1], None, ALU.mult).then_inc(w_scaled, 1)
                v.wait_ge(w_hi_done, k + 1)
                v.tensor_tensor(w_lo[:, k], stage, w_hi[:, k].bitcast(F32), ALU.subtract).then_inc(w_split, 1)
            v.wait_ge(ini, 16 * 16)
            v.wait_ge(setup_act, 3)
            v.tensor_scalar(lam[:, 2], vec[:, 3], -1.0, 0.0, ALU.mult, ALU.max).then_inc(conv, 1)
            v.wait_ge(conv, 1)
            v.tensor_tensor(lam[:, 2], lam[:, 2], lam[:, 0], ALU.add).then_inc(conv, 1)
            v.wait_ge(conv, 2)
            v.tensor_scalar(lam[:, 1], lam[:, 2], RG_C / 2, None, ALU.mult).then_inc(setup_act, 1)
            v.wait_ge(setup, 3)

            def spread(b, n, cols):
                if not (isinstance(b, int) and b == 0):
                    v.wait_ge(rs_turned, b)
                for s in range(-(-n // P)):
                    rows = min(P, n)
                    last = v.tensor_scalar(rs_wide[0:rows, s], ones[0:rows], keep["rs"][0:rows, cols(s)], None, ALU.mult)
                last.then_inc(rs_spread, 1)

            def lows(b, j, n):
                v.wait_ge(x_hi_done, b + 1)
                v.tensor_tensor(x_lo[:, j, :, 0:n], x_raw4[:, j, :, 0:n], x_hi[:, j, :, 0:n].bitcast(F32),
                                ALU.subtract).then_inc(x_split, 1)

            NCONV = 3 * LT + 1

            def convolve(b, nth, j, is_first, src, out):
                base = NCONV * b + 2
                if src is None:
                    v.wait_ge(xa_out, LT * (b + 1))
                    if is_first:
                        v.memset(xa[:, j, :, 0:CONV_W - 1], 0.0).then_inc(conv, 1)
                    else:
                        v.tensor_copy(xa[:, j, :, 0:CONV_W - 1], xa[:, (j + 1) % 2, :, TB:]).then_inc(conv, 1)
                    v.wait_ge(conv, base + 1)
                    src = lambda c, k: xa[:, j, c, k:k + TB]
                for c in range(LT):
                    v.tensor_scalar(out(c), src(c, 0), cw[:, c, 0:1], vec[:, 0, c:c + 1], ALU.mult, ALU.add).then_inc(conv, 1)
                for k in range(1, CONV_W):
                    for c in range(LT):
                        v.wait_ge(conv, base + 1 + LT * (k - 1) + c + 1)
                        v.scalar_tensor_tensor(out(c), src(c, k), cw[:, c, k:k + 1], out(c), ALU.mult,
                                               ALU.add).then_inc(conv if k < CONV_W - 1 else conv_done, 1)

            def recur(b, j, n, is_first, sample):
                def step(kind, op):
                    for c in range(LT):
                        if kind > 0:
                            v.wait_ge(lru, lru_count(b, kind - 1, c))
                        op(c).then_inc(lru, 1)

                R, Q, I = (lambda c: r[:, c, 0:n]), (lambda c: q[:, c, 0:n]), (lambda c: ig[:, c, 0:n])
                X, G, S = (lambda c: xc[:, j, c, 0:n]), (lambda c: g[:, j, c, 0:n]), (lambda c: sg[:, j, c, 0:n])
                v.wait_ge(tanh_done, LT * (b + 1))
                step(L_ADD, lambda c: v.tensor_scalar(Q(c), R(c), 1.0, None, ALU.add))
                step(L_REC, lambda c: v.reciprocal(Q(c), Q(c)))
                v.wait_ge(root_done, LT * (b + 1))
                step(L_MUL, lambda c: v.scalar_tensor_tensor(R(c), R(c), 2.0, Q(c), ALU.mult, ALU.mult))
                if is_first:
                    v.wait_ge(lru, lru_count(b, L_MUL, LT - 1))
                    v.memset(r[:, :, 0:1], 1.0).then_inc(samp2, 1)
                    v.wait_ge(samp2, 1)
                step(L_A, lambda c: v.tensor_scalar(Q(c), Q(c), 2.0, -1.0, ALU.mult, ALU.add))
                step(L_I, lambda c: v.tensor_tensor(R(c), R(c), I(c), ALU.mult))
                step(L_X, lambda c: v.tensor_tensor(R(c), R(c), X(c), ALU.mult))
                if sample:
                    v.wait_ge(lru, lru_count(b, L_X, LT - 1))
                    a0 = q[:, :, 0:n].rearrange("p c (n k) -> p c n k", k=TS)[:, :, :, 0]
                    x0 = r[:, :, 0:n].rearrange("p c (n k) -> p c n k", k=TS)[:, :, :, 0]
                    v.tensor_tensor(h_s[:], h_s[:], a0, ALU.mult).then_inc(samp2, 1)
                    v.wait_ge(samp2, 2)
                    v.tensor_tensor(x0, x0, h_s[:], ALU.add).then_inc(samp2, 1)
                    v.memset(a0, 0.0).then_inc(samp2, 1)
                    v.wait_ge(samp2, 4)
                if not (is_first or sample):
                    v.wait_ge(carried, b)
                step(L_SCAN, lambda c: v.tensor_tensor_scan(
                    X(c), Q(c), R(c), 0.0 if is_first or sample else carry[:, c:c + 1], ALU.mult, ALU.add))
                if not sample:
                    v.wait_ge(lru, lru_count(b, L_SCAN, LT - 1))
                    v.tensor_copy(carry[:], xc[:, j, :, TB - 1]).then_inc(carried, 1)
                v.wait_ge(silu_sig, LT * (b + 1))
                step(L_G, lambda c: v.tensor_tensor(G(c), G(c), S(c), ALU.mult))
                step(L_Y, lambda c: v.tensor_tensor(G(c), G(c), X(c), ALU.mult))

            def norm(b, nth, j, n):
                v.wait_ge(ss_root, b + 1)
                v.reciprocal(inv[:, 0:n], inv[:, 0:n]).then_inc(inv_done, 1)
                v.wait_ge(inv_done, b + 1)
                if not (isinstance(b, int) and b < 2):
                    v.wait_ge(y_stored[j], 16 * nth)
                for c in range(LT):
                    v.scalar_tensor_tensor(y[:, j, c, 0:n], g[:, j, c, 0:n], vec[:, 4, c:c + 1], inv[:, 0:n],
                                           ALU.mult, ALU.mult).then_inc(y_done, 1)

            spread(0, TB, lambda s: slice(s, s + 1))
            spread(1, TB, lambda s: slice(SUB + s, SUB + s + 1))
            lows(0, 0, TB)

            def main(b, nth, j, n, is_first, second, first, last):
                n1 = SMP if last and j else TB
                if not (is_first or second):
                    norm(b - 2, nth - 1, j, TB)
                convolve(b, nth, j, is_first, None, lambda c: xc[:, j, c])
                if not is_first:
                    v.wait_ge(tok_done, SUB * b)
                lows(b + 1, (j + 1) % 2, n1)
                if not (last and j):
                    spread(b + 2, SMP if last else TB, lambda s: ds((b + 2) * SUB + s, 1))
                if not is_first:
                    recur(b - 1, (j + 1) % 2, TB, second, False)

            def body(i, first, last):
                for j in range(2):
                    main(2 * i + j, i, j, TB, first and j == 0, first and j == 1, first, last)
            peeled(v, NB // 2, body, 2)
            norm(NB - 2, NB // 2 - 1, 0, TB)
            v.tensor_copy(xs[:, :, :, 0:3], conv_s[:]).then_inc(conv, 1)
            v.wait_ge(conv, NCONV * NB + 3)
            v.wait_ge(xa_out, LT * (NB + 1))
            convolve(NB, 0, 0, False, lambda c, k: xs[:, c, :, k:k + TS],
                     lambda c: xc[:, 0, c, 0:SMP].rearrange("p (n k) -> p n k", k=TS))
            recur(NB - 1, 1, TB, False, False)
            norm(NB - 1, NB // 2 - 1, 1, TB)
            recur(NB, 0, SMP, False, True)
            v.tensor_copy(h_s[:], xc[:, 0, :, 0:SMP].rearrange("p c (n k) -> p c n k", k=TS)[:, :, :, TS - 1]).then_inc(samp2, 1)
            norm(NB, NB // 2, 0, SMP)


UNROLL = 4
ROUNDS = SEQ // P // UNROLL
O_ROW = D_ATT + 2 * HEADS


class Tile:

    def __init__(self, level, i, s):
        dil = LEVELS[level][1]
        self.level, self.s, self.dil = level, s, dil
        self.u = ROUNDS * UNROLL * level + UNROLL * i + s
        self.nth = ROUNDS * level + i
        here = isinstance(i, int) and i == 0
        self.half = (here and s == 0, here, s % 2 == 0)[level]
        self.start = (P * UNROLL * i + P * s, P * dil * i + s, 2 * i + s // 2 + P * dil * (s % 2))[level]


def for_tiles(eng, visit):
    before = [None, None]
    for level in range(len(LEVELS)):
        lead = (1, 2, 1)[level]

        def body(i):
            for s in range(UNROLL):
                if s >= 2:
                    back = Tile(level, i, s - 2)
                elif isinstance(i, int) and i == 0:
                    back = before[s]
                else:
                    back = Tile(level, i - 1, s + 2)
                visit(Tile(level, i, s), back)
        for i in range(lead):
            body(i)
        with eng.Fori(lead, ROUNDS, 1) as i:
            body(i)
        before = [Tile(level, ROUNDS - 1, 2), Tile(level, ROUNDS - 1, 3)]
    for tile in before:
        visit(None, tile)


def attend(nc, top, t, keep):
    with ExitStack() as ctx:
        f = Frame(nc, ctx)
        qT = f.sb("qT", [P, PAIRS, SEQ])
        kT = f.sb("kT", [P, PAIRS, SEQ])
        bias = f.sb("bias", [P, len(LEVELS), HEADS, 2 * P])
        q = f.sb("q_tiles", [P, UNROLL, PAIRS, P])
        k = f.sb("k_tiles", [P, UNROLL, PAIRS, 2 * P])
        v = f.sb("v_tiles", [P, UNROLL, 2, D_ATT])
        p = f.sb("p", [P, 2, HEADS, 2 * P])
        pT = f.sb("pT", [P, HEADS, 2, P])
        o = f.sb("o", [P, UNROLL, O_ROW])
        s_ps = f.ps("s_ps", [P, 2, 1024])
        t_ps = f.ps("pT_ps", [P, PAIRS, 512])
        o_ps = f.ps("o_ps", [P, 512])
        qk_loaded = f.sem("qk_loaded")
        v_loaded = [f.sem(f"v_loaded{j}") for j in range(UNROLL)]
        o_stored = [f.sem(f"o_stored{j}") for j in range(UNROLL)]
        qk_copied = f.sem("qk_copied")
        s_done, scored, p_done = f.sem("s_done"), f.sem("scored"), f.sem("p_done")
        p_turned, pT_out, pv_done, o_out = f.sem("p_turned"), f.sem("pT_out"), f.sem("pv_done"), f.sem("o_out")
        block = ctx.enter_context(nc.Block())

        def keys(tile):
            n = P if tile.half else 2 * P
            return ds(tile.start - (0 if tile.half else P * tile.dil), n, step=tile.dil), n

        @block.sync
        def _(sp):
            for h in range(PAIRS):
                sp.dma_start(qT[:, h], t["qkT_all"][:, h, 0:SEQ]).then_inc(qk_loaded, 16)
                sp.dma_start(kT[:, h], t["qkT_all"][:, PAIRS + h, 0:SEQ]).then_inc(qk_loaded, 16)
            sp.dma_start(bias[:], t["bias_p"]).then_inc(qk_loaded, 16)

            def visit(tile, back):
                if tile is not None:
                    if not (isinstance(tile.nth, int) and tile.nth == 0):
                        hold(sp, keep, pv_done, tile.u - UNROLL + 1)
                    own = ds(tile.start, P, step=tile.dil)
                    if tile.half:
                        for c in range(2):
                            cols = slice(c * D_ATT // 2, (c + 1) * D_ATT // 2)
                            sp.dma_start(v[:, tile.s, 1, cols], t["v_all"][own, cols]).then_inc(v_loaded[tile.s], 16)
                    else:
                        prev = ds(tile.start - P * tile.dil, P, step=tile.dil)
                        sp.dma_start(v[:, tile.s, 0], t["v_all"][prev, :]).then_inc(v_loaded[tile.s], 16)
                        sp.dma_start(v[:, tile.s, 1], t["v_all"][own, :]).then_inc(v_loaded[tile.s], 16)
                if back is not None:
                    hold(sp, keep, o_out, back.u + 1)
                    sp.dma_start(t["o_all"][back.level][ds(back.start, P, step=back.dil), :],
                                 o[:, back.s]).then_inc(o_stored[back.s], 16)
            for_tiles(sp, visit)
            for s in range(UNROLL):
                sp.wait_ge(o_stored[s], 16 * ROUNDS * len(LEVELS))

        @block.gpsimd
        def _(pool):
            pool.wait_ge(qk_loaded, 16 * (2 * PAIRS + 1))

            def visit(tile, back):
                if tile is not None:
                    if not (isinstance(tile.nth, int) and tile.nth == 0):
                        pool.wait_ge(s_done, HEADS * (tile.u - UNROLL + 1))
                    nc.gpsimd.tensor_copy(q[:, tile.s], qT[:, :, ds(tile.start, P, step=tile.dil)])
                    at, n = keys(tile)
                    nc.gpsimd.tensor_copy(k[:, tile.s, :, 0:n], kT[:, :, at]).then_inc(qk_copied, 1)
            for_tiles(pool, visit)

        @block.tensor
        def _(pe):
            pe.wait_ge(qk_loaded, 16 * (2 * PAIRS + 1))

            def visit(tile, back):
                if back is not None:
                    pe.wait_ge(p_done, HEADS * (back.u + 1))
                    if not (isinstance(back.u, int) and back.u == 0):
                        pe.wait_ge(pT_out, PAIRS * back.u)
                    for h in range(HEADS):
                        for half in ((1,) if back.half else (0, 1)):
                            last = pe.transpose(t_ps[:, h // 2, ((h % 2) * 2 + half) * P:((h % 2) * 2 + half + 1) * P],
                                                p[:, back.s % 2, h, half * P:(half + 1) * P], keep["ident"][:])
                        if h % 2:
                            last.then_inc(p_turned, 1)
                if tile is not None:
                    _, n = keys(tile)
                    pe.wait_ge(qk_copied, tile.u + 1)
                    for h in range(HEADS):
                        if h in (0, 1, 4, 5) and not (isinstance(tile.u, int) and tile.u == 0):
                            pe.wait_ge(scored, HEADS * (tile.u - 1) + {0: 3, 1: 4, 4: 5, 5: 6}[h])
                        o64 = slice(DH * (h % 2), DH * (h % 2) + DH)
                        col = (h // 2) * 2 * P + 2 * P - n
                        pe.matmul(s_ps[:, h % 2, col:col + n], q[o64, tile.s, h // 2],
                                  k[o64, tile.s, h // 2, 0:n], start=True, stop=True).then_inc(s_done, 1)
                if back is not None:
                    pe.wait_ge(v_loaded[back.s], 32 * (back.nth + 1))
                    if not (isinstance(back.u, int) and back.u == 0):
                        pe.wait_ge(o_out, back.u)
                    for h in range(HEADS):
                        if h % 2 == 0:
                            pe.wait_ge(pT_out, PAIRS * back.u + h // 2 + 1)
                        for half in ((1,) if back.half else (0, 1)):
                            last = pe.matmul(o_ps[:, h * DH:(h + 1) * DH], pT[:, h, half],
                                             v[:, back.s, half, h * DH:(h + 1) * DH],
                                             start=(half == 1 if back.half else half == 0), stop=(half == 1))
                    last.then_inc(pv_done, 1)
            for_tiles(pe, visit)

        @block.vector
        def _(dve):
            def visit(tile, back):
                if back is not None:
                    if not (isinstance(back.u, int) and back.u == 0):
                        dve.wait_ge(pv_done, back.u)
                    for h in range(PAIRS):
                        dve.wait_ge(p_turned, PAIRS * back.u + h + 1)
                        src = t_ps[:, h].rearrange("p (e x q) -> p e x q", e=2, x=2)
                        dst = pT[:, 2 * h:2 * h + 2]
                        if back.half:
                            src, dst = src[:, :, 1], dst[:, :, 1]
                        dve.tensor_copy(dst, src).then_inc(pT_out, 1)
                if tile is not None:
                    _, n = keys(tile)
                    if not (isinstance(tile.nth, int) and tile.nth == 0):
                        dve.wait_ge(o_stored[tile.s], 16 * tile.nth)
                    for h in range(HEADS):
                        hold(dve, keep, s_done, HEADS * tile.u + {0: 3, 1: 4, 2: 4, 3: 4, 4: 5, 5: 6}[h])
                        col = (h // 2) * 2 * P + 2 * P - n
                        dve.tensor_tensor_reduce(
                            out=p[:, tile.s % 2, h, 2 * P - n:], in0=s_ps[:, h % 2, col:col + n],
                            in1=bias[:, tile.level, h, 2 * P - n:], scale=1.0, scalar=-NEG, op0=ALU.add, op1=ALU.min,
                            accum_out=o[:, tile.s, D_ATT + h:D_ATT + h + 1]).then_inc(scored, 1)
            for_tiles(dve, visit)

        @block.scalar
        def _(act):
            def visit(tile, back):
                if tile is not None:
                    _, n = keys(tile)
                    for h in range(HEADS):
                        act.wait_ge(scored, HEADS * tile.u + h + 1)
                        rows = p[:, tile.s % 2, h, 2 * P - n:]
                        act.activation(rows, rows, ACT.Exp, scale=-1.0, bias=o[:, tile.s, D_ATT + h:D_ATT + h + 1],
                                       accum_out=o[:, tile.s, D_ATT + HEADS + h:D_ATT + HEADS + h + 1]).then_inc(p_done, 1)
                if back is not None:
                    act.wait_ge(pv_done, back.u + 1)
                    act.activation(o[:, back.s, 0:D_ATT], o_ps[:, 0:D_ATT], ACT.Copy).then_inc(o_out, 1)
            for_tiles(act, visit)


KC = SEQ // CH
KTILES = KC // P
TA, TBL = 16, 32
TWO_PI_HI = 6.28125
TWO_PI_LO = 2 * np.pi - TWO_PI_HI
PRE_ANGLE, PRE = 56, 366
LN2_HI = 0.693359375
LN2_LO = float(np.log(2)) - LN2_HI
ROUND = 1.5 * 2.0 ** 23


def ssm(nc, top, t, keep):
    with ExitStack() as ctx:
        f = Frame(nc, ctx)
        par = f.sb("s_par", [P, 3, GROUPS])
        bc = f.sb("s_bc", [P, 4, GROUPS, GC])
        sign = f.sb("s_sign", [P, 1])
        turn_i = f.sb("s_turn", [P, P])
        dcol = f.sb("s_d", [P, GROUPS])
        v1 = f.sb("s_v1", [P, 12, GROUPS])
        i32 = f.sb("s_i32", [P, GROUPS], mybir.dt.int32)
        mag = f.sb("s_mag", [P, CH + 1, GROUPS])
        un = f.sb("s_un", [P, 2, CH + 1, GROUPS])
        pw = f.sb("s_pw", [P, 2, CH + 1, GROUPS])
        wk = f.sb("s_wk", [P, 2, GROUPS])
        tb = f.sb("s_tb", [P, 2, GROUPS, TBL])
        ta = f.sb("s_ta", [P, 2, GROUPS, TA])
        tab4 = f.sb("s_tab4", [P, 4, GROUPS, TA])
        x12 = f.sb("s_x12", [P, 2, GROUPS, GC])
        tmp = f.sb("s_tmp", [P, GROUPS, CH + 1, GC])
        wv = f.sb("s_wv", [P, 2, GROUPS, CH, GC])
        rr = f.sb("s_rr", [P, 2, GROUPS, CH + 1, GC])
        ug = f.sb("s_ug", [P, KTILES * CH + 1, D_SSM])
        ugs = f.sb("s_ugs", [NS, CH, D_SSM])
        yb = f.sb("s_yb", [P, KTILES * CH + 1, D_SSM])
        ybs = f.sb("s_ybs", [NS, CH, D_SSM])
        u_g = f.sb("s_u_g", [P, KTILES, CH, GC])
        us_g = f.sb("s_us_g", [NS, CH, GC])
        wv_g = f.sb("s_wv_g", [P, 2, CH * GC])
        xz = f.sb("s_xz", [P, 240])
        rz = f.sb("s_rz", [P, 240])
        rot = f.sb("s_rot", [P, 4, TA, TBL])
        lhs = f.sb("s_lhs", [P, 2, P])
        uT = f.sb("s_uT", [P, KC + NS])
        dm = f.sb("s_dm", [P, P])
        z1 = f.sb("s_z1", [P, KC])
        z2 = f.sb("s_z2", [P, KC])
        rho = f.sb("s_rho", [P, KC])
        h = f.sb("s_h", [P, 2, KC + 1])
        h_last = f.sb("s_h_last", [P, 2, GROUPS])
        x0 = f.sb("s_x0", [P, GROUPS, NS])
        x0i = f.sb("s_x0i", [P, GROUPS, NS])
        x1 = f.sb("s_x1", [P, GROUPS, NS])
        xe = f.sb("s_xe", [P, GROUPS])

        x0_g = f.sb("s_x0_g", [P, NS])
        last_h, x0_copied = f.sem("s_last_h"), f.sem("s_x0_copied")

        small_ps = f.ps("s_small", [P, 512])
        u_ps = f.ps("s_u_ps", [P, 512])
        us_ps = f.ps("s_us_ps", [P, 512])
        v_ps = f.ps("s_v_ps", [P, 2, 512])
        vs_ps = f.ps("s_vs_ps", [P, 512])
        y_ps = f.ps("s_y_ps", [P, 512])
        ys_ps = f.ps("s_ys_ps", [P, 512])

        loaded, pre, act_s, xi_done = f.sem("s_loaded"), f.sem("s_pre"), f.sem("s_act"), f.sem("s_xi")
        copied, zeroed, w_turned, lhs_out = f.sem("s_copied"), f.sem("s_zeroed"), f.sem("s_w_turned"), f.sem("s_lhs_out")
        u_turned, uT_out, v_done, rot_done = f.sem("s_u_turned"), f.sem("s_uT_out"), f.sem("s_v_done"), f.sem("s_rot_done")
        dm_done, dm_out, z_step, h_done = f.sem("s_dm_done"), f.sem("s_dm_out"), f.sem("s_z_step"), f.sem("s_h_done")
        y_done, y_out, us_done, rho_done = f.sem("s_y_done"), f.sem("s_y_out"), f.sem("s_us_done"), f.sem("s_rho_done")
        pool_s, last_done, state_out = f.sem("s_pool"), f.sem("s_last"), f.sem("s_state_out")
        inner = ExitStack()
        block = inner.enter_context(nc.Block())
        LOADS = 16 * 12
        NZ = 8

        @block.sync
        def _(sp):
            for dst, name in ((par, "ssm_par"), (bc, "ssm_bc"), (sign, "ssm_sign"), (turn_i, "ssm_turn"),
                              (dcol, "ssm_d"), (x0, "ssm_x0")):
                sp.dma_start(dst[:], t[name]).then_inc(loaded, 16)
            rows = t["ug_all"][0:SEQ, 0:D_SSM].rearrange("(a k c) e -> k a c e", k=P, c=CH)
            for a in range(KTILES):
                sp.dma_start(ug[:, a * CH:(a + 1) * CH], rows[:, a]).then_inc(loaded, 16)
            sp.dma_start(ugs[:], t["ug_all"][SEQ:SEQ + SMP, 0:D_SSM].rearrange("(n c) e -> n c e", c=CH)).then_inc(loaded, 16)
            sp.dma_start(rho[:], t["ones"]).then_inc(loaded, 16)
            sp.wait_ge(last_done, 2)
            for half, (a, b) in enumerate((("ssm_re_p", "ssm_re_s"), ("ssm_im_p", "ssm_im_s"))):
                at = slice(STATE * half, STATE * half + STATE)
                sp.dma_start(t[a], xe[at]).then_inc(state_out, 16)
                sp.dma_start(t[b], x1[at]).then_inc(state_out, 16)
            sp.wait_ge(y_out, 2 * GROUPS)
            sp.dma_start(t["ys_mid"].rearrange("(n c) e -> n c e", c=CH), ybs[:]).then_inc(state_out, 16)
            sp.wait_ge(state_out, 80)

        @block.gpsimd
        def _(pool):
            nc.gpsimd.memset(xz[:], 0.0).then_inc(zeroed, 1)
            nc.gpsimd.memset(rz[:], 0.0).then_inc(zeroed, 1)
            nc.gpsimd.memset(h[:, :, 0:1], 0.0).then_inc(zeroed, 1)
            pool.wait_ge(zeroed, 2)
            pool.wait_ge(loaded, LOADS)
            pool.wait_ge(pre, PRE)

            def body(g, first, last):
                if not first:
                    pool.wait_ge(u_turned, g)
                    pool.wait_ge(w_turned, g)
                    pool.wait_ge(dm_done, g)
                nc.gpsimd.tensor_copy(u_g[:], ug[:, 0:KTILES * CH].rearrange("p (a c) e -> p a c e", c=CH)[:, :, :, ds(g * GC, GC)])
                nc.gpsimd.tensor_copy(us_g[:], ugs[:, :, ds(g * GC, GC)])
                nc.gpsimd.tensor_copy(wv_g.rearrange("p x (c e) -> p x c e", c=CH), wv[:, :, g])
                nc.gpsimd.tensor_copy(xz[:, 112:128], x12[:, 0, g])
                nc.gpsimd.tensor_copy(rz[:, 112:240].rearrange("p (c e) -> p c e", c=CH), rr[:, 0, g, 0:CH]).then_inc(copied, 1)
                if not first:
                    pool.wait_ge(h_done, g)
                shape = [P, TA, TBL]
                A = lambda x: ta[:, x, g].rearrange("p (a o) -> p a o", o=1).broadcast_to(shape)
                B = lambda x: tb[:, x, g].rearrange("p (o b) -> p o b", o=1).broadcast_to(shape)
                for k, (x, y) in enumerate(((0, 0), (1, 0), (1, 1), (0, 1))):
                    last_op = nc.gpsimd.tensor_tensor(rot[:, k], A(x), B(y), ALU.mult).then_inc(pool_s, 1)
                pool.wait_ge(pool_s, 4 * g + 4)
                nc.gpsimd.tensor_tensor(rot[:, 0], rot[:, 0], rot[:, 2], ALU.subtract).then_inc(rot_done, 1)
                nc.gpsimd.tensor_tensor(rot[:, 1], rot[:, 1], rot[:, 3], ALU.add).then_inc(rot_done, 1)
            peeled(pool, GROUPS, body)

        @block.tensor
        def _(pe):
            pe.wait_ge(loaded, LOADS)
            pe.matmul(vs_ps[:, 0:GROUPS * NS], turn_i[:], x0[:], start=True, stop=True).then_inc(xi_done, 1)

            def body(g, first, last):
                pe.wait_ge(copied, g + 1)
                if not first:
                    pe.wait_ge(us_done, g)
                    pe.wait_ge(uT_out, g)
                for a in range(KTILES):
                    pe.transpose(u_ps[:, a * P:(a + 1) * P], u_g[:, a].rearrange("p c e -> p (c e)"), keep["ident"][:])
                pe.transpose(us_ps[:, 0:NS], us_g.rearrange("n c e -> n (c e)"), keep["ident"][0:NS, 0:NS]).then_inc(u_turned, 1)
                if not first:
                    pe.wait_ge(dm_out, g)
                for x in range(2):
                    w = pe.transpose(small_ps[:, x * P:(x + 1) * P], wv_g[:, x], keep["ident"][:])
                w.then_inc(w_turned, 1)
                pe.wait_ge(lhs_out, g + 1)
                for c in range(CH):
                    at = slice(112 - GC * c, 240 - GC * c)
                    m = pe.matmul(small_ps[:, 2 * P:3 * P], xz[:, at], rz[:, at], start=(c == 0), stop=(c == CH - 1))
                m.then_inc(dm_done, 1)
                pe.wait_ge(uT_out, g + 1)
                pe.wait_ge(us_done, g + 1)
                if not first:
                    pe.wait_ge(z_step, NZ * (g - 1) + 2)
                for x in range(2):
                    pe.matmul(v_ps[:, x], lhs[:, x], uT[:, 0:KC], start=True, stop=True).then_inc(v_done, 1)
                if first:
                    pe.wait_ge(last_done, 1)
                else:
                    pe.wait_ge(z_step, NZ * g)
                pe.matmul(vs_ps[:, 0:NS], lhs[:, 0], uT[:, KC:], start=True, stop=True).then_inc(v_done, 1)
                pe.wait_ge(h_done, g + 1)
                pe.wait_ge(dm_out, g + 1)
                if not first:
                    pe.wait_ge(y_out, 2 * g)
                for a in range(KTILES):
                    at, out = slice(a * P, (a + 1) * P), y_ps[:, a * P:(a + 1) * P]
                    pe.matmul(out, uT[:, at], dm[:], start=True, stop=False)
                    for x in range(2):
                        m = pe.matmul(out, h[:, x, at], rr[:, x, g, 1:].rearrange("p c e -> p (c e)"), start=False, stop=(x == 1))
                m.then_inc(y_done, 1)
                pe.wait_ge(x0_copied, g + 1)
                pe.matmul(ys_ps[0:NS, 0:P], uT[:, KC:], dm[:], start=True, stop=False)
                pe.matmul(ys_ps[0:NS, 0:P], x0_g[:], rr[:, 0, g, 1:].rearrange("p c e -> p (c e)"),
                          start=False, stop=True).then_inc(y_done, 1)
            peeled(pe, GROUPS, body)
            pe.wait_ge(last_h, GROUPS)
            pe.matmul(small_ps[:, 0:GROUPS], keep["ident"][:], h_last[:, 0], start=True, stop=False)
            pe.matmul(small_ps[:, 0:GROUPS], turn_i[:], h_last[:, 1], start=False, stop=True).then_inc(v_done, 1)

        @block.scalar
        def _(act):
            act.wait_ge(loaded, LOADS)
            count = [0]

            def step(op):
                count[0] += 1
                op.then_inc(act_s, 1)
            act.wait_ge(pre, PRE_ANGLE)
            step(act.activation(v1[:, 5], v1[:, 3], ACT.Sin))
            step(act.activation(v1[:, 6], v1[:, 3], ACT.Sin, scale=0.5))

            def body(g, first, last):
                act.wait_ge(w_turned, g + 1)
                if not first:
                    act.wait_ge(v_done, 3 * g)
                act.activation(lhs[:], small_ps[:, 0:2 * P].rearrange("p (x s) -> p x s", x=2), ACT.Copy).then_inc(lhs_out, 1)
                act.wait_ge(u_turned, g + 1)
                if not first:
                    act.wait_ge(y_done, 2 * g)
                act.activation(uT[:, 0:KC], u_ps[:], ACT.Copy).then_inc(uT_out, 1)
                act.activation(uT[:, KC:], us_ps[:, 0:NS], ACT.Copy).then_inc(us_done, 1)
                act.activation(x0_g[:], x0[:, g], ACT.Copy).then_inc(x0_copied, 1)
                act.wait_ge(y_done, 2 * g + 1)
                act.activation(yb[:, 0:KTILES * CH].rearrange("p (a c) e -> p a c e", c=CH)[:, :, :, ds(g * GC, GC)], y_ps.rearrange("p (a c e) -> p a c e", a=KTILES, c=CH),
                               ACT.Copy).then_inc(y_out, 1)
                act.wait_ge(y_done, 2 * g + 2)
                act.activation(ybs[:, :, ds(g * GC, GC)], ys_ps[0:NS, 0:P].rearrange("p (c e) -> p c e", c=CH),
                               ACT.Copy).then_inc(y_out, 1)
            peeled(act, GROUPS, body)

        @block.vector
        def _(v):
            v.wait_ge(loaded, LOADS)
            count = [0]

            def step(op):
                count[0] += 1
                op.then_inc(pre, 1)
                v.wait_ge(pre, count[0])

            def tt(out, a, b, op=ALU.mult):
                step(v.tensor_tensor(out, a, b, op))

            def ts(out, a, s1, s2, op0, op1=None):
                step(v.tensor_scalar(out, a, s1, s2, op0, op1) if op1 is not None else v.tensor_scalar(out, a, s1, None, op0))

            s = lambda n: v1[:, n]
            lr, li = par[:, 0], par[:, 1]

            def exp(out, x, n, y, i32):
                ts(y, x, 88.0, -87.0, ALU.min, ALU.max)
                ts(n, y, 1 / np.log(2), ROUND, ALU.mult, ALU.add)
                ts(n, n, ROUND, None, ALU.subtract)
                step(v.scalar_tensor_tensor(y, n, -LN2_HI, y, ALU.mult, ALU.add))
                step(v.scalar_tensor_tensor(y, n, -LN2_LO, y, ALU.mult, ALU.add))
                ts(n, n, 127.0, 2.0 ** 23, ALU.add, ALU.mult)
                step(v.tensor_copy(i32, n))
                ts(out, y, 1 / 5040, 1 / 720, ALU.mult, ALU.add)
                for k in (1 / 120, 1 / 24, 1 / 6, 1 / 2, 1.0, 1.0):
                    tt(out, out, y)
                    ts(out, out, k, None, ALU.add)
                tt(out, out, i32.bitcast(F32))
            exp(s(0), par[:, 2], s(5), s(6), i32[:])
            tt(s(1), lr, s(0))
            exp(mag[:, 1], s(1), s(5), s(6), i32[:])
            for n in range(2, CH + 1):
                tt(mag[:, n], mag[:, n // 2], mag[:, n - n // 2])
            tt(s(2), li, s(0))
            ts(s(3), s(2), 1 / (2 * np.pi), ROUND, ALU.mult, ALU.add)
            ts(s(3), s(3), ROUND, None, ALU.subtract)
            step(v.scalar_tensor_tensor(s(2), s(3), -TWO_PI_HI, s(2), ALU.mult, ALU.add))
            step(v.scalar_tensor_tensor(s(2), s(3), -TWO_PI_LO, s(2), ALU.mult, ALU.add))
            ts(s(3), s(2), 3.1415925, -3.1415925, ALU.min, ALU.max)
            assert count[0] == PRE_ANGLE
            v.wait_ge(act_s, 2)
            U = lambda x, n: un[:, x, n]

            def unit(r, i):
                tt(s(10), r, r)
                tt(s(11), i, i)
                tt(s(10), s(10), s(11), ALU.add)
                ts(s(10), s(10), -0.5, 1.5, ALU.mult, ALU.add)
                tt(r, r, s(10))
                tt(i, i, s(10))

            def square(r2, i2, r, i):
                tt(s(8), r, r)
                tt(s(9), i, i)
                step(v.scalar_tensor_tensor(s(11), r, 2.0, i, ALU.mult, ALU.mult))
                tt(r2, s(8), s(9), ALU.subtract)
                step(v.tensor_copy(i2, s(11)))
                unit(r2, i2)

            def product(outs, a, b, temps):
                tt(temps[0], a[0], b[0])
                tt(temps[1], a[1], b[1])
                tt(temps[2], a[0], b[1])
                tt(temps[3], a[1], b[0])
                tt(outs[0], temps[0], temps[1], ALU.subtract)
                tt(outs[1], temps[2], temps[3], ALU.add)

            step(v.memset(un[:, 0, 0], 1.0))
            step(v.memset(un[:, 1, 0], 0.0))
            step(v.memset(mag[:, 0], 1.0))
            step(v.tensor_copy(U(1, 1), s(5)))
            tt(s(7), s(6), s(6))
            ts(U(0, 1), s(7), -2.0, 1.0, ALU.mult, ALU.add)
            unit(U(0, 1), U(1, 1))
            square(U(0, 2), U(1, 2), U(0, 1), U(1, 1))
            product((U(0, 3), U(1, 3)), (U(0, 2), U(1, 2)), (U(0, 1), U(1, 1)), [s(n) for n in range(8, 12)])
            square(U(0, 4), U(1, 4), U(0, 2), U(1, 2))
            for n in (1, 2, 3):
                product((U(0, 4 + n), U(1, 4 + n)), (U(0, 4), U(1, 4)), (U(0, n), U(1, n)), [s(n) for n in range(8, 12)])
            square(U(0, 8), U(1, 8), U(0, 4), U(1, 4))
            for x in range(2):
                tt(pw[:, x], un[:, x], mag[:])
            tt(s(2), lr, lr)
            tt(s(3), li, li)
            tt(s(2), s(2), s(3), ALU.add)
            step(v.reciprocal(s(2), s(2)))
            ts(s(3), pw[:, 0, 1], -1.0, None, ALU.add)
            yi = pw[:, 1, 1]
            tt(s(4), s(3), lr)
            tt(s(5), yi, li)
            tt(s(4), s(4), s(5), ALU.add)
            tt(s(4), s(4), s(2))
            tt(s(5), yi, lr)
            tt(s(6), s(3), li)
            tt(s(5), s(5), s(6), ALU.subtract)
            tt(s(5), s(5), s(2))
            wide = lambda x: x.rearrange("p (g o) -> p g o", o=1).broadcast_to([P, GROUPS, GC])
            ts(bc[:, 1], bc[:, 1], sign[:], None, ALU.mult)
            ts(bc[:, 2], bc[:, 2], sign[:], -1.0, ALU.mult, ALU.mult)
            ts(bc[:, 3], bc[:, 3], -1.0, None, ALU.mult)
            small = tmp[:, :, 0]
            tt(x12[:, 0], bc[:, 0], wide(s(4)))
            tt(small, bc[:, 1], wide(s(5)))
            tt(x12[:, 0], x12[:, 0], small, ALU.add)
            tt(x12[:, 1], bc[:, 1], wide(s(4)))
            tt(small, bc[:, 0], wide(s(5)))
            tt(x12[:, 1], x12[:, 1], small, ALU.subtract)

            def over(x, n):
                return x.rearrange("p g (o c) -> p g o c", o=1).broadcast_to([P, GROUPS, n, GC])

            def powers(x, ns):
                w = pw[:, x].rearrange("p n (g o) -> p g n o", o=1)
                w = w[:, :, ns] if ns is not None else w
                return w.broadcast_to([P, GROUPS, w.shape[2], GC])
            for c in range(CH):
                n = slice(CH - 1 - c, CH - c)
                pr, pi = powers(0, n), powers(1, n)
                X1, X2 = over(x12[:, 0], 1), over(x12[:, 1], 1)
                w0, w1, one = wv[:, 0, :, c:c + 1], wv[:, 1, :, c:c + 1], tmp[:, :, 0:1]
                tt(w0, X1, pr)
                tt(one, X2, pi)
                tt(w0, w0, one, ALU.add)
                tt(w1, X1, pi)
                tt(one, X2, pr)
                tt(w1, w1, one, ALU.subtract)
            D1, D2 = over(bc[:, 2], CH + 1), over(bc[:, 3], CH + 1)
            pr, pi = powers(0, None), powers(1, None)
            tt(rr[:, 0], D1, pr)
            tt(tmp[:], D2, pi)
            tt(rr[:, 0], rr[:, 0], tmp[:], ALU.add)
            tt(rr[:, 1], D2, pr)
            tt(tmp[:], D1, pi)
            tt(rr[:, 1], rr[:, 1], tmp[:], ALU.subtract)
            for x in range(2):
                step(v.tensor_copy(wk[:, x], U(x, 8)))
            for table, size in ((tb, TBL), (ta, TA)):
                step(v.memset(table[:, 0, :, 0:1], 1.0))
                step(v.memset(table[:, 1, :, 0:1], 0.0))
                n = 1
                while n < size:
                    shape = [P, GROUPS, n]
                    w = [wk[:, x].rearrange("p (g o) -> p g o", o=1).broadcast_to(shape) for x in range(2)]
                    product([table[:, x, :, n:2 * n] for x in range(2)], [table[:, x, :, 0:n] for x in range(2)], w,
                            [tab4[:, k, :, 0:n] for k in range(4)])
                    square(wk[:, 0], wk[:, 1], wk[:, 0], wk[:, 1])
                    n *= 2
            v.wait_ge(xi_done, 1)
            step(v.tensor_copy(x0i[:], vs_ps[:, 0:GROUPS * NS].rearrange("p (g n) -> p g n", g=GROUPS)))
            states = lambda x: x.rearrange("p (g o) -> p g o", o=1).broadcast_to([P, GROUPS, NS])
            tt(x1[:], x0[:], states(pw[:, 0, CH]))
            tt(x0i[:], x0i[:], states(pw[:, 1, CH]))
            tt(x1[:], x1[:], x0i[:], ALU.add)
            v.tensor_copy(s(0), s(1)).then_inc(last_done, 1)
            assert count[0] == PRE, count[0]

            def body(g, first, last):
                rate = mag[:, CH, ds(g, 1)]
                cos, sin = rot[:, 0].rearrange("p a b -> p (a b)"), rot[:, 1].rearrange("p a b -> p (a b)")
                v.wait_ge(rot_done, 2 * g + 2)
                v.wait_ge(v_done, 3 * g + 1)
                v.tensor_tensor(z1[:], v_ps[:, 0], cos, ALU.mult).then_inc(z_step, 1)
                v.wait_ge(v_done, 3 * g + 2)
                v.tensor_tensor(z2[:], v_ps[:, 1], sin, ALU.mult).then_inc(z_step, 1)
                v.wait_ge(z_step, NZ * g + 2)
                v.tensor_tensor(z1[:], z1[:], z2[:], ALU.add).then_inc(z_step, 1)
                v.wait_ge(z_step, NZ * g + 3)
                v.tensor_scalar(z2[:], rho[:], rate, None, ALU.mult).then_inc(z_step, 1)
                v.wait_ge(z_step, NZ * g + 4)
                v.tensor_tensor_scan(z1[:], z2[:], z1[:], 0.0, ALU.mult, ALU.add).then_inc(z_step, 1)
                v.wait_ge(z_step, NZ * g + 5)
                if first:
                    v.wait_ge(zeroed, 3)
                else:
                    v.wait_ge(y_done, 2 * g)
                v.tensor_tensor(h[:, 0, 1:], z1[:], cos, ALU.mult).then_inc(z_step, 1)
                v.tensor_tensor(h[:, 1, 1:], z1[:], sin, ALU.mult).then_inc(h_done, 1)
                v.wait_ge(dm_done, g + 1)
                v.scalar_tensor_tensor(dm[:], keep["ident"][:], dcol[:, ds(g, 1)], small_ps[:, 2 * P:3 * P],
                                       ALU.mult, ALU.add).then_inc(dm_out, 1)
                v.wait_ge(z_step, NZ * g + 6)
                v.wait_ge(h_done, g + 1)
                v.tensor_copy(h_last[:, :, ds(g, 1)], h[:, :, KC:]).then_inc(last_h, 1)
                v.wait_ge(v_done, 3 * g + 3)
                v.tensor_tensor(x1[:, g], x1[:, g], vs_ps[:, 0:NS], ALU.add).then_inc(z_step, 2)
            peeled(v, GROUPS, body)
            v.wait_ge(v_done, 3 * GROUPS + 1)
            v.tensor_copy(xe[:], small_ps[:, 0:GROUPS]).then_inc(last_done, 1)

        inner.close()
        ssm_gate(nc, f, t, keep, yb, ug, v_ps, small_ps, u_ps)


def ssm_gate(nc, f, t, keep, yb, ug, v_ps, small_ps, u_ps):
    gb = ug
    nt = SEQ // P
    wide = f.sb("g_wide", [P, 2, D_SSM])
    w = f.sb("g_w", [P, 2, D_SSM])
    gl = f.sb("g_gl", [P, 2, 2, P])
    glT = f.sb("g_glT", [P, 2, 2, P])
    z = f.sb("g_z", [P, 2, D_SSM])
    sg = f.sb("g_sg", [P, D_SSM])
    sq = f.sb("g_sq", [P, D_SSM])
    ss = f.sb("g_ss", [P, nt + 1])
    rs = f.sb("g_rs", [P, nt + 1])
    eps = f.sb("g_eps", [P, 1])
    loaded, gelu_done, copied, turned = f.sem("g_loaded"), f.sem("g_gelu"), f.sem("g_copied"), f.sem("g_turned")
    glT_out, z_done, z_biased, z_sig = f.sem("g_glT_out"), f.sem("g_z_done"), f.sem("g_z_biased"), f.sem("g_z_sig")
    gb_sig, step, y_done, squared = f.sem("g_gb_sig"), f.sem("g_step"), f.sem("g_y_done"), f.sem("g_squared")
    set_up, rooted, inv, normed, stored = f.sem("g_set_up"), f.sem("g_rooted"), f.sem("g_inv"), f.sem("g_normed"), f.sem("g_stored")
    with nc.Block() as block:
        @block.sync
        def _(sp):
            sp.dma_start(wide[:], t["ssm_wide"].rearrange("(o n) e -> o n e", o=1).broadcast_to([P, 2, D_SSM])).then_inc(loaded, 16)
            sp.dma_start(w[:], t["glu_w"].rearrange("(a p) e -> p a e", p=P)).then_inc(loaded, 16)
            rows = t["ug_all"][0:SEQ, D_SSM:].rearrange("(a k c) e -> k a c e", k=P, c=CH)
            for a in range(KTILES):
                sp.dma_start(gb[:, a * CH:(a + 1) * CH], rows[:, a]).then_inc(loaded, 16)
            sp.dma_start(gb[0:SMP, nt], t["ug_all"][SEQ:SEQ + SMP, D_SSM:]).then_inc(loaded, 16)
            sp.dma_start(yb[0:SMP, nt], t["ys_mid"]).then_inc(loaded, 16)
            out = t["yb_all"][0:SEQ, :].rearrange("(a k c) e -> k a c e", k=P, c=CH)
            for a in range(KTILES):
                sp.wait_ge(normed, CH * (a + 1))
                sp.dma_start(out[:, a], yb[:, a * CH:(a + 1) * CH]).then_inc(stored, 16)
            sp.wait_ge(normed, nt + 1)
            sp.dma_start(t["yb_all"][SEQ:SEQ + SMP, :], yb[0:SMP, nt]).then_inc(stored, 16)
            sp.wait_ge(stored, 16 * (KTILES + 1))

        def tiles(eng, visit):
            def body(i, first, last):
                for j in range(2):
                    visit(2 * i + j, j, P, first)
            peeled(eng, nt // 2, body)
            visit(nt, 0, SMP, False)

        @block.gpsimd
        def _(pool):
            nc.gpsimd.memset(eps[:], EPS).then_inc(set_up, 1)
            pool.wait_ge(gelu_done, 2)

            def visit(n, j, rows, first):
                if not first:
                    pool.wait_ge(y_done, n - 1)
                nc.gpsimd.tensor_copy(gl[0:rows, j].rearrange("p a e -> p (a e)"), yb[0:rows, n]).then_inc(copied, 1)
            tiles(pool, visit)

        @block.tensor
        def _(pe):
            pe.wait_ge(loaded, 16 * 8)

            def visit(n, j, rows, first):
                pe.wait_ge(copied, n + 1)
                if not first:
                    pe.wait_ge(glT_out, n - 1)
                for a in range(2):
                    m = pe.transpose(turn_ps[j][:, a * P:a * P + rows], gl[0:rows, j, a], keep["ident"][0:rows, 0:rows])
                m.then_inc(turned, 1)
                pe.wait_ge(glT_out, n + 1)
                if not first:
                    pe.wait_ge(z_biased, n - 1)
                for a in range(2):
                    m = pe.matmul(v_ps[0:rows, j, 0:D_SSM], glT[:, j, a, 0:rows], w[:, a], start=(a == 0), stop=(a == 1))
                m.then_inc(z_done, 1)
            turn_ps = [small_ps, u_ps]
            tiles(pe, visit)

        @block.scalar
        def _(act):
            act.wait_ge(loaded, 16 * 8)
            act.wait_ge(set_up, 2)
            act.activation(yb[:, 0:nt], yb[:, 0:nt], ACT.Gelu_apprx_tanh).then_inc(gelu_done, 1)
            act.activation(yb[0:SMP, nt], yb[0:SMP, nt], ACT.Gelu_apprx_tanh).then_inc(gelu_done, 1)
            turn_ps = [small_ps, u_ps]

            def visit(n, j, rows, first):
                act.wait_ge(turned, n + 1)
                if not first:
                    act.wait_ge(z_done, n - 1)
                act.activation(glT[:, j, :, 0:rows], turn_ps[j][:, 0:2 * P].rearrange("p (a t) -> p a t", a=2)[:, :, 0:rows],
                               ACT.Copy).then_inc(glT_out, 1)
                act.wait_ge(z_biased, n + 1)
                act.activation(z[0:rows, j], z[0:rows, j], ACT.Sigmoid).then_inc(z_sig, 1)
                if not (first and j == 0):
                    act.wait_ge(y_done, n)
                act.activation(sg[0:rows], gb[0:rows, n], ACT.Sigmoid).then_inc(gb_sig, 1)
                act.wait_ge(y_done, n + 1)
                if not (first and j == 0):
                    act.wait_ge(squared, n)
                act.activation(sq[0:rows], yb[0:rows, n], ACT.Square, accum_out=ss[0:rows, ds(n, 1)]).then_inc(squared, 1)
            tiles(act, visit)
            act.wait_ge(squared, nt + 1)
            act.activation(rs[:], ss[:], ACT.Sqrt, scale=1.0 / D_SSM, bias=eps[:]).then_inc(rooted, 1)

        @block.vector
        def _(v):
            v.memset(ss[:], 1.0).then_inc(set_up, 1)
            v.wait_ge(loaded, 16 * 8)
            v.wait_ge(gelu_done, 2)

            def visit(n, j, rows, first):
                v.wait_ge(z_done, n + 1)
                if not first:
                    v.wait_ge(y_done, n - 1)
                v.tensor_tensor(z[0:rows, j], v_ps[0:rows, j, 0:D_SSM], wide[0:rows, 0], ALU.add).then_inc(z_biased, 1)
                y, gate = yb[0:rows, n], gb[0:rows, n]
                v.wait_ge(z_sig, n + 1)
                v.wait_ge(copied, n + 1)
                v.tensor_tensor(y, y, z[0:rows, j], ALU.mult).then_inc(step, 1)
                v.wait_ge(gb_sig, n + 1)
                v.tensor_tensor(sg[0:rows], sg[0:rows], gate, ALU.mult).then_inc(step, 1)
                v.wait_ge(step, 2 * n + 2)
                v.tensor_tensor(y, y, sg[0:rows], ALU.mult).then_inc(y_done, 1)
            tiles(v, visit)
            v.wait_ge(rooted, 1)
            v.reciprocal(rs[:], rs[:]).then_inc(inv, 1)
            v.wait_ge(inv, 1)
            for n in range(nt + 1):
                rows = P if n < nt else SMP
                v.scalar_tensor_tensor(yb[0:rows, n], yb[0:rows, n], rs[0:rows, n:n + 1], wide[0:rows, 1],
                                       ALU.mult, ALU.mult).then_inc(normed, 1)


KTS = 13
SAMPLE_TILES = [(0, slice(0, 8, 1))] + [(1, slice(c, 8, 4)) for c in range(4)] + [(2, slice(c, c + 1, 1)) for c in range(8)]
SEG = P + TS


def sample_attend(nc, top, t, keep):
    L = len(LEVELS)
    ROWS = 2 * TS
    with ExitStack() as ctx:
        f = Frame(nc, ctx)
        k = f.sb("c_k", [P, 2, KTS, PAIRS, P])
        v = f.sb("c_v", [P, 2, KTS, D_ATT])
        qk = f.sb("c_qk", [P, 2 * PAIRS, SMP])
        vn = f.sb("c_vn", [TS, 2, D_ATT])
        bias = f.sb("c_bias", [ROWS, PAIRS, L * SEG])
        q_mask = f.sb("c_q_mask", [P, KTS, 2, TS])
        w_mask = f.sb("c_w_mask", [P, KTS, TS])
        q_m = f.sb("c_q_m", [P, 2, KTS, PAIRS, ROWS])
        w = f.sb("c_w", [ROWS, PAIRS, L * SEG])
        low = f.sb("c_low", [ROWS, PAIRS])
        den = f.sb("c_den", [ROWS, PAIRS])
        wn = f.sb("c_wn", [ROWS, PAIRS, TS])
        w_m = f.sb("c_w_m", [P, KTS, HEADS, TS])
        wnT = f.sb("c_wnT", [TS, HEADS * TS])
        o = f.sb("c_o", [TS, 2, D_ATT])
        s_ps = f.ps("c_s_ps", [P, 2, PAIRS, 512])
        t_ps = f.ps("c_t_ps", [P, 512])
        o_ps = f.ps("c_o_ps", [P, 512])
        loaded, q_masked = f.sem("c_loaded"), f.sem("c_q_masked")
        k_loaded = [f.sem(f"c_k_loaded{j}") for j in range(2)]
        v_loaded = [f.sem(f"c_v_loaded{j}") for j in range(2)]
        stored = [f.sem(f"c_stored{j}") for j in range(2)]
        s_done, biased, low_done, exp_done = f.sem("c_s_done"), f.sem("c_biased"), f.sem("c_low_done"), f.sem("c_exp_done")
        den_inv, scaled, new_step, turned = f.sem("c_den_inv"), f.sem("c_scaled"), f.sem("c_new_step"), f.sem("c_turned")
        w_masked, wnT_out, o_done, o_out = f.sem("c_w_masked"), f.sem("c_wnT_out"), f.sem("c_o_done"), f.sem("c_o_out")
        block = ctx.enter_context(nc.Block())

        def sequences(eng, visit):
            def body(i, first, last):
                for j in range(2):
                    visit(2 * i + j, j, i)
            peeled(eng, NS // 2, body)

        def early(n, until):
            return isinstance(n, int) and n < until

        @block.sync
        def _(sp):
            sp.dma_start(qk[:], t["qkT_all"][:, :, SEQ:]).then_inc(loaded, 16)
            sp.dma_start(q_mask[:], t["q_mask"]).then_inc(loaded, 16)
            sp.dma_start(w_mask[:], t["w_mask"]).then_inc(loaded, 16)
            sp.dma_start(bias[:], t["bias_s"]).then_inc(loaded, 16)

            def load(n, j, i):
                if not early(n, 2):
                    hold(sp, keep, s_done, n - 1)
                sp.dma_start(k[:, j], t["cache_kT"][ds(n, 1)].rearrange("o p a -> (o p) a")).then_inc(k_loaded[j], 16)
                if not early(n, 2):
                    hold(sp, keep, o_done, n - 1)
                sp.dma_start(v[:, j], t["cache_v"][ds(n, 1)].rearrange("o p a -> (o p) a")).then_inc(v_loaded[j], 16)
                sp.dma_start(vn[:, j], t["v_all"][ds(SEQ + n * TS, TS), :]).then_inc(v_loaded[j], 16)

            def visit(n, j, i):
                if not (isinstance(n, int) and n + 1 >= NS):
                    load(n + 1, (j + 1) % 2, i + j)
                hold(sp, keep, o_out, n + 1)
                sp.dma_start(t["os_all"][ds(n * TS, TS), :], o[:, j]).then_inc(stored[j], 16)
            load(0, 0, 0)
            sequences(sp, visit)
            for j in range(2):
                sp.wait_ge(stored[j], 16 * (NS // 2))

        @block.gpsimd
        def _(pool):
            pool.wait_ge(loaded, 64)

            def mask_q(n, j, i):
                if not early(n, 2):
                    pool.wait_ge(s_done, n - 1)
                for x in range(PAIRS):
                    q = qk[:, x, ds(n * TS, TS)].rearrange("p (a e t) -> p a e t", a=1, e=1).broadcast_to([P, KTS, 2, TS])
                    m = nc.gpsimd.tensor_tensor(q_m[:, j, :, x].rearrange("p a (e t) -> p a e t", e=2), q, q_mask[:], ALU.mult)
                m.then_inc(q_masked, 1)
            sequences(pool, mask_q)

        @block.tensor
        def _(pe):
            pe.wait_ge(loaded, 64)

            def scores(n, j, i):
                pe.wait_ge(q_masked, n + 1)
                pe.wait_ge(k_loaded[j], 16 * (i + 1))
                if not early(n, 2):
                    pe.wait_ge(biased, n - 1)
                for x in range(PAIRS):
                    out = s_ps[0:ROWS, j, x]
                    for a, (level, _) in enumerate(SAMPLE_TILES):
                        new = a == 0 or SAMPLE_TILES[a - 1][0] != level
                        end = a == KTS - 1 or SAMPLE_TILES[a + 1][0] != level
                        pe.matmul(out[:, level * SEG:level * SEG + P], q_m[:, j, a, x], k[:, j, a, x], start=new, stop=end,
                                  skip_group_check=True)
                    for level in range(L):
                        m = pe.matmul(out[:, level * SEG + P:(level + 1) * SEG], q_m[:, j, 0, x],
                                      qk[:, PAIRS + x, ds(n * TS, TS)], start=True, stop=True, skip_group_check=True)
                m.then_inc(s_done, 1)

            def weighted(n, j, i):
                if not early(n, 1):
                    pe.wait_ge(w_masked, n)
                    pe.wait_ge(wnT_out, n)
                pe.wait_ge(scaled, n + 1)
                hold(pe, keep, new_step, 2 * n + 2)
                for l in range(L):
                    for x in range(PAIRS):
                        at = (l * PAIRS + x) * ROWS
                        pe.transpose(t_ps[:, at:at + ROWS], w[:, x, l * SEG:l * SEG + P], keep["ident"][0:ROWS, 0:ROWS])
                for x in range(PAIRS):
                    at = (L * PAIRS + x) * ROWS
                    m = pe.transpose(t_ps[0:TS, at:at + ROWS], wn[:, x], keep["ident"][0:ROWS, 0:ROWS])
                m.then_inc(turned, 1)
                pe.wait_ge(w_masked, n + 1)
                pe.wait_ge(wnT_out, n + 1)
                pe.wait_ge(v_loaded[j], 32 * (i + 1))
                if not early(n, 1):
                    pe.wait_ge(o_out, n)
                for h in range(HEADS):
                    out = o_ps[0:TS, h * DH:(h + 1) * DH]
                    for a in range(KTS):
                        pe.matmul(out, w_m[:, a, h], v[:, j, a, h * DH:(h + 1) * DH], start=(a == 0), stop=False,
                                  skip_group_check=True)
                    m = pe.matmul(out, wnT[:, h * TS:(h + 1) * TS], vn[:, j, h * DH:(h + 1) * DH],
                                  start=False, stop=True, skip_group_check=True)
                m.then_inc(o_done, 1)

            def visit(n, j, i):
                if not (isinstance(n, int) and n + 1 >= NS):
                    scores(n + 1, (j + 1) % 2, i + j)
                weighted(n, j, i)
            scores(0, 0, 0)
            sequences(pe, visit)

        @block.scalar
        def _(act):
            act.wait_ge(loaded, 64)

            def visit(n, j, i):
                act.wait_ge(low_done, n + 1)
                for x in range(PAIRS):
                    act.activation(w[:, x], w[:, x], ACT.Exp, scale=-1.0, bias=low[:, x:x + 1],
                                   accum_out=den[:, x:x + 1]).then_inc(exp_done, 1)
                act.wait_ge(o_done, n + 1)
                if not early(n, 2):
                    act.wait_ge(stored[j], 16 * i)
                act.activation(o[:, j], o_ps[0:TS, 0:D_ATT], ACT.Copy).then_inc(o_out, 1)
            sequences(act, visit)

        @block.vector
        def _(dve):
            dve.wait_ge(loaded, 64)

            def visit(n, j, i):
                dve.wait_ge(s_done, n + 1)
                if not early(n, 1):
                    dve.wait_ge(turned, n)
                dve.tensor_tensor(w[:], s_ps[0:ROWS, j, :, 0:L * SEG], bias[:], ALU.add).then_inc(biased, 1)
                dve.wait_ge(biased, n + 1)
                dve.tensor_reduce(low[:], w[:], AX.X, ALU.min).then_inc(low_done, 1)
                dve.wait_ge(exp_done, PAIRS * (n + 1))
                dve.reciprocal(den[:], den[:]).then_inc(den_inv, 1)
                dve.wait_ge(den_inv, n + 1)
                for x in range(PAIRS):
                    m = dve.tensor_scalar(w[:, x], w[:, x], den[:, x:x + 1], None, ALU.mult)
                m.then_inc(scaled, 1)
                dve.wait_ge(scaled, n + 1)
                new = w.rearrange("r x (l k) -> r x l k", l=L)[:, :, :, P:]
                dve.tensor_tensor(wn[:], new[:, :, 0], new[:, :, 1], ALU.add).then_inc(new_step, 1)
                dve.wait_ge(new_step, 2 * n + 1)
                dve.tensor_tensor(wn[:], wn[:], new[:, :, 2], ALU.add).then_inc(new_step, 1)
                dve.wait_ge(turned, n + 1)
                if not early(n, 1):
                    dve.wait_ge(o_done, n)
                dve.tensor_copy(wnT[:], t_ps[0:TS, L * PAIRS * ROWS:(L + 1) * PAIRS * ROWS]).then_inc(wnT_out, 1)
                for l in range(L):
                    tiles = [a for a, (level, _) in enumerate(SAMPLE_TILES) if level == l]
                    at, shape = slice(tiles[0], tiles[-1] + 1), [P, len(tiles), HEADS, TS]
                    src = t_ps[:, l * PAIRS * ROWS:(l + 1) * PAIRS * ROWS].rearrange("p (o h t) -> p o h t", o=1, h=HEADS)
                    mask = w_mask[:, at].rearrange("p a (o t) -> p a o t", o=1)
                    m = dve.tensor_tensor(w_m[:, at], src.broadcast_to(shape), mask.broadcast_to(shape), ALU.mult)
                m.then_inc(w_masked, 1)
            sequences(dve, visit)


def project_out(nc, top, t, keep):
    nt = SEQ // P
    L = len(LEVELS)
    TC = (D_SSM + D_ATT) // P
    with ExitStack() as ctx:
        f = Frame(nc, ctx)
        w_raw = f.sb("wo_raw", [P, 2, D])
        w_hi = f.sb("wo_hi", [P, KT, D], F32R)
        w_lo = f.sb("wo_lo", [P, KT, D], F32R)
        o = f.sb("o_in", [P, 2, L, O_ROW])
        gc = f.sb("gc_in", [P, 2, D_ATT])
        ya = f.sb("ya_in", [P, 2, LT, P])
        yb = f.sb("yb_in", [P, 2, D_SSM])
        yc = f.sb("yc", [P, 2, D_ATT])
        x = f.sb("x_in", [P, 2, D])
        y_out = f.sb("y_out", [P, 2, D])
        y_hi = f.sb("y_hi", [P, 2, KT, P], F32R)
        y_lo = f.sb("y_lo", [P, 2, KT, P], F32R)
        low = f.sb("low", [P, HEADS])
        wt = f.sb("weights", [P, L, HEADS])
        wd = f.sb("weighted_den", [P, L, HEADS])
        gate = f.sb("gc_gate", [P, D_ATT])
        sq = f.sb("yc_sq", [P, D_ATT])
        ms = f.sb("yc_ms", [P, 2])
        gain = f.sb("yc_gain", [P, D_ATT])
        eps = f.sb("eps_o", [P, 1])
        out_ps = f.ps("out_ps", [P, 2, 2, 512])
        t_ps = f.ps("yT_ps", [P, 2, 1024])
        w_loaded = [f.sem(f"wo_loaded{j}") for j in range(2)]
        o_loaded = [f.sem(f"o_in_loaded{j}") for j in range(2)]
        ab_loaded = [f.sem(f"ab_in_loaded{j}") for j in range(2)]
        x_loaded = [f.sem(f"x_in_loaded{j}") for j in range(2)]
        y_stored = [f.sem(f"y_stored{j}") for j in range(2)]
        set_up, rooted = f.sem("o_set_up"), f.sem("yc_rooted")
        w_hi_done, w_split, gain_loaded = f.sem("wo_hi_done"), f.sem("wo_split"), f.sem("yc_gain_loaded")
        low_done, exp_done, step = f.sem("low_done"), f.sem("exp_done"), f.sem("yc_step")
        gate_exp, gate_den, gate_inv, gate_done = f.sem("gate_exp"), f.sem("gate_den"), f.sem("gate_inv"), f.sem("gate_done")
        gated, squared, inv, normed = f.sem("yc_gated"), f.sem("yc_squared"), f.sem("yc_inv"), f.sem("yc_normed")
        turned, hi_done, split, projected, added = f.sem("y_turned"), f.sem("y_hi_done"), f.sem("y_split"), f.sem("projected"), f.sem("added")
        block = ctx.enter_context(nc.Block())
        NSTEP = 10

        def height(n):
            if not isinstance(n, int) or n < nt:
                return P
            return SMP if n == nt else 0

        def tokens(n):
            return slice(SEQ, SEQ + SMP) if height(n) == SMP else ds(n * P, P)

        def steps(eng, visit, tail=1):
            def body(i, first, last):
                for j in range(2):
                    visit(2 * i + j, j, i)
            peeled(eng, nt // 2, body, tail=tail)
            visit(nt, 0, nt // 2)

        def early(n, until):
            return isinstance(n, int) and n < until

        @block.sync
        def _(sp):
            def load_o(n, j):
                if not height(n):
                    return
                if not early(n, 2):
                    hold(sp, keep, normed, n - 1)
                if height(n) == SMP:
                    sp.wait_ge(split, nt - 1)
                    sp.dma_start(yc[0:SMP, j], t["os_all"]).then_inc(o_loaded[j], 16)
                else:
                    sp.dma_start(o[:, j], t["o_all"][:, tokens(n), :].rearrange("l p e -> p l e")).then_inc(o_loaded[j], 16)
                sp.dma_start(gc[0:height(n), j], t["gc_all"][tokens(n), :]).then_inc(o_loaded[j], 16)

            def load_ab(n, j):
                if not height(n):
                    return
                if not early(n, 2):
                    hold(sp, keep, split, n - 1)
                sp.dma_start(ya[:, j, :, 0:height(n)], t["yaT_all"][:, :, tokens(n)]).then_inc(ab_loaded[j], 16)
                sp.dma_start(yb[0:height(n), j], t["yb_all"][tokens(n), :]).then_inc(ab_loaded[j], 16)

            def load_x(n, j):
                if not height(n):
                    return
                if not early(n, 2):
                    hold(sp, keep, added, n - 1)
                sp.dma_start(x[0:height(n), j], t["x_s"] if height(n) == SMP else t["x_p"][ds(n * P, P), :]).then_inc(x_loaded[j], 16)

            sp.dma_start(gain[:], t["yc_gain"].rearrange("(o d) -> o d", o=1).broadcast_to([P, D_ATT])).then_inc(gain_loaded, 16)
            load_o(0, 0)
            for k in range(KT):
                if k == 3:
                    load_ab(0, 0)
                    load_o(1, 1)
                if k >= 2:
                    sp.wait_ge(w_split, k - 1)
                sp.dma_start(w_raw[:, k % 2], t["w_out"][:, k]).then_inc(w_loaded[k % 2], 16)
            load_ab(1, 1)
            load_o(2, 0)
            load_x(0, 0)

            def visit(n, j, nth):
                load_o(n + 3, (j + 1) % 2)
                load_ab(n + 2, j)
                load_x(n + 1, (j + 1) % 2)
                hold(sp, keep, added, n + 1)
                sp.dma_start(t["y_s"] if height(n) == SMP else t["y_p"][ds(n * P, P), :],
                             y_out[0:height(n), j]).then_inc(y_stored[j], 16)
            steps(sp, visit, tail=2)
            sp.wait_ge(y_stored[0], 16 * (nt // 2 + 1))
            sp.wait_ge(y_stored[1], 16 * (nt // 2))

        @block.gpsimd
        def _(pool):
            def make_gate(n, j):
                rows = height(n)
                pool.wait_ge(gate_inv, n + 1)
                nc.gpsimd.tensor_tensor(gate[0:rows], gate[0:rows], gc[0:rows, j], ALU.mult).then_inc(gate_done, 1)
            nc.gpsimd.memset(eps[:], EPS).then_inc(set_up, 1)
            make_gate(0, 0)
            for k in range(KT):
                pool.wait_ge(w_hi_done, k + 1)
                nc.gpsimd.tensor_tensor(w_lo[:, k], w_raw[:, k % 2], w_hi[:, k].bitcast(F32), ALU.subtract).then_inc(w_split, 1)
            make_gate(1, 1)

            def visit(n, j, nth):
                if height(n + 2):
                    make_gate(n + 2, j)
            steps(pool, visit)

        @block.tensor
        def _(pe):
            def turn(n, j, nth):
                rows = height(n)
                pe.wait_ge(ab_loaded[j], 32 * (nth + 1))
                pe.wait_ge(normed, n + 1)
                if not early(n, 2):
                    pe.wait_ge(split, n - 1)
                for c in range(TC):
                    src = yb[0:rows, j, c * P:(c + 1) * P] if c < 2 else yc[0:rows, j, (c - 2) * P:(c - 1) * P]
                    m = pe.transpose(t_ps[:, j, c * P:c * P + rows], src, keep["ident"][0:rows, 0:rows])
                m.then_inc(turned, 1)

            def project(n, j, half):
                rows = height(n)
                for k in range(KT):
                    out, cols = out_ps[0:rows, j, half], slice(half * 512, half * 512 + 512)
                    yh = y_hi[:, j, k, 0:rows]
                    pe.matmul(out, yh, w_hi[:, k, cols], start=(k == 0), stop=False)
                    pe.matmul(out, yh, w_lo[:, k, cols], start=False, stop=False)
                    m = pe.matmul(out, y_lo[:, j, k, 0:rows], w_hi[:, k, cols], start=False, stop=(k == KT - 1))
                m.then_inc(projected, 1)
            turn(0, 0, 0)
            pe.wait_ge(w_split, KT)

            def visit(n, j, nth):
                pe.wait_ge(split, n + 1)
                if not early(n, 2):
                    pe.wait_ge(added, n - 1)
                project(n, j, 0)
                if height(n + 1):
                    turn(n + 1, (j + 1) % 2, nth + j)
                project(n, j, 1)
            steps(pe, visit)

        @block.scalar
        def _(act):
            def start_gate(n, j, nth):
                act.wait_ge(o_loaded[j], 32 * (nth + 1))
                if not early(n, 1):
                    act.wait_ge(gated, n)
                act.activation(gate[0:height(n)], gc[0:height(n), j], ACT.Exp, scale=-1.0).then_inc(gate_exp, 1)
                act.wait_ge(gate_exp, n + 1)
                act.activation(gate[0:height(n)], gate[0:height(n)], ACT.Copy, bias=1.0).then_inc(gate_den, 1)
                if height(n) == P:
                    act.wait_ge(low_done, n + 1)
                    act.activation(wt[:], wt[:], ACT.Exp).then_inc(exp_done, 1)

            def mean_square(n, j):
                rows = height(n)
                act.wait_ge(gated, n + 1)
                if not early(n, 1):
                    act.wait_ge(squared, n)
                act.activation(sq[0:rows], yc[0:rows, j], ACT.Square, scale=D_ATT ** -0.5,
                               accum_out=ms[0:rows, j:j + 1]).then_inc(squared, 1)
                act.wait_ge(squared, n + 1)
                act.activation(ms[0:rows, j:j + 1], ms[0:rows, j:j + 1], ACT.Sqrt, bias=eps[0:rows]).then_inc(rooted, 1)

            def highs(n, j, nth):
                rows = height(n)
                act.wait_ge(ab_loaded[j], 32 * (nth + 1))
                if not early(n, 2):
                    act.wait_ge(projected, 2 * n - 2)
                act.activation(y_hi[:, j, 0:LT, 0:rows], ya[:, j, :, 0:rows], ACT.Copy).then_inc(hi_done, 1)
                act.wait_ge(turned, n + 1)
                act.activation(y_hi[:, j, LT:, 0:rows], t_ps[:, j, 0:TC * P].rearrange("p (c t) -> p c t", c=TC)[:, :, 0:rows],
                               ACT.Copy).then_inc(hi_done, 1)
            act.wait_ge(set_up, 1)
            start_gate(0, 0, 0)
            mean_square(0, 0)
            for k in range(KT):
                act.wait_ge(w_loaded[k % 2], 16 * (k // 2 + 1))
                act.activation(w_hi[:, k], w_raw[:, k % 2], ACT.Copy).then_inc(w_hi_done, 1)
            start_gate(1, 1, 0)
            mean_square(1, 1)
            highs(0, 0, 0)

            def visit(n, j, nth):
                if height(n + 2):
                    start_gate(n + 2, j, nth + 1)
                if height(n + 1):
                    highs(n + 1, (j + 1) % 2, nth + j)
                if height(n + 2):
                    mean_square(n + 2, j)
            steps(act, visit)

        @block.vector
        def _(v):
            v.wait_ge(gain_loaded, 16)

            def join(n, j, nth):
                rows = height(n)
                v.wait_ge(o_loaded[j], 32 * (nth + 1))
                Y = yc[0:rows, j]
                base = NSTEP * n
                if rows == P:
                    mins, dens = o[:, j, :, D_ATT:D_ATT + HEADS], o[:, j, :, D_ATT + HEADS:]
                    v.tensor_tensor(low[:], mins[:, 0], mins[:, 1], ALU.min).then_inc(step, 1)
                    v.wait_ge(step, base + 1)
                    v.tensor_tensor(low[:], low[:], mins[:, 2], ALU.min).then_inc(step, 1)
                    v.wait_ge(step, base + 2)
                    v.tensor_tensor(wt[:], low.rearrange("p (o h) -> p o h", o=1).broadcast_to([P, L, HEADS]), mins,
                                    ALU.subtract).then_inc(low_done, 1)
                v.wait_ge(gate_den, n + 1)
                v.reciprocal(gate[0:rows], gate[0:rows]).then_inc(gate_inv, 1)
                if rows == P:
                    v.wait_ge(exp_done, n + 1)
                    v.tensor_tensor(wd[:], wt[:], dens, ALU.mult).then_inc(step, 1)
                    v.wait_ge(step, base + 3)
                    v.tensor_tensor(low[:], wd[:, 0], wd[:, 1], ALU.add).then_inc(step, 1)
                    v.wait_ge(step, base + 4)
                    v.tensor_tensor(low[:], low[:], wd[:, 2], ALU.add).then_inc(step, 1)
                    v.wait_ge(step, base + 5)
                    v.reciprocal(low[:], low[:]).then_inc(step, 1)
                    v.wait_ge(step, base + 6)
                    v.tensor_tensor(wt[:], wt[:], low.rearrange("p (o h) -> p o h", o=1).broadcast_to([P, L, HEADS]),
                                    ALU.mult).then_inc(step, 1)
                    v.wait_ge(step, base + 7)
                    rows_o = o[:, j, :, 0:D_ATT].rearrange("p l (h d) -> p l h d", d=DH)
                    for l in range(L):
                        m = v.tensor_tensor(rows_o[:, l], rows_o[:, l],
                                            wt[:, l].rearrange("p (h o) -> p h o", o=1).broadcast_to([P, HEADS, DH]), ALU.mult)
                    m.then_inc(step, 1)
                    v.wait_ge(step, base + 8)
                    v.tensor_tensor(Y, o[:, j, 0, 0:D_ATT], o[:, j, 1, 0:D_ATT], ALU.add).then_inc(step, 1)
                    v.wait_ge(step, base + 9)
                    v.tensor_tensor(Y, Y, o[:, j, 2, 0:D_ATT], ALU.add).then_inc(step, 1)
                    v.wait_ge(step, base + 10)
                v.wait_ge(gate_done, n + 1)
                v.tensor_tensor(Y, Y, gate[0:rows], ALU.mult).then_inc(gated, 1)

            def norm(n, j):
                rows = height(n)
                v.wait_ge(rooted, n + 1)
                v.reciprocal(ms[0:rows, j:j + 1], ms[0:rows, j:j + 1]).then_inc(inv, 1)
                v.wait_ge(inv, n + 1)
                v.scalar_tensor_tensor(yc[0:rows, j], yc[0:rows, j], ms[0:rows, j:j + 1], gain[0:rows],
                                       ALU.mult, ALU.mult).then_inc(normed, 1)

            def lows(n, j):
                rows = height(n)
                v.wait_ge(hi_done, 2 * n + 1)
                v.tensor_tensor(y_lo[:, j, 0:LT, 0:rows], ya[:, j, :, 0:rows], y_hi[:, j, 0:LT, 0:rows].bitcast(F32), ALU.subtract)
                v.wait_ge(hi_done, 2 * n + 2)
                v.tensor_tensor(y_lo[:, j, LT:, 0:rows], t_ps[:, j, 0:TC * P].rearrange("p (c t) -> p c t", c=TC)[:, :, 0:rows],
                                y_hi[:, j, LT:, 0:rows].bitcast(F32), ALU.subtract).then_inc(split, 1)

            def add(n, j, half):
                cols = slice(half * 512, half * 512 + 512)
                v.wait_ge(projected, 2 * n + half + 1)
                return v.tensor_tensor(y_out[0:height(n), j, cols], out_ps[0:height(n), j, half], x[0:height(n), j, cols], ALU.add)
            for n in range(2):
                join(n, n, 0)
                norm(n, n)
            lows(0, 0)

            def visit(n, j, nth):
                if height(n + 2):
                    join(n + 2, j, nth + 1)
                if height(n + 1):
                    lows(n + 1, (j + 1) % 2)
                v.wait_ge(x_loaded[j], 16 * (nth + 1))
                if not early(n, 2):
                    v.wait_ge(y_stored[j], 16 * nth)
                add(n, j, 0)
                if height(n + 2):
                    norm(n + 2, j)
                add(n, j, 1).then_inc(added, 1)
            steps(v, visit)


def constants(nc, top, t):
    keep = {
        "ident": top.sb("ident", [P, P]),
        "qk_gain": top.sb("qk_gain", [P, 2 * D_ATT]),
        "rs": top.sb("rs_keep", [P, SEQ // P + 1]),
    }
    loaded = top.sem("constants_loaded")
    gained = top.sem("q_gain_scaled")
    with nc.Block() as block:
        @block.sync
        def _(sp):
            sp.dma_start(keep["ident"][:], t["identity"]).then_inc(loaded, 16)
            for name, half in (("q_norm_g", 0), ("k_norm_g", 1)):
                for h in range(HEADS):
                    at = half * D_ATT + h * DH
                    sp.dma_start(keep["qk_gain"][:, at:at + DH],
                                 t[name].rearrange("(o d) -> o d", o=1).broadcast_to([P, DH])).then_inc(loaded, 16)
            sp.wait_ge(loaded, 16 * (1 + 2 * HEADS))

        @block.vector
        def _(v):
            v.wait_ge(loaded, 16 * (1 + 2 * HEADS))
            v.tensor_scalar(keep["qk_gain"][:, 0:D_ATT], keep["qk_gain"][:, 0:D_ATT], -(DH ** -0.5), None, ALU.mult).then_inc(gained, 1)
    keep["loaded"] = loaded
    return keep


def program(nc, t):
    with ExitStack() as ctx:
        top = Frame(nc, ctx)
        keep = constants(nc, top, t)
        project_attention(nc, top, t, keep)
        project_recurrent(nc, top, t, keep)
        attend(nc, top, t, keep)
        ssm(nc, top, t, keep)
        sample_attend(nc, top, t, keep)
        project_out(nc, top, t, keep)


OUTS = {
    "y_p": (SEQ, D), "y_s": (SMP, D), "conv_p": (P, LT, 3), "lru_p": (P, LT),
    "ssm_re_p": (STATE, GROUPS), "ssm_im_p": (STATE, GROUPS), "k_p": (KEEP, D_ATT), "v_p": (KEEP, D_ATT),
    "conv_s": (P, LT, NS, 3), "lru_s": (P, LT, NS), "ssm_re_s": (STATE, GROUPS, NS), "ssm_im_s": (STATE, GROUPS, NS),
    "k_s": (SMP, D_ATT), "v_s": (SMP, D_ATT),
}
SCRATCH = {
    "v_all": (SEQ + SMP, D_ATT), "gc_all": (SEQ + SMP, D_ATT), "k_all": (SEQ + SMP, D_ATT),
    "ys_mid": (SMP, D_SSM), "yb_all": (SEQ + SMP, D_SSM), "os_all": (SMP, D_ATT),
    "o_all": (len(LEVELS), SEQ, O_ROW),
    "qkT_all": (P, 2 * PAIRS, SEQ + SMP), "ug_all": (SEQ + SMP, 2 * D_SSM), "yaT_all": (P, LT, SEQ + SMP),
}


def slopes():
    return np.exp2(-8.0 * np.arange(1, HEADS + 1) / HEADS).astype(np.float32)


def prompt_bias():
    delta = np.arange(P)[:, None] - np.arange(2 * P)[None] + P
    out = np.zeros((P, len(LEVELS), HEADS, 2 * P), np.float32)
    for n, (_, dil) in enumerate(LEVELS):
        for h, slope in enumerate(slopes()):
            out[:, n, h] = np.where((delta >= 0) & (delta <= P), slope * (delta * dil).astype(np.float32), -NEG)
    return out


def tiles_of(cache):
    n = PAST
    parts = [cache[:, n - P:]]
    parts += [cache[:, n - 4 * P + c::4] for c in range(4)]
    parts += [cache[:, n - 16 * P + c::16] for c in range(16 // 2)]
    return np.stack(parts, 1)


def sample_bias():
    out = np.full((2, TS, PAIRS, len(LEVELS), SEG), -NEG, np.float32)
    m = np.arange(P)
    for h, slope in enumerate(slopes()):
        for l, (_, dil) in enumerate(LEVELS):
            for step in range(TS):
                delta = P + step // dil - m
                row = out[h % 2, step, h // 2, l]
                row[:P] = np.where(delta <= P, slope * (delta * dil).astype(np.float32), -NEG)
                for back in range(0, step + 1, dil):
                    row[P + step - back] = slope * np.float32(back)
    return out.reshape(2 * TS, PAIRS, -1)


def sample_masks():
    serves = np.zeros((KTS, TS), np.float32)
    for a, (_, steps) in enumerate(SAMPLE_TILES):
        serves[a, steps] = 1.0
    heads = np.repeat(np.eye(2, dtype=np.float32), DH, 0)
    q_mask = heads[:, None, :, None] * serves[None, :, None, :]
    return np.ascontiguousarray(q_mask), np.ascontiguousarray(np.broadcast_to(serves, (P, KTS, TS)))


def lay_out(i):
    w = i["w_in"][0].reshape(KT, P, -1).transpose(1, 0, 2)
    twice = lambda x: np.concatenate([x, x])
    eye = np.eye(STATE, dtype=np.float32)
    br, bi = (i[n][0].transpose(1, 0, 2) for n in ("ssm_b_re", "ssm_b_im"))
    cr, ci = (i[n][0].transpose(2, 0, 1) for n in ("ssm_c_re", "ssm_c_im"))
    return {
        "xT_p": i["x_prompt"][0].T.reshape(KT, P, SEQ).transpose(1, 0, 2),
        "xT_s": i["x_sample"].reshape(SMP, D).T.reshape(KT, P, SMP).transpose(1, 0, 2),
        "x_p": i["x_prompt"][0],
        "x_s": i["x_sample"].reshape(SMP, D),
        "norm_g": i["norm_g"][0].reshape(KT, P).T,
        "w_att": w[:, :, D_R:],
        "w_rec": w[:, :, :D_R],
        "q_norm_g": i["q_norm_g"][0],
        "k_norm_g": i["k_norm_g"][0],
        "conv_w": i["conv_w"][0].reshape(CONV_W, LT, P).transpose(2, 1, 0),
        "lru_vec": np.stack([i[n][0][:D_LRU].reshape(LT, P).T for n in ("conv_b", "b_r", "b_i", "lru_lambda", "out_norm_g")], 1),
        "w_r": i["w_r"][0],
        "w_i": i["w_i"][0],
        "state_conv": i["state_conv"][0].transpose(2, 0, 1).reshape(LT, P, NS, 3).transpose(1, 0, 2, 3),
        "state_lru": i["state_lru"][0].T.reshape(LT, P, NS).transpose(1, 0, 2),
        "ssm_par": twice(np.stack([i[n][0].T for n in ("ssm_lambda_re", "ssm_lambda_im", "ssm_log_dt")], 1)),
        "ssm_bc": np.stack([np.concatenate(x) for x in ((br, bi), (bi, br), (cr, ci), (ci, cr))], 1),
        "ssm_sign": np.repeat(np.float32([[-1], [1]]), STATE, 0),
        "ssm_turn": np.block([[0 * eye, eye], [-eye, 0 * eye]]),
        "ssm_d": np.tile(i["ssm_d"][0].reshape(GROUPS, GC).T, (CH, 1)),
        "ssm_x0": np.concatenate([i[n][0].transpose(2, 1, 0) for n in ("state_ssm_re", "state_ssm_im")]),
        "ssm_wide": np.stack([i["glu_b"][0], i["out_norm_g"][0][D_LRU:D_LRU + D_SSM]]),
        "glu_w": i["glu_w"][0],
        "yc_gain": i["out_norm_g"][0][D_LRU + D_SSM:],
        "w_out": i["w_out"][0].reshape(KT, P, D).transpose(1, 0, 2),
        "ones": np.ones((P, KC), np.float32),
        "cache_kT": tiles_of(i["cache_k"][0]).reshape(NS, KTS, P, PAIRS, P).transpose(0, 4, 1, 3, 2).reshape(NS, P, -1),
        "cache_v": tiles_of(i["cache_v"][0]).reshape(NS, KTS, P, D_ATT).transpose(0, 2, 1, 3).reshape(NS, P, -1),
        "bias_s": sample_bias(),
        "q_mask": sample_masks()[0],
        "w_mask": sample_masks()[1],
        "bias_p": prompt_bias(),
        "identity": np.eye(P, dtype=np.float32),
    }


def kernel(**inputs):
    import concourse.bacc as bacc
    from concourse.bass_utils import run_bass_kernel_spmd

    nc = bacc.Bacc("TRN2", target_bir_lowering=False, num_devices=1)
    arrays = {f"in_{n}": np.ascontiguousarray(a) for n, a in lay_out({n: np.asarray(a) for n, a in inputs.items()}).items()}
    t = {n[3:]: nc.dram_tensor(n, a.shape, F32, kind="ExternalInput").ap() for n, a in arrays.items()}
    for n, s in OUTS.items():
        t[n] = nc.dram_tensor(f"out_{n}", s, F32, kind="ExternalOutput").ap()
    for n, s in SCRATCH.items():
        t[n] = nc.dram_tensor(f"mid_{n}", s, F32, kind="Internal").ap()
    program(nc, t)
    r = run_bass_kernel_spmd(nc, [arrays], core_ids=[0]).results[0]
    o = {n: r[f"out_{n}"] for n in OUTS}
    return (
        o["y_p"].reshape(1, SEQ, D), o["y_s"].reshape(NS, TS, D),
        o["conv_p"].transpose(2, 1, 0).reshape(1, 1, 3, D_LRU), o["lru_p"].T.reshape(1, 1, D_LRU),
        o["ssm_re_p"].T.reshape(1, 1, GROUPS, STATE), o["ssm_im_p"].T.reshape(1, 1, GROUPS, STATE),
        o["k_p"].reshape(1, 1, KEEP, HEADS, DH), o["v_p"].reshape(1, 1, KEEP, HEADS, DH),
        o["conv_s"].transpose(2, 3, 1, 0).reshape(1, NS, 3, D_LRU), o["lru_s"].transpose(2, 1, 0).reshape(1, NS, D_LRU),
        o["ssm_re_s"].transpose(2, 1, 0).reshape(1, NS, GROUPS, STATE),
        o["ssm_im_s"].transpose(2, 1, 0).reshape(1, NS, GROUPS, STATE),
        o["k_s"].reshape(1, NS, TS, HEADS, DH), o["v_s"].reshape(1, NS, TS, HEADS, DH),
    )
```

```python
from contextlib import ExitStack

import numpy as np

import concourse.bass as bass
from concourse import mybir

F32 = mybir.dt.float32
F32R = mybir.dt.float32r
ALU = mybir.AluOpType
ACT = mybir.ActivationFunctionType
AX = mybir.AxisListType
ds = bass.ds

P = 128
STAGES = 3
D = 1024
KT = D // P
SEQ = 4096
NS, TS = 8, 8
SMP = NS * TS
PAST = 2048
D_LRU, D_SSM, D_ATT = 384, 256, 384
HEADS, DH = 6, 64
PAIRS = HEADS // 2
LT = D_LRU // P
CONV_W = 4
GROUPS, GC, STATE = 16, 16, 64
CH = 8
EPS = 1e-6
NEG = -1e30
LEVELS = ((128, 1), (512, 4), (2048, 16))
KEEP = 2048
D_A = 4 * D_ATT
D_R = 2 * D_LRU + 2 * D_SSM
RG_C = 8.0


def peeled(eng, n, body, lead=1, tail=1):
    for i in range(lead):
        body(i, i == 0, False)
    with eng.Fori(lead, n - tail, 1) as i:
        body(i, False, False)
    for i in range(n - tail, n):
        body(i, False, i == n - 1)


def hold(eng, keep, sem, value):
    if not isinstance(value, int):
        value = eng.to_reg(value)
        eng.wait_ge(keep["loaded"], 16)
    eng.wait_ge(sem, value)


class Frame:

    def __init__(self, nc, ctx):
        self.nc, self.ctx, self.sems = nc, ctx, []
        ctx.callback(self.release)

    def release(self):
        self.nc.clear_and_free_semaphores(self.sems)
        self.nc.all_engine_barrier()

    def sb(self, name, shape, dt=F32):
        return self.ctx.enter_context(self.nc.sbuf_tensor(name, shape, dt))

    def ps(self, name, shape, dt=F32):
        return self.ctx.enter_context(self.nc.psum_tensor(name, shape, dt))

    def sem(self, name):
        self.sems.append(self.nc.alloc_semaphore(name))
        return self.sems[-1]


KC = SEQ // CH
KTILES = KC // P
TA, TBL = 16, 32
TWO_PI_HI = 6.28125
TWO_PI_LO = 2 * np.pi - TWO_PI_HI
PRE_ANGLE = 65
LN2_HI = 0.693359375
LN2_LO = float(np.log(2)) - LN2_HI
ROUND = 1.5 * 2.0 ** 23


def table_buffers(top):
    sb = lambda name, shape: top.sb(f"s_{name}", [P] + shape)
    return {
        "par": sb("par", [3, GROUPS]),
        "bc": sb("bc", [4, GROUPS, GC]),
        "sign": sb("sign", [1]),
        "v1": sb("v1", [13, GROUPS]),
        "mag": sb("mag", [CH + 1, GROUPS]),
        "un": sb("un", [2, CH + 1, GROUPS]),
        "pw": sb("pw", [2, CH + 1, GROUPS]),
        "wk": sb("wk", [2, GROUPS]),
        "tb": sb("tb", [2, GROUPS, TBL]),
        "ta": sb("ta", [2, GROUPS, TA]),
        "x12": sb("x12", [2, GROUPS, GC]),
    }


def ssm_tables(nc, pool, T, i32, x_tmp, tab4, chain, sines, inverted):
    par, bc, sign, v1, mag, un, pw, wk, tb, ta, x12 = (T[n] for n in (
        "par", "bc", "sign", "v1", "mag", "un", "pw", "wk", "tb", "ta", "x12"))
    count = [0]

    def step(op):
        count[0] += 1
        op.then_inc(chain, 1)
        pool.wait_ge(chain, count[0])

    def tt(out, a, b, op=ALU.mult):
        step(nc.gpsimd.tensor_tensor(out, a, b, op))

    def ts(out, a, s1, s2, op0, op1=None):
        step(nc.gpsimd.tensor_scalar(out, a, s1, s2, op0, op1) if op1 is not None else nc.gpsimd.tensor_scalar(out, a, s1, None, op0))

    s = lambda n: v1[:, n]

    def scaled_add(out, x, scale, y):
        ts(s(7), x, scale, None, ALU.mult)
        tt(out, s(7), y, ALU.add)
    lr, li = par[:, 0], par[:, 1]

    def exp(out, x, n, y, i32):
        ts(y, x, 88.0, -87.0, ALU.min, ALU.max)
        ts(n, y, 1 / np.log(2), ROUND, ALU.mult, ALU.add)
        ts(n, n, ROUND, None, ALU.subtract)
        scaled_add(y, n, -LN2_HI, y)
        scaled_add(y, n, -LN2_LO, y)
        ts(n, n, 127.0, 2.0 ** 23, ALU.add, ALU.mult)
        step(nc.gpsimd.tensor_copy(i32, n))
        ts(out, y, 1 / 5040, 1 / 720, ALU.mult, ALU.add)
        for k in (1 / 120, 1 / 24, 1 / 6, 1 / 2, 1.0, 1.0):
            tt(out, out, y)
            ts(out, out, k, None, ALU.add)
        tt(out, out, i32.bitcast(F32))
    tt(s(12), lr, lr)
    tt(s(3), li, li)
    tt(s(12), s(12), s(3), ALU.add)
    exp(s(0), par[:, 2], s(5), s(6), i32[:])
    tt(s(1), lr, s(0))
    exp(mag[:, 1], s(1), s(5), s(6), i32[:])
    for n in range(2, CH + 1):
        tt(mag[:, n], mag[:, n // 2], mag[:, n - n // 2])
    tt(s(2), li, s(0))
    ts(s(3), s(2), 1 / (2 * np.pi), ROUND, ALU.mult, ALU.add)
    ts(s(3), s(3), ROUND, None, ALU.subtract)
    scaled_add(s(2), s(3), -TWO_PI_HI, s(2))
    scaled_add(s(2), s(3), -TWO_PI_LO, s(2))
    ts(s(3), s(2), 3.1415925, -3.1415925, ALU.min, ALU.max)
    assert count[0] == PRE_ANGLE
    pool.wait_ge(sines, 2)
    U = lambda x, n: un[:, x, n]

    def unit(r, i):
        tt(s(10), r, r)
        tt(s(11), i, i)
        tt(s(10), s(10), s(11), ALU.add)
        ts(s(10), s(10), -0.5, 1.5, ALU.mult, ALU.add)
        tt(r, r, s(10))
        tt(i, i, s(10))

    def square(r2, i2, r, i):
        tt(s(8), r, r)
        tt(s(9), i, i)
        ts(s(11), r, 2.0, None, ALU.mult)
        tt(s(11), s(11), i)
        tt(r2, s(8), s(9), ALU.subtract)
        step(nc.gpsimd.tensor_copy(i2, s(11)))
        unit(r2, i2)

    def product(outs, a, b, temps):
        tt(temps[0], a[0], b[0])
        tt(temps[1], a[1], b[1])
        tt(temps[2], a[0], b[1])
        tt(temps[3], a[1], b[0])
        tt(outs[0], temps[0], temps[1], ALU.subtract)
        tt(outs[1], temps[2], temps[3], ALU.add)

    step(nc.gpsimd.memset(un[:, 0, 0], 1.0))
    step(nc.gpsimd.memset(un[:, 1, 0], 0.0))
    step(nc.gpsimd.memset(mag[:, 0], 1.0))
    step(nc.gpsimd.tensor_copy(U(1, 1), s(5)))
    tt(s(7), s(6), s(6))
    ts(U(0, 1), s(7), -2.0, 1.0, ALU.mult, ALU.add)
    unit(U(0, 1), U(1, 1))
    square(U(0, 2), U(1, 2), U(0, 1), U(1, 1))
    product((U(0, 3), U(1, 3)), (U(0, 2), U(1, 2)), (U(0, 1), U(1, 1)), [s(n) for n in range(8, 12)])
    square(U(0, 4), U(1, 4), U(0, 2), U(1, 2))
    for n in (1, 2, 3):
        product((U(0, 4 + n), U(1, 4 + n)), (U(0, 4), U(1, 4)), (U(0, n), U(1, n)), [s(n) for n in range(8, 12)])
    square(U(0, 8), U(1, 8), U(0, 4), U(1, 4))
    for x in range(2):
        tt(pw[:, x], un[:, x], mag[:])
    pool.wait_ge(inverted, 1)
    ts(s(3), pw[:, 0, 1], -1.0, None, ALU.add)
    yi = pw[:, 1, 1]
    tt(s(4), s(3), lr)
    tt(s(5), yi, li)
    tt(s(4), s(4), s(5), ALU.add)
    tt(s(4), s(4), s(12))
    tt(s(5), yi, lr)
    tt(s(6), s(3), li)
    tt(s(5), s(5), s(6), ALU.subtract)
    tt(s(5), s(5), s(12))
    wide = lambda x: x.rearrange("p (g o) -> p g o", o=1).broadcast_to([P, GROUPS, GC])
    ts(bc[:, 1], bc[:, 1], sign[:], None, ALU.mult)
    ts(bc[:, 2], bc[:, 2], sign[:], -1.0, ALU.mult, ALU.mult)
    ts(bc[:, 3], bc[:, 3], -1.0, None, ALU.mult)
    small = x_tmp
    tt(x12[:, 0], bc[:, 0], wide(s(4)))
    tt(small, bc[:, 1], wide(s(5)))
    tt(x12[:, 0], x12[:, 0], small, ALU.add)
    tt(x12[:, 1], bc[:, 1], wide(s(4)))
    tt(small, bc[:, 0], wide(s(5)))
    tt(x12[:, 1], x12[:, 1], small, ALU.subtract)

    for x in range(2):
        step(nc.gpsimd.tensor_copy(wk[:, x], U(x, 8)))
    for table, size in ((tb, TBL), (ta, TA)):
        step(nc.gpsimd.memset(table[:, 0, :, 0:1], 1.0))
        step(nc.gpsimd.memset(table[:, 1, :, 0:1], 0.0))
        n = 1
        while n < size:
            shape = [P, GROUPS, n]
            w = [wk[:, x].rearrange("p (g o) -> p g o", o=1).broadcast_to(shape) for x in range(2)]
            product([table[:, x, :, n:2 * n] for x in range(2)], [table[:, x, :, 0:n] for x in range(2)], w,
                    [tab4[:, k, :, 0:n] for k in range(4)])
            square(wk[:, 0], wk[:, 1], wk[:, 0], wk[:, 1])
            n *= 2


TB = 256
NB = SEQ // TB
SUB = TB // P


def project_attention(nc, t, keep):
    with ExitStack() as ctx:
        f = Frame(nc, ctx)
        w_hi = f.sb("wa_hi", [P, KT, D_A], F32R)
        w_lo = f.sb("wa_lo", [P, KT, D_A], F32R)
        w_raw = f.sb("wa_raw", [P, D_A])
        gain = f.sb("wa_gain", [P, KT])
        x_raw = f.sb("xa_raw", [P, 2, KT, TB])
        x_hi = f.sb("xa_hi", [P, 2, KT, TB], F32R)
        x_lo = f.sb("xa_lo", [P, 2, KT, TB], F32R)
        x_tok = f.sb("x_tok", [P, SUB, D])
        sq_sum = f.sb("sq_sum", [P, 2, SUB])
        rs = f.sb("rs_a", [P, 2, SUB])
        z = f.sb("z_a", [P, 2, D_A])
        qk_n = f.sb("qk_n", [P, 2, 2 * D_ATT])
        ss = f.sb("qk_ss", [P, 2, 2 * HEADS])
        qkT = f.sb("qkT_stage", [P, 2, 2 * PAIRS, P])
        T = keep["tables"]
        i32 = f.sb("s_i32", [P, GROUPS], mybir.dt.int32)
        x_tmp = f.sb("s_x_tmp", [P, GROUPS, GC])
        tab4 = f.sb("s_tab4", [P, 4, GROUPS, TA])
        par_loaded, chain, sines, inverted = f.sem("s_par_loaded"), f.sem("s_chain"), f.sem("s_sines"), f.sem("s_inverted")
        z_ps = f.ps("z_ps", [P, 2, 3, 512])
        t_ps = f.ps("t_ps", [P, 2, 512])
        gains = keep["qk_gain"]

        def stage(k):
            return w_raw[:] if k % STAGES == 2 else z[:, k % STAGES]

        gain_loaded, tok_loaded = f.sem("gain_loaded"), f.sem("tok_loaded")
        w_loaded = [f.sem(f"wa_loaded{j}") for j in range(STAGES)]
        x_loaded = [f.sem(f"xa_loaded{j}") for j in range(2)]
        w_hi_done, w_split = f.sem("wa_hi_done"), f.sem("wa_split")
        x_hi_done, x_split = f.sem("xa_hi_done"), f.sem("xa_split")
        squared, rs_done, rs_root = f.sem("squared"), f.sem("rs_done"), f.sem("rs_root")
        z_done, z_out = f.sem("z_done"), f.sem("z_out")
        qk_ss_done, qk_root, qk_normed = f.sem("qk_ss_done"), f.sem("qk_root"), f.sem("qk_normed")
        turned, turned_out = f.sem("turned"), f.sem("turned_out")
        vg_stored = [f.sem(f"vg_stored{j}") for j in range(2)]
        kn_stored = [f.sem(f"kn_stored{j}") for j in range(2)]
        qkT_stored = [f.sem(f"qkT_stored{j}") for j in range(2)]
        dve, rs_ready = f.sem("dve_a"), f.sem("rs_ready")
        rs_keep = keep["rs"]
        block = ctx.enter_context(nc.Block())
        NT = SEQ // P

        @block.sync
        def _(sp):
            def load_x(blk, j):
                sp.dma_start(x_raw[:, j], t["xT_p"][:, :, ds(blk * TB, TB)]).then_inc(x_loaded[j], 16)
            sp.dma_start(gain[:], t["norm_g"]).then_inc(gain_loaded, 16)
            for k in range(KT):
                if k >= STAGES:
                    sp.wait_ge(w_split, k - STAGES + 1)
                sp.dma_start(stage(k), t["w_att"][:, k]).then_inc(w_loaded[k % STAGES], 16)
                if k == 1:
                    load_x(0, 0)
                    for name in ("par", "bc", "sign"):
                        sp.dma_start(T[name][:], t[f"ssm_{name}"]).then_inc(par_loaded, 16)

            def load_tokens(blk, first):
                if not first:
                    hold(sp, keep, squared, SUB * blk)
                src = t["x_p"].rearrange("(n p) d -> p n d", p=P)
                sp.dma_start(x_tok[:], src[:, ds(blk * SUB, SUB)]).then_inc(tok_loaded, 16)
            load_tokens(0, True)

            def store(tile, s, at, rows):
                hold(sp, keep, z_out, tile + 1)
                sp.dma_start(t["v_all"][at, :], z[0:rows, s, 2 * D_ATT:3 * D_ATT]).then_inc(vg_stored[s], 16)
                sp.dma_start(t["gc_all"][at, :], z[0:rows, s, 3 * D_ATT:]).then_inc(vg_stored[s], 16)
                hold(sp, keep, qk_normed, tile + 1)
                sp.dma_start(t["k_all"][at, :], qk_n[0:rows, s, D_ATT:]).then_inc(kn_stored[s], 16)

            def store_turned(tile, b, at, rows):
                hold(sp, keep, turned_out, tile + 1)
                sp.dma_start(t["qkT_all"][:, :, at], qkT[:, b, :, 0:rows]).then_inc(qkT_stored[b], 16)

            def stores(blk, first):
                for s in range(SUB):
                    tile = blk * SUB + s
                    store(tile, s, ds(tile * P, P), P)
                    if not (first and s == 0):
                        store_turned(tile - 1, (s + 1) % 2, ds((tile - 1) * P, P), P)

            def body(i, first, last):
                for j in range(2):
                    if not first:
                        hold(sp, keep, x_split, 2 * i + j - 1)
                        hold(sp, keep, x_hi_done, 2 * i + j - 1)
                    if not (first and j == 0):
                        load_x(2 * i + j, j)
                        load_tokens(2 * i + j, False)
                    if not (first and j == 0):
                        stores(2 * i + j - 1, first)
            peeled(sp, NB // 2, body)
            hold(sp, keep, x_split, NB - 1)
            sp.dma_start(x_raw[:, 0, :, 0:SMP], t["xT_s"]).then_inc(x_loaded[0], 16)
            hold(sp, keep, squared, SUB * NB)
            sp.dma_start(x_tok[0:SMP, 0], t["x_s"]).then_inc(tok_loaded, 16)
            stores(NB - 1, False)
            store(NT, 0, slice(SEQ, SEQ + SMP), SMP)
            store_turned(NT - 1, 1, slice(SEQ - P, SEQ), P)
            store_turned(NT, 0, slice(SEQ, SEQ + SMP), SMP)
            for s, n in ((0, NT // 2 + 1), (1, NT // 2)):
                sp.wait_ge(vg_stored[s], 32 * n)
                sp.wait_ge(kn_stored[s], 16 * n)
                sp.wait_ge(qkT_stored[s], 16 * n)

        @block.gpsimd
        def _(pool):
            pool.wait_ge(par_loaded, 48)
            ssm_tables(nc, pool, T, i32, x_tmp[:], tab4, chain, sines, inverted)

        @block.tensor
        def _(pe):
            def products(tile, j, s, rows, free_count):
                b = s % 2
                if free_count is not None:
                    pe.wait_ge(z_out, free_count)
                for c in range(3):
                    for k in range(KT):
                        xh = x_hi[:, j, k, s * P:s * P + rows]
                        xl = x_lo[:, j, k, s * P:s * P + rows]
                        out = z_ps[0:rows, b, c]
                        cols = slice(c * 512, c * 512 + 512)
                        pe.matmul(out, xh, w_hi[:, k, cols], start=(k == 0), stop=False)
                        pe.matmul(out, xh, w_lo[:, k, cols], start=False, stop=False)
                        last = pe.matmul(out, xl, w_hi[:, k, cols], start=False, stop=(k == KT - 1))
                last.then_inc(z_done, 1)

            def turn(tile, b, rows, free_count):
                pe.wait_ge(qk_normed, tile + 1)
                if free_count is not None:
                    pe.wait_ge(turned_out, free_count)
                for c in range(2 * PAIRS):
                    last = pe.transpose(t_ps[:, c // 3, (c % 3) * P:(c % 3) * P + rows],
                                        qk_n[0:rows, b, c * P:(c + 1) * P], keep["ident"][0:rows, 0:rows])
                last.then_inc(turned, 1)

            pe.wait_ge(w_split, KT)

            def body(i, first, last):
                for j in range(2):
                    pe.wait_ge(x_split, 2 * i + j + 1)
                    for s in range(SUB):
                        tile = (2 * i + j) * SUB + s
                        early = first and j == 0
                        products(tile, j, s, P, None if early else tile - 1)
                        if not (early and s == 0):
                            turn(tile - 1, (s + 1) % 2, P, None if (early and s == 1) else tile - 1)
            peeled(pe, NB // 2, body)
            pe.wait_ge(x_split, NB + 1)
            products(NT, 0, 0, SMP, NT - 1)
            turn(NT - 1, 1, P, NT - 1)
            turn(NT, 0, SMP, NT)

        @block.scalar
        def _(act):
            def split(nth, j, n):
                act.wait_ge(x_loaded[j], (nth + 1) * 16)
                act.activation(x_hi[:, j, :, 0:n], x_raw[:, j, :, 0:n], ACT.Copy).then_inc(x_hi_done, 1)

            def squares(blk, j, tiles, rows):
                act.wait_ge(tok_loaded, (blk + 1) * 16)
                for s in range(tiles):
                    act.activation(x_tok[0:rows, s], x_tok[0:rows, s], ACT.Square,
                                   accum_out=sq_sum[0:rows, j, s:s + 1]).then_inc(squared, 1)

            def copy_out(tile, j, s, rows):
                act.wait_ge(z_done, tile + 1)
                for c in range(3):
                    last = act.activation(z[0:rows, s, c * 512:c * 512 + 512], z_ps[0:rows, s, c], ACT.Copy,
                                          scale=rs[0:rows, j, s:s + 1])
                last.then_inc(z_out, 1)

            def qk_sqrt(tile, s, rows):
                act.wait_ge(qk_ss_done, tile + 1)
                act.activation(ss[0:rows, s], ss[0:rows, s], ACT.Sqrt).then_inc(qk_root, 1)

            def sqrt_rs(blk, j, rows, tiles):
                act.wait_ge(rs_done, blk + 1)
                act.activation(sq_sum[0:rows, j, 0:tiles], sq_sum[0:rows, j, 0:tiles], ACT.Sqrt).then_inc(rs_root, 1)

            def body(i, first, last):
                for j in range(2):
                    blk = 2 * i + j
                    early = first and j == 0
                    squares(blk, j, SUB, P)
                    sqrt_rs(blk, j, P, SUB)
                    act.wait_ge(rs_ready, blk + 1)
                    for s in range(SUB):
                        tile = blk * SUB + s
                        if not early:
                            act.wait_ge(vg_stored[s], 32 * blk)
                            act.wait_ge(qk_normed, tile - 1)
                        if s == 0:
                            if not early:
                                act.wait_ge(z_done, blk * SUB)
                            split(i + j, (j + 1) % 2, SMP if last and j else TB)
                        copy_out(tile, j, s, P)
                        qk_sqrt(tile, s, P)

            act.wait_ge(gain_loaded, 16)
            for k in range(KT):
                act.wait_ge(w_loaded[k % STAGES], 16 * (k // STAGES + 1))
                act.activation(w_hi[:, k], stage(k), ACT.Copy, scale=gain[:, k:k + 1]).then_inc(w_hi_done, 1)
                if k == 3:
                    split(0, 0, TB)
            act.wait_ge(chain, PRE_ANGLE)
            act.activation(T["v1"][:, 5], T["v1"][:, 3], ACT.Sin).then_inc(sines, 1)
            act.activation(T["v1"][:, 6], T["v1"][:, 3], ACT.Sin, scale=0.5).then_inc(sines, 1)
            peeled(act, NB // 2, body)
            squares(NB, 0, 1, SMP)
            sqrt_rs(NB, 0, SMP, 1)
            act.wait_ge(rs_ready, NB + 1)
            act.wait_ge(vg_stored[0], 32 * NB)
            act.wait_ge(qk_normed, NT - 1)
            copy_out(NT, 0, 0, SMP)
            qk_sqrt(NT, 0, SMP)

        @block.vector
        def _(v):
            v.wait_ge(gain_loaded, 16)
            for k in range(KT):
                v.wait_ge(w_hi_done, k + 1)
                v.scalar_tensor_tensor(w_lo[:, k], stage(k), gain[:, k:k + 1], w_hi[:, k].bitcast(F32),
                                       ALU.mult, ALU.subtract).then_inc(w_split, 1)
            v.wait_ge(chain, 3)
            v.reciprocal(T["v1"][:, 12], T["v1"][:, 12]).then_inc(inverted, 1)

            def lows(blk, j, n):
                v.wait_ge(x_hi_done, blk + 1)
                v.tensor_tensor(x_lo[:, j, :, 0:n], x_raw[:, j, :, 0:n], x_hi[:, j, :, 0:n].bitcast(F32),
                                ALU.subtract).then_inc(x_split, 1)

            def inv_rms(blk, j, rows, tiles, col):
                v.wait_ge(squared, blk * SUB + tiles)
                v.tensor_scalar(sq_sum[0:rows, j, 0:tiles], sq_sum[0:rows, j, 0:tiles], 1.0 / D, EPS,
                                ALU.mult, ALU.add).then_inc(rs_done, 1)
                v.wait_ge(rs_root, blk + 1)
                v.reciprocal(rs[0:rows, j, 0:tiles], sq_sum[0:rows, j, 0:tiles]).then_inc(rs_ready, 1)
                v.wait_ge(rs_ready, blk + 1)
                v.tensor_copy(rs_keep[0:rows, col], rs[0:rows, j, 0:tiles])

            def qk_norm(tile, s, rows, n):
                v.wait_ge(z_out, tile + 1)
                if n is not None:
                    v.wait_ge(turned, tile - 1)
                    v.wait_ge(kn_stored[s], 16 * n)
                qk = z[0:rows, s, 0:2 * D_ATT]
                out = qk_n[0:rows, s]
                v.tensor_tensor(out, qk, qk, ALU.mult).then_inc(dve, 1)
                v.wait_ge(dve, 4 * tile + 1)
                v.tensor_reduce(ss[0:rows, s], out.rearrange("p (h d) -> p h d", d=DH), AX.X, ALU.add).then_inc(dve, 1)
                v.wait_ge(dve, 4 * tile + 2)
                v.tensor_scalar(ss[0:rows, s], ss[0:rows, s], 1.0 / DH, EPS, ALU.mult, ALU.add).then_inc(qk_ss_done, 1)
                v.wait_ge(qk_root, tile + 1)
                v.reciprocal(ss[0:rows, s], ss[0:rows, s]).then_inc(dve, 1)
                v.wait_ge(dve, 4 * tile + 3)
                r = ss[0:rows, s].rearrange("p (h o) -> p h o", o=1).broadcast_to([rows, 2 * HEADS, DH])
                v.tensor_tensor(out.rearrange("p (h d) -> p h d", d=DH), qk.rearrange("p (h d) -> p h d", d=DH), r,
                                ALU.mult).then_inc(dve, 1)
                v.wait_ge(dve, 4 * tile + 4)
                v.tensor_tensor(out, out, gains[0:rows], ALU.mult).then_inc(qk_normed, 1)

            def turned_copy(tile, b, rows, n):
                v.wait_ge(turned, tile + 1)
                if n is not None:
                    v.wait_ge(qkT_stored[b], 16 * n)
                for c in range(2):
                    last = v.tensor_copy(qkT[:, b, 3 * c:3 * c + 3, 0:rows],
                                         t_ps[:, c, 0:3 * P].rearrange("p (c t) -> p c t", c=3)[:, :, 0:rows])
                last.then_inc(turned_out, 1)

            def body(i, first, last):
                for j in range(2):
                    blk = 2 * i + j
                    early = first and j == 0
                    inv_rms(blk, j, P, SUB, ds(blk * SUB, SUB))
                    for s in range(SUB):
                        tile = blk * SUB + s
                        if s == 0:
                            if not early:
                                v.wait_ge(z_done, blk * SUB)
                            lows(blk + 1, (j + 1) % 2, SMP if last and j else TB)
                        qk_norm(tile, s, P, None if early else blk)
                        if not (early and s == 0):
                            turned_copy(tile - 1, (s + 1) % 2, P, None if early or (first and s == 0) else blk - 1 + s)
            lows(0, 0, TB)
            peeled(v, NB // 2, body)
            inv_rms(NB, 0, SMP, 1, slice(NT, NT + 1))
            qk_norm(NT, 0, SMP, NB)
            turned_copy(NT - 1, 1, P, NB - 1)
            turned_copy(NT, 0, SMP, NB)



def project_recurrent(nc, t, keep):
    with ExitStack() as ctx:
        f = Frame(nc, ctx)
        w_hi = f.sb("wr_hi", [P, KT, D_R], F32R)
        w_lo = f.sb("wr_lo", [P, KT, D_R], F32R)
        gain = f.sb("wr_gain", [P, KT])
        x_raw = f.sb("xr_raw", [P, 2, KT * TB])
        x_hi = f.sb("xr_hi", [P, 2, KT, TB], F32R)
        x_lo = f.sb("xr_lo", [P, 2, KT, TB], F32R)
        ones = f.sb("ones_r", [P, P])
        rs_wide = f.sb("rs_wide", [P, SUB, P])
        rs_row = f.sb("rs_row", [P, 2, TB])
        xa = f.sb("xa", [P, 2, LT, CONV_W - 1 + TB])
        xc = f.sb("xc", [P, 2, LT, TB])
        g = f.sb("ga", [P, 2, LT, TB])
        sg = f.sb("sg", [P, 2, LT, TB])
        r = f.sb("r", [P, LT, TB])
        ig = f.sb("ig", [P, LT, TB])
        q = f.sb("q", [P, LT, TB])
        y = f.sb("ya", [P, 2, LT, TB])
        inv = f.sb("inv_a", [P, TB])
        ug = f.sb("ug", [P, SUB, 2 * D_SSM])
        cw = f.sb("cw", [P, LT, CONV_W])
        vec = f.sb("lru_vec", [P, 5, LT])
        wg = f.sb("wg", [P, 2, LT, P])
        lam = f.sb("lam", [P, 3, LT])
        carry = f.sb("h_carry", [P, LT])
        eps = f.sb("eps_r", [P, 1])
        conv_s = f.sb("conv_s_in", [P, LT, NS, 3])
        h_s = f.sb("h_s_in", [P, LT, NS])
        xs = f.sb("xa_s", [P, LT, NS, 3 + TS])

        ch_ps = f.ps("ch_ps", [P, LT, 512])
        tok_ps = f.ps("tok_ps", [P, SUB, 512])
        gate_ps = f.ps("gate_ps", [P, 2, 512])
        row_ps = f.ps("row_ps", [P, 512])

        gain_loaded = f.sem("gainr_loaded")
        outs_copied = f.sem("outs_copied")
        w_loaded = [f.sem(f"wr_loaded{j}") for j in range(STAGES)]
        x_loaded = [f.sem(f"xr_loaded{j}") for j in range(2)]
        w_hi_done, w_split = f.sem("wr_hi_done"), f.sem("wr_split")
        x_scaled, x_hi_done, x_split = f.sem("xr_scaled"), f.sem("xr_hi_done"), f.sem("xr_split")
        rs_spread, rs_turned, rs_copied = f.sem("rs_spread"), f.sem("rs_turned"), f.sem("rs_copied")
        ch_done, xa_out, ga_out = f.sem("ch_done"), f.sem("xa_out"), f.sem("ga_out")
        tok_done, tok_out = f.sem("tok_done"), f.sem("tok_out")
        ug_stored = [f.sem(f"ug_stored{j}") for j in range(SUB)]
        y_stored = [f.sem(f"ya_stored{j}") for j in range(2)]
        silu_sig, conv_done, gates_done, gates_out = f.sem("silu_sig"), f.sem("conv_done"), f.sem("gates_done"), f.sem("gates_out")
        tanh_done, root_done, squared = f.sem("tanh_done"), f.sem("root_done"), f.sem("ya_squared")
        ss_done, ss_root, y_done = f.sem("ss_done"), f.sem("ss_root"), f.sem("ya_done")
        lru, conv, setup, setup_act = f.sem("lru_step"), f.sem("conv_step"), f.sem("lru_setup"), f.sem("lru_setup_act")
        ini, state_out = f.sem("lru_inputs"), f.sem("state_out")
        r_out, state_step, inv_done, carried = f.sem("r_out"), f.sem("state_step"), f.sem("inv_done"), f.sem("carried")
        block = ctx.enter_context(nc.Block())
        x_raw4 = x_raw.rearrange("p j (k n) -> p j k n", k=KT)

        def stage(k):
            return x_raw.rearrange("p j n -> p (j n)")[:, k % STAGES * D_R:(k % STAGES + 1) * D_R]
        NLRU = 9 * LT
        L_ADD, L_REC, L_MUL, L_A, L_I, L_X, L_SCAN, L_G, L_Y = range(9)

        def lru_count(b, step, ch):
            return NLRU * b + LT * step + ch + 1

        @block.sync
        def _(sp):
            sp.dma_start(gain[:], t["norm_g"]).then_inc(gain_loaded, 16)
            for k in range(KT):
                if k >= STAGES:
                    sp.wait_ge(w_split, k - STAGES + 1)
                sp.dma_start(stage(k), t["w_rec"][:, k]).then_inc(w_loaded[k % STAGES], 16)
                if k == KT - 1:
                    sp.dma_start(cw[:], t["conv_w"]).then_inc(ini, 16)
                    sp.dma_start(vec[:], t["lru_vec"]).then_inc(ini, 16)
                    sp.dma_start(conv_s[:], t["state_conv"]).then_inc(ini, 16)
                    sp.dma_start(h_s[:], t["state_lru"]).then_inc(ini, 16)
                    sp.wait_ge(setup, 1)
                    for n, name in enumerate(("w_r", "w_i")):
                        for b in range(6):
                            o = 64 * (b % 2)
                            sp.dma_start(wg[o:o + 64, n, b // 2, o:o + 64], t[name][b]).then_inc(ini, 16)

            def load(nth, j, at):
                if not (isinstance(nth, int) and nth == 0):
                    hold(sp, keep, x_split, 2 * nth + j - 1)
                sp.dma_start(x_raw4[:, j], t["xT_p"][:, :, ds(at, TB)]).then_inc(x_loaded[j], 16)

            def store_tokens(blk, s, at, rows):
                hold(sp, keep, tok_out, SUB * blk + s + 1)
                sp.dma_start(t["ug_all"][at, :], ug[0:rows, s]).then_inc(ug_stored[s], 16)

            def store_y(blk, j, at, n):
                hold(sp, keep, y_done, LT * (blk + 1))
                sp.dma_start(t["yaT_all"][:, :, at], y[:, j, :, 0:n]).then_inc(y_stored[j], 16)

            sp.wait_ge(w_split, KT)
            load(0, 0, 0)
            load(0, 1, TB)
            for name, rows in (("k", slice(SEQ - KEEP, SEQ)), ("v", slice(SEQ - KEEP, SEQ))):
                sp.dma_start(t[f"{name}_p"], t[f"{name}_all"][rows, :]).then_inc(outs_copied, 16)
                sp.dma_start(t[f"{name}_s"], t[f"{name}_all"][SEQ:SEQ + SMP, :]).then_inc(outs_copied, 16)

            def body(i, first, last):
                for j in range(2):
                    b = 2 * i + j
                    if not last:
                        load(i + 1, j, (b + 2) * TB)
                    elif j == 0:
                        sp.wait_ge(x_split, NB - 1)
                        sp.dma_start(x_raw4[:, 0, :, 0:SMP], t["xT_s"]).then_inc(x_loaded[0], 16)
                    for s in range(SUB):
                        store_tokens(b, s, ds(b * TB + s * P, P), P)
                    if not first:
                        store_y(b - 2, j, ds((b - 2) * TB, TB), TB)
            peeled(sp, NB // 2, body, 2)
            store_tokens(NB, 0, slice(SEQ, SEQ + SMP), SMP)
            store_y(NB - 2, 0, ds((NB - 2) * TB, TB), TB)
            store_y(NB - 1, 1, ds((NB - 1) * TB, TB), TB)
            sp.dma_start(t["conv_p"], xa[:, 1, :, TB:]).then_inc(state_out, 16)
            sp.dma_start(t["lru_p"], carry[:]).then_inc(state_out, 16)
            store_y(NB, 0, slice(SEQ, SEQ + SMP), SMP)
            sp.wait_ge(state_step, 5)
            sp.dma_start(t["lru_s"], h_s[:]).then_inc(state_out, 16)
            for c in range(LT):
                sp.dma_start(t["conv_s"][:, c], xs[:, c, :, TS:]).then_inc(state_out, 16)
            sp.wait_ge(state_out, 48 + 16 * LT)
            sp.wait_ge(outs_copied, 64)
            sp.wait_ge(ug_stored[0], 16 * (NB + 1))
            sp.wait_ge(ug_stored[1], 16 * NB)
            sp.wait_ge(y_stored[0], 16 * (NB // 2 + 1))
            sp.wait_ge(y_stored[1], 16 * (NB // 2))

        @block.gpsimd
        def _(pool):
            nc.gpsimd.memset(wg[:], 0.0).then_inc(setup, 1)
            nc.gpsimd.memset(ones[:], 1.0).then_inc(setup, 1)
            nc.gpsimd.memset(eps[:], EPS).then_inc(setup, 1)

            def scale(b, nth, j, n):
                pool.wait_ge(x_loaded[j], 16 * (nth + 1))
                pool.wait_ge(rs_copied, b + 1)
                for k in range(KT):
                    last = nc.gpsimd.tensor_tensor(x_raw4[:, j, k, 0:n], x_raw4[:, j, k, 0:n], rs_row[:, j, 0:n], ALU.mult)
                last.then_inc(x_scaled, 1)
            scale(0, 0, 0, TB)

            def body(i, first, last):
                for j in range(2):
                    b = 2 * i + j
                    scale(b + 1, i + j, (j + 1) % 2, SMP if last and j else TB)
            peeled(pool, NB // 2, body, 2)

        @block.tensor
        def _(pe):
            def spread_rows(b, j, n):
                pe.wait_ge(rs_spread, b + 1)
                for s in range(-(-n // P)):
                    rows = min(P, n - s * P)
                    last = pe.matmul(row_ps[:, s * P:s * P + rows], rs_wide[0:rows, s, :],
                                     keep["ident"][0:rows, 0:rows], start=(s == 0), stop=True, skip_group_check=True)
                last.then_inc(rs_turned, 1)

            def channels(b, j, c, n):
                for k in range(KT):
                    out = ch_ps[:, c % LT, 0:n]
                    cols = slice(c * P, c * P + P)
                    pe.matmul(out, w_hi[:, k, cols], x_hi[:, j, k, 0:n], start=(k == 0), stop=False)
                    pe.matmul(out, w_hi[:, k, cols], x_lo[:, j, k, 0:n], start=False, stop=False)
                    last = pe.matmul(out, w_lo[:, k, cols], x_hi[:, j, k, 0:n], start=False, stop=(k == KT - 1))
                last.then_inc(ch_done, 1)

            def tokens(j, s, rows):
                for k in range(KT):
                    xh = x_hi[:, j, k, s * P:s * P + rows]
                    out = tok_ps[0:rows, s]
                    cols = slice(2 * D_LRU, D_R)
                    pe.matmul(out, xh, w_hi[:, k, cols], start=(k == 0), stop=False)
                    pe.matmul(out, xh, w_lo[:, k, cols], start=False, stop=False)
                    last = pe.matmul(out, x_lo[:, j, k, s * P:s * P + rows], w_hi[:, k, cols], start=False, stop=(k == KT - 1))
                last.then_inc(tok_done, 1)

            def gates(b, j, n):
                for c in range(LT):
                    pe.wait_ge(conv_done, LT * b + c + 1)
                    if not (isinstance(b, int) and b == 0 and c < 2):
                        pe.wait_ge(gates_out, LT * b + max(c - 1, 0))
                    for m in range(2):
                        last = pe.matmul(gate_ps[:, c % 2, m * TB:m * TB + n],
                                         wg[:, m, c], xc[:, j, c, 0:n], start=True, stop=True)
                    last.then_inc(gates_done, 1)

            def sum_squares(b, j, n):
                pe.wait_ge(squared, LT * (b + 1))
                for c in range(LT):
                    last = pe.matmul(row_ps[:, TB:TB + n], ones[:], sg[:, j, c, 0:n], start=(c == 0), stop=(c == LT - 1))
                last.then_inc(ss_done, 1)

            pe.wait_ge(setup, 3)
            pe.wait_ge(ini, 16 * 16)
            spread_rows(0, 0, TB)

            def main(b, j, n, first, last, is_first_block, tail):
                early = isinstance(b, int)
                pe.wait_ge(x_split, b + 1)
                for c in range(LT):
                    if not is_first_block:
                        pe.wait_ge(ga_out, LT * (b - 1) + c + 1)
                    channels(b, j, c, n)
                    if c == 0 and not tail:
                        if not (early and b < 3):
                            pe.wait_ge(ss_root, b - 2)
                        pe.wait_ge(rs_copied, b + 1)
                        spread_rows(b + 1, (j + 1) % 2, SMP if (last and j) else TB)
                if not (early and b < 2):
                    pe.wait_ge(rs_copied, min(b + 2, NB + 1) if early else b + 2)
                    sum_squares(b - 2, j, TB)
                if not is_first_block:
                    gates(b - 1, (j + 1) % 2, TB)
                for c in range(LT):
                    pe.wait_ge(xa_out, LT * b + c + 1)
                    channels(b, j, LT + c, n)
                for s in range(-(-n // P)):
                    if not is_first_block:
                        pe.wait_ge(tok_out, SUB * (b - 1) + s + 1)
                    tokens(j, s, min(P, n))

            def body(i, first, last):
                for j in range(2):
                    main(2 * i + j, j, TB, first, last, first and j == 0, False)
            peeled(pe, NB // 2, body, 2)
            main(NB, 0, SMP, False, True, False, True)
            pe.wait_ge(ss_root, NB - 1)
            sum_squares(NB - 1, 1, TB)
            gates(NB, 0, SMP)
            pe.wait_ge(ss_root, NB)
            sum_squares(NB, 0, SMP)

        @block.scalar
        def _(act):
            act.wait_ge(gain_loaded, 16)
            for k in range(KT):
                act.wait_ge(w_loaded[k % STAGES], 16 * (k // STAGES + 1))
                act.activation(w_hi[:, k], stage(k), ACT.Copy, scale=gain[:, k:k + 1]).then_inc(w_hi_done, 1)
            act.wait_ge(ini, 16 * 16)
            act.activation(lam[:, 0], vec[:, 3], ACT.Abs).then_inc(setup_act, 1)
            act.wait_ge(setup_act, 1)
            act.activation(lam[:, 0], lam[:, 0], ACT.Exp, scale=-1.0).then_inc(setup_act, 1)
            act.wait_ge(setup_act, 2)
            act.activation(lam[:, 0], lam[:, 0], ACT.Ln, bias=1.0).then_inc(setup_act, 1)
            act.wait_ge(setup_act, 4)

            def copy_rows(b, j, n):
                act.wait_ge(rs_turned, b + 1)
                act.activation(rs_row[:, j, 0:n], row_ps[:, 0:n], ACT.Copy).then_inc(rs_copied, 1)

            def split(b, j, n):
                act.wait_ge(x_scaled, b + 1)
                act.activation(x_hi[:, j, :, 0:n], x_raw4[:, j, :, 0:n], ACT.Copy).then_inc(x_hi_done, 1)

            def gate_functions(b, j, n):
                for c in range(LT):
                    act.wait_ge(gates_done, LT * b + c + 1)
                    if not (isinstance(b, int) and b == 0):
                        act.wait_ge(lru, lru_count(b - 1, L_SCAN, c))
                    act.activation(r[:, c, 0:n], gate_ps[:, c % 2, 0:n], ACT.Sigmoid, bias=vec[:, 1, c:c + 1]).then_inc(r_out, 1)
                    act.activation(ig[:, c, 0:n], gate_ps[:, c % 2, TB:TB + n], ACT.Sigmoid, bias=vec[:, 2, c:c + 1]).then_inc(gates_out, 1)
                for c in range(LT):
                    act.wait_ge(r_out, LT * b + c + 1)
                    act.activation(r[:, c, 0:n], r[:, c, 0:n], ACT.Tanh, scale=lam[:, 1, c:c + 1]).then_inc(tanh_done, 1)

            def roots(b, j, n):
                for c in range(LT):
                    act.wait_ge(lru, lru_count(b, L_ADD, c))
                    act.activation(r[:, c, 0:n], r[:, c, 0:n], ACT.Sqrt).then_inc(root_done, 1)

            def squares(b, j, n):
                for c in range(LT):
                    act.wait_ge(lru, lru_count(b, L_Y, c))
                    act.activation(sg[:, j, c, 0:n], g[:, j, c, 0:n], ACT.Square).then_inc(squared, 1)

            def norm_root(b, n):
                act.wait_ge(ss_done, b + 1)
                if not (isinstance(b, int) and b == 0):
                    act.wait_ge(y_done, LT * b)
                act.activation(inv[:, 0:n], row_ps[:, TB:TB + n], ACT.Sqrt, scale=1.0 / D_LRU, bias=eps[:]).then_inc(ss_root, 1)

            copy_rows(0, 0, TB)
            split(0, 0, TB)

            def main(b, nth, j, n, is_first, second, last, tail):
                for c in range(LT):
                    act.wait_ge(ch_done, 2 * LT * b + c + 1)
                    if not (is_first or second):
                        act.wait_ge(conv_done, LT * (b - 1) + 1)
                    dst = xs[:, c, :, 3:] if tail else xa[:, j, c, CONV_W - 1:]
                    src = ch_ps[:, c, 0:n]
                    act.activation(dst, src.rearrange("p (n k) -> p n k", k=TS) if tail else src, ACT.Copy).then_inc(xa_out, 1)
                    if c == 0 and not tail:
                        copy_rows(b + 1, (j + 1) % 2, SMP if last and j else TB)
                if not (is_first or second):
                    squares(b - 2, j, TB)
                    norm_root(b - 2, TB)
                if not is_first:
                    gate_functions(b - 1, (j + 1) % 2, TB)
                if not tail:
                    if not is_first:
                        act.wait_ge(tok_done, SUB * b)
                    split(b + 1, (j + 1) % 2, SMP if last and j else TB)
                for c in range(LT):
                    act.wait_ge(ch_done, 2 * LT * b + LT + c + 1)
                    if not (is_first or second):
                        act.wait_ge(y_done, LT * (b - 2) + c + 1)
                    act.activation(g[:, j, c, 0:n], ch_ps[:, c, 0:n], ACT.Copy).then_inc(ga_out, 1)
                for c in range(LT):
                    act.wait_ge(ga_out, LT * b + c + 1)
                    if not (is_first or second):
                        act.wait_ge(ss_done, b - 1)
                    act.activation(sg[:, j, c, 0:n], g[:, j, c, 0:n], ACT.Sigmoid).then_inc(silu_sig, 1)
                if not is_first:
                    roots(b - 1, (j + 1) % 2, TB)
                for s in range(-(-n // P)):
                    rows = min(P, n)
                    act.wait_ge(tok_done, SUB * b + s + 1)
                    if not is_first:
                        act.wait_ge(ug_stored[s], 16 * b)
                    act.activation(ug[0:rows, s], tok_ps[0:rows, s], ACT.Copy).then_inc(tok_out, 1)

            def body(i, first, last):
                for j in range(2):
                    main(2 * i + j, i, j, TB, first and j == 0, first and j == 1, last, False)
            peeled(act, NB // 2, body, 2)
            main(NB, NB // 2, 0, SMP, False, False, True, True)
            squares(NB - 1, 1, TB)
            norm_root(NB - 1, TB)
            gate_functions(NB, 0, SMP)
            roots(NB, 0, SMP)
            squares(NB, 0, SMP)
            norm_root(NB, SMP)

        @block.vector
        def _(v):
            v.wait_ge(gain_loaded, 16)
            for k in range(KT):
                v.wait_ge(w_hi_done, k + 1)
                v.scalar_tensor_tensor(w_lo[:, k], stage(k), gain[:, k:k + 1], w_hi[:, k].bitcast(F32),
                                       ALU.mult, ALU.subtract).then_inc(w_split, 1)
            v.wait_ge(ini, 16 * 16)
            v.wait_ge(setup_act, 3)
            v.tensor_scalar(lam[:, 2], vec[:, 3], -1.0, 0.0, ALU.mult, ALU.max).then_inc(conv, 1)
            v.wait_ge(conv, 1)
            v.tensor_tensor(lam[:, 2], lam[:, 2], lam[:, 0], ALU.add).then_inc(conv, 1)
            v.wait_ge(conv, 2)
            v.tensor_scalar(lam[:, 1], lam[:, 2], RG_C / 2, None, ALU.mult).then_inc(setup_act, 1)
            v.wait_ge(setup, 3)

            def spread(b, n, cols):
                if not (isinstance(b, int) and b == 0):
                    v.wait_ge(rs_turned, b)
                for s in range(-(-n // P)):
                    rows = min(P, n)
                    last = v.tensor_scalar(rs_wide[0:rows, s], ones[0:rows], keep["rs"][0:rows, cols(s)], None, ALU.mult)
                last.then_inc(rs_spread, 1)

            def lows(b, j, n):
                v.wait_ge(x_hi_done, b + 1)
                v.tensor_tensor(x_lo[:, j, :, 0:n], x_raw4[:, j, :, 0:n], x_hi[:, j, :, 0:n].bitcast(F32),
                                ALU.subtract).then_inc(x_split, 1)

            NCONV = 3 * LT + 1

            def convolve(b, nth, j, is_first, src, out):
                base = NCONV * b + 2
                if src is None:
                    v.wait_ge(xa_out, LT * (b + 1))
                    if is_first:
                        v.memset(xa[:, j, :, 0:CONV_W - 1], 0.0).then_inc(conv, 1)
                    else:
                        v.tensor_copy(xa[:, j, :, 0:CONV_W - 1], xa[:, (j + 1) % 2, :, TB:]).then_inc(conv, 1)
                    v.wait_ge(conv, base + 1)
                    src = lambda c, k: xa[:, j, c, k:k + TB]
                for c in range(LT):
                    v.tensor_scalar(out(c), src(c, 0), cw[:, c, 0:1], vec[:, 0, c:c + 1], ALU.mult, ALU.add).then_inc(conv, 1)
                for k in range(1, CONV_W):
                    for c in range(LT):
                        v.wait_ge(conv, base + 1 + LT * (k - 1) + c + 1)
                        v.scalar_tensor_tensor(out(c), src(c, k), cw[:, c, k:k + 1], out(c), ALU.mult,
                                               ALU.add).then_inc(conv if k < CONV_W - 1 else conv_done, 1)

            def recur(b, j, n, is_first, sample):
                def step(kind, op):
                    for c in range(LT):
                        if kind > 0:
                            v.wait_ge(lru, lru_count(b, kind - 1, c))
                        op(c).then_inc(lru, 1)

                R, Q, I = (lambda c: r[:, c, 0:n]), (lambda c: q[:, c, 0:n]), (lambda c: ig[:, c, 0:n])
                X, G, S = (lambda c: xc[:, j, c, 0:n]), (lambda c: g[:, j, c, 0:n]), (lambda c: sg[:, j, c, 0:n])
                v.wait_ge(tanh_done, LT * (b + 1))
                step(L_ADD, lambda c: v.tensor_scalar(Q(c), R(c), 1.0, None, ALU.add))
                step(L_REC, lambda c: v.reciprocal(Q(c), Q(c)))
                v.wait_ge(root_done, LT * (b + 1))
                step(L_MUL, lambda c: v.scalar_tensor_tensor(R(c), R(c), 2.0, Q(c), ALU.mult, ALU.mult))
                if is_first:
                    v.wait_ge(lru, lru_count(b, L_MUL, LT - 1))
                    v.memset(r[:, :, 0:1], 1.0).then_inc(state_step, 1)
                    v.wait_ge(state_step, 1)
                step(L_A, lambda c: v.tensor_scalar(Q(c), Q(c), 2.0, -1.0, ALU.mult, ALU.add))
                step(L_I, lambda c: v.tensor_tensor(R(c), R(c), I(c), ALU.mult))
                step(L_X, lambda c: v.tensor_tensor(R(c), R(c), X(c), ALU.mult))
                if sample:
                    v.wait_ge(lru, lru_count(b, L_X, LT - 1))
                    a0 = q[:, :, 0:n].rearrange("p c (n k) -> p c n k", k=TS)[:, :, :, 0]
                    x0 = r[:, :, 0:n].rearrange("p c (n k) -> p c n k", k=TS)[:, :, :, 0]
                    v.tensor_tensor(h_s[:], h_s[:], a0, ALU.mult).then_inc(state_step, 1)
                    v.wait_ge(state_step, 2)
                    v.tensor_tensor(x0, x0, h_s[:], ALU.add).then_inc(state_step, 1)
                    v.memset(a0, 0.0).then_inc(state_step, 1)
                    v.wait_ge(state_step, 4)
                if not (is_first or sample):
                    v.wait_ge(carried, b)
                step(L_SCAN, lambda c: v.tensor_tensor_scan(
                    X(c), Q(c), R(c), 0.0 if is_first or sample else carry[:, c:c + 1], ALU.mult, ALU.add))
                if not sample:
                    v.wait_ge(lru, lru_count(b, L_SCAN, LT - 1))
                    v.tensor_copy(carry[:], xc[:, j, :, TB - 1]).then_inc(carried, 1)
                v.wait_ge(silu_sig, LT * (b + 1))
                step(L_G, lambda c: v.tensor_tensor(G(c), G(c), S(c), ALU.mult))
                step(L_Y, lambda c: v.tensor_tensor(G(c), G(c), X(c), ALU.mult))

            def norm(b, nth, j, n):
                v.wait_ge(ss_root, b + 1)
                v.reciprocal(inv[:, 0:n], inv[:, 0:n]).then_inc(inv_done, 1)
                v.wait_ge(inv_done, b + 1)
                if not (isinstance(b, int) and b < 2):
                    v.wait_ge(y_stored[j], 16 * nth)
                for c in range(LT):
                    v.scalar_tensor_tensor(y[:, j, c, 0:n], g[:, j, c, 0:n], vec[:, 4, c:c + 1], inv[:, 0:n],
                                           ALU.mult, ALU.mult).then_inc(y_done, 1)

            spread(0, TB, lambda s: slice(s, s + 1))
            spread(1, TB, lambda s: slice(SUB + s, SUB + s + 1))
            lows(0, 0, TB)

            def main(b, nth, j, n, is_first, second, first, last):
                n1 = SMP if last and j else TB
                if not (is_first or second):
                    norm(b - 2, nth - 1, j, TB)
                convolve(b, nth, j, is_first, None, lambda c: xc[:, j, c])
                if not is_first:
                    v.wait_ge(tok_done, SUB * b)
                lows(b + 1, (j + 1) % 2, n1)
                if not (last and j):
                    spread(b + 2, SMP if last else TB, lambda s: ds((b + 2) * SUB + s, 1))
                if not is_first:
                    recur(b - 1, (j + 1) % 2, TB, second, False)

            def body(i, first, last):
                for j in range(2):
                    main(2 * i + j, i, j, TB, first and j == 0, first and j == 1, first, last)
            peeled(v, NB // 2, body, 2)
            norm(NB - 2, NB // 2 - 1, 0, TB)
            v.tensor_copy(xs[:, :, :, 0:3], conv_s[:]).then_inc(conv, 1)
            v.wait_ge(conv, NCONV * NB + 3)
            v.wait_ge(xa_out, LT * (NB + 1))
            convolve(NB, 0, 0, False, lambda c, k: xs[:, c, :, k:k + TS],
                     lambda c: xc[:, 0, c, 0:SMP].rearrange("p (n k) -> p n k", k=TS))
            recur(NB - 1, 1, TB, False, False)
            norm(NB - 1, NB // 2 - 1, 1, TB)
            recur(NB, 0, SMP, False, True)
            v.tensor_copy(h_s[:], xc[:, 0, :, 0:SMP].rearrange("p c (n k) -> p c n k", k=TS)[:, :, :, TS - 1]).then_inc(state_step, 1)
            norm(NB, NB // 2, 0, SMP)


UNROLL = 4
ROUNDS = SEQ // P // UNROLL
O_ROW = D_ATT + 2 * HEADS


HEAD_ROUNDS = 2


class Tile:

    def __init__(self, level, i, s):
        dil = LEVELS[level][1]
        self.level, self.s, self.dil = level, s, dil
        self.u = ROUNDS * UNROLL * level + UNROLL * i + s
        self.nth = ROUNDS * level + i
        here = isinstance(i, int) and i == 0
        self.half = (here and s == 0, here, s % 2 == 0)[level]
        self.start = (P * UNROLL * i + P * s, P * dil * i + s, 2 * i + s // 2 + P * dil * (s % 2))[level]


def for_tiles(eng, visit):
    before = [None, None]
    for level in range(len(LEVELS)):
        lead = (HEAD_ROUNDS, 2, 1)[level]

        def body(i):
            for s in range(UNROLL):
                if s >= 2:
                    back = Tile(level, i, s - 2)
                elif isinstance(i, int) and i == 0:
                    back = before[s]
                else:
                    back = Tile(level, i - 1, s + 2)
                visit(Tile(level, i, s), back)
        for i in range(lead):
            body(i)
        with eng.Fori(lead, ROUNDS, 1) as i:
            body(i)
        before = [Tile(level, ROUNDS - 1, 2), Tile(level, ROUNDS - 1, 3)]
    for tile in before:
        visit(None, tile)


def attend(nc, t, keep):
    with ExitStack() as ctx:
        f = Frame(nc, ctx)
        qT = f.sb("qT", [P, PAIRS, SEQ])
        kT = f.sb("kT", [P, PAIRS, SEQ])
        bias = f.sb("bias", [P, len(LEVELS), HEADS, 2 * P])
        q = f.sb("q_tiles", [P, UNROLL, PAIRS, P])
        k = f.sb("k_tiles", [P, UNROLL, PAIRS, 2 * P])
        v = f.sb("v_tiles", [P, UNROLL, 2, D_ATT])
        p = f.sb("p", [P, 2, HEADS, 2 * P])
        pT = f.sb("pT", [P, HEADS, 2, P])
        o = f.sb("o", [P, UNROLL, O_ROW])
        s_ps = f.ps("s_ps", [P, 2, 1024])
        t_ps = f.ps("pT_ps", [P, PAIRS, 512])
        o_ps = f.ps("o_ps", [P, 512])
        head_loaded, qk_loaded = f.sem("head_loaded"), f.sem("qk_loaded")
        v_loaded = [f.sem(f"v_loaded{j}") for j in range(UNROLL)]
        o_stored = [f.sem(f"o_stored{j}") for j in range(UNROLL)]
        qk_copied = f.sem("qk_copied")
        s_done, scored, p_done = f.sem("s_done"), f.sem("scored"), f.sem("p_done")
        p_turned, pT_out, pv_done, o_out = f.sem("p_turned"), f.sem("pT_out"), f.sem("pv_done"), f.sem("o_out")
        block = ctx.enter_context(nc.Block())

        def keys(tile):
            n = P if tile.half else 2 * P
            return ds(tile.start - (0 if tile.half else P * tile.dil), n, step=tile.dil), n

        @block.sync
        def _(sp):
            head, rest = slice(0, HEAD_ROUNDS * UNROLL * P), slice(HEAD_ROUNDS * UNROLL * P, SEQ)
            sp.dma_start(qT[:, :, head], t["qkT_all"][:, 0:PAIRS, head]).then_inc(head_loaded, 16)
            sp.dma_start(kT[:, :, head], t["qkT_all"][:, PAIRS:, head]).then_inc(head_loaded, 16)
            sp.dma_start(bias[:, 0], t["bias_p"][:, 0]).then_inc(head_loaded, 16)

            def load_rest():
                sp.dma_start(kT[:, :, rest], t["qkT_all"][:, PAIRS:, rest]).then_inc(qk_loaded, 16)
                sp.dma_start(qT[:, :, rest], t["qkT_all"][:, 0:PAIRS, rest]).then_inc(qk_loaded, 16)
                sp.dma_start(bias[:, 1:], t["bias_p"][:, 1:]).then_inc(qk_loaded, 16)

            def visit(tile, back):
                if tile is not None:
                    if not (isinstance(tile.nth, int) and tile.nth == 0):
                        hold(sp, keep, pv_done, tile.u - UNROLL + 1)
                    own = ds(tile.start, P, step=tile.dil)
                    if tile.half:
                        for c in range(2):
                            cols = slice(c * D_ATT // 2, (c + 1) * D_ATT // 2)
                            sp.dma_start(v[:, tile.s, 1, cols], t["v_all"][own, cols]).then_inc(v_loaded[tile.s], 16)
                    else:
                        prev = ds(tile.start - P * tile.dil, P, step=tile.dil)
                        sp.dma_start(v[:, tile.s, 0], t["v_all"][prev, :]).then_inc(v_loaded[tile.s], 16)
                        sp.dma_start(v[:, tile.s, 1], t["v_all"][own, :]).then_inc(v_loaded[tile.s], 16)
                    if isinstance(tile.u, int) and tile.u == 2:
                        load_rest()
                if back is not None:
                    hold(sp, keep, o_out, back.u + 1)
                    sp.dma_start(t["o_all"][back.level][ds(back.start, P, step=back.dil), :],
                                 o[:, back.s]).then_inc(o_stored[back.s], 16)
            for_tiles(sp, visit)
            for s in range(UNROLL):
                sp.wait_ge(o_stored[s], 16 * ROUNDS * len(LEVELS))

        @block.gpsimd
        def _(pool):
            pool.wait_ge(head_loaded, 48)

            def visit(tile, back):
                if tile is not None:
                    if not (tile.level == 0 and isinstance(tile.nth, int)):
                        pool.wait_ge(qk_loaded, 48)
                    if not (isinstance(tile.nth, int) and tile.nth == 0):
                        pool.wait_ge(s_done, HEADS * (tile.u - UNROLL + 1))
                    nc.gpsimd.tensor_copy(q[:, tile.s], qT[:, :, ds(tile.start, P, step=tile.dil)])
                    at, n = keys(tile)
                    nc.gpsimd.tensor_copy(k[:, tile.s, :, 0:n], kT[:, :, at]).then_inc(qk_copied, 1)
            for_tiles(pool, visit)

        @block.tensor
        def _(pe):
            def visit(tile, back):
                if back is not None:
                    pe.wait_ge(p_done, HEADS * (back.u + 1))
                    if not (isinstance(back.u, int) and back.u == 0):
                        pe.wait_ge(pT_out, PAIRS * back.u)
                    for h in range(HEADS):
                        for half in ((1,) if back.half else (0, 1)):
                            last = pe.transpose(t_ps[:, h // 2, ((h % 2) * 2 + half) * P:((h % 2) * 2 + half + 1) * P],
                                                p[:, back.s % 2, h, half * P:(half + 1) * P], keep["ident"][:])
                        if h % 2:
                            last.then_inc(p_turned, 1)
                if tile is not None:
                    _, n = keys(tile)
                    pe.wait_ge(qk_copied, tile.u + 1)
                    for h in range(HEADS):
                        if h in (0, 1, 4, 5) and not (isinstance(tile.u, int) and tile.u == 0):
                            pe.wait_ge(scored, HEADS * (tile.u - 1) + {0: 3, 1: 4, 4: 5, 5: 6}[h])
                        o64 = slice(DH * (h % 2), DH * (h % 2) + DH)
                        col = (h // 2) * 2 * P + 2 * P - n
                        pe.matmul(s_ps[:, h % 2, col:col + n], q[o64, tile.s, h // 2],
                                  k[o64, tile.s, h // 2, 0:n], start=True, stop=True).then_inc(s_done, 1)
                if back is not None:
                    pe.wait_ge(v_loaded[back.s], 32 * (back.nth + 1))
                    if not (isinstance(back.u, int) and back.u == 0):
                        pe.wait_ge(o_out, back.u)
                    for h in range(HEADS):
                        if h % 2 == 0:
                            pe.wait_ge(pT_out, PAIRS * back.u + h // 2 + 1)
                        for half in ((1,) if back.half else (0, 1)):
                            last = pe.matmul(o_ps[:, h * DH:(h + 1) * DH], pT[:, h, half],
                                             v[:, back.s, half, h * DH:(h + 1) * DH],
                                             start=(half == 1 if back.half else half == 0), stop=(half == 1))
                    last.then_inc(pv_done, 1)
            for_tiles(pe, visit)

        @block.vector
        def _(dve):
            def visit(tile, back):
                if back is not None:
                    if not (isinstance(back.u, int) and back.u == 0):
                        dve.wait_ge(pv_done, back.u)
                    for h in range(PAIRS):
                        dve.wait_ge(p_turned, PAIRS * back.u + h + 1)
                        src = t_ps[:, h].rearrange("p (e x q) -> p e x q", e=2, x=2)
                        dst = pT[:, 2 * h:2 * h + 2]
                        if back.half:
                            src, dst = src[:, :, 1], dst[:, :, 1]
                        dve.tensor_copy(dst, src).then_inc(pT_out, 1)
                if tile is not None:
                    _, n = keys(tile)
                    if not (isinstance(tile.nth, int) and tile.nth == 0):
                        dve.wait_ge(o_stored[tile.s], 16 * tile.nth)
                    for h in range(HEADS):
                        hold(dve, keep, s_done, HEADS * tile.u + {0: 3, 1: 4, 2: 4, 3: 4, 4: 5, 5: 6}[h])
                        col = (h // 2) * 2 * P + 2 * P - n
                        dve.tensor_tensor_reduce(
                            out=p[:, tile.s % 2, h, 2 * P - n:], in0=s_ps[:, h % 2, col:col + n],
                            in1=bias[:, tile.level, h, 2 * P - n:], scale=1.0, scalar=-NEG, op0=ALU.add, op1=ALU.min,
                            accum_out=o[:, tile.s, D_ATT + h:D_ATT + h + 1]).then_inc(scored, 1)
            for_tiles(dve, visit)

        @block.scalar
        def _(act):
            def visit(tile, back):
                if tile is not None:
                    _, n = keys(tile)
                    for h in range(HEADS):
                        act.wait_ge(scored, HEADS * tile.u + h + 1)
                        rows = p[:, tile.s % 2, h, 2 * P - n:]
                        act.activation(rows, rows, ACT.Exp, scale=-1.0, bias=o[:, tile.s, D_ATT + h:D_ATT + h + 1],
                                       accum_out=o[:, tile.s, D_ATT + HEADS + h:D_ATT + HEADS + h + 1]).then_inc(p_done, 1)
                if back is not None:
                    act.wait_ge(pv_done, back.u + 1)
                    act.activation(o[:, back.s, 0:D_ATT], o_ps[:, 0:D_ATT], ACT.Copy).then_inc(o_out, 1)
            for_tiles(act, visit)




PRE = 55


def ssm(nc, t, keep):
    with ExitStack() as ctx:
        f = Frame(nc, ctx)
        bc, mag, pw, tb, ta, x12 = (keep["tables"][n] for n in ("bc", "mag", "pw", "tb", "ta", "x12"))
        turn_i = f.sb("s_turn", [P, P])
        dcol = f.sb("s_d", [P, GROUPS])
        wv = f.sb("s_wv", [P, 2, GROUPS, CH, GC])
        rr = f.sb("s_rr", [P, 2, GROUPS, CH + 1, GC])
        ug = f.sb("s_ug", [P, KTILES * CH + 1, D_SSM])
        ugs = f.sb("s_ugs", [NS, CH, D_SSM])
        gb = f.sb("s_gb", [P, KTILES * CH + 1, D_SSM])
        yb = f.sb("s_yb", [P, KTILES * CH + 1, D_SSM])
        tmp, tmp2 = (yb[:, n * (CH + 1):(n + 1) * (CH + 1)].rearrange("p c (g e) -> p g c e", g=GROUPS) for n in range(2))
        ybs = f.sb("s_ybs", [NS, CH, D_SSM])
        u_g = f.sb("s_u_g", [P, KTILES, CH, GC])
        us_g = f.sb("s_us_g", [NS, CH, GC])
        wv_g = f.sb("s_wv_g", [P, 2, CH * GC])
        xz = f.sb("s_xz", [P, 240])
        rz = f.sb("s_rz", [P, 240])
        rot = f.sb("s_rot", [P, 4, TA, TBL])
        cs = f.sb("s_cs", [P, 2, TA, TBL])
        lhs = f.sb("s_lhs", [P, 2, P])
        uT = f.sb("s_uT", [P, KC + NS])
        dm = f.sb("s_dm", [P, P])
        z1 = f.sb("s_z1", [P, KC])
        z2 = f.sb("s_z2", [P, KC])
        rho = f.sb("s_rho", [P, KC])
        h = f.sb("s_h", [P, 2, KC + 1])
        h_last = f.sb("s_h_last", [P, 2, GROUPS])
        x0 = f.sb("s_x0", [P, GROUPS, NS])
        x0i = f.sb("s_x0i", [P, GROUPS, NS])
        x1 = f.sb("s_x1", [P, GROUPS, NS])
        xe = f.sb("s_xe", [P, GROUPS])

        x0_g = f.sb("s_x0_g", [P, NS])
        last_h, x0_copied = f.sem("s_last_h"), f.sem("s_x0_copied")

        small_ps = f.ps("s_small", [P, 512])
        u_ps = f.ps("s_u_ps", [P, 512])
        us_ps = f.ps("s_us_ps", [P, 512])
        v_ps = f.ps("s_v_ps", [P, 2, 512])
        vs_ps = f.ps("s_vs_ps", [P, 512])
        y_ps = f.ps("s_y_ps", [P, 512])
        ys_ps = f.ps("s_ys_ps", [P, 512])

        loaded, pre, xi_done = f.sem("s_loaded"), f.sem("s_pre"), f.sem("s_xi")
        within_done, staged, gb_loaded, rr_step = f.sem("s_within_done"), f.sem("s_staged"), f.sem("s_gb_loaded"), f.sem("s_rr_step")
        copied, zeroed, w_turned, lhs_out = f.sem("s_copied"), f.sem("s_zeroed"), f.sem("s_w_turned"), f.sem("s_lhs_out")
        u_turned, uT_out, v_done, rot_done = f.sem("s_u_turned"), f.sem("s_uT_out"), f.sem("s_v_done"), f.sem("s_rot_done")
        dm_done, dm_out, z_step, h_done = f.sem("s_dm_done"), f.sem("s_dm_out"), f.sem("s_z_step"), f.sem("s_h_done")
        y_done, y_out, us_done = f.sem("s_y_done"), f.sem("s_y_out"), f.sem("s_us_done")
        pool_s, last_done, state_out = f.sem("s_pool"), f.sem("s_last"), f.sem("s_state_out")

        def over(x, n):
            return x.rearrange("p g (o c) -> p g o c", o=1).broadcast_to([P, GROUPS, n, GC])

        def powers(x, ns):
            w = pw[:, x].rearrange("p n (g o) -> p g n o", o=1)
            w = w[:, :, ns] if ns is not None else w
            return w.broadcast_to([P, GROUPS, w.shape[2], GC])
        inner = ExitStack()
        block = inner.enter_context(nc.Block())
        LOADS = 16 * 9
        NZ = 8

        @block.sync
        def _(sp):
            for dst, name in ((turn_i, "ssm_turn"), (dcol, "ssm_d"), (x0, "ssm_x0")):
                sp.dma_start(dst[:], t[name]).then_inc(loaded, 16)
            rows = t["ug_all"][0:SEQ, 0:D_SSM].rearrange("(a k c) e -> k a c e", k=P, c=CH)
            for a in range(KTILES):
                sp.dma_start(ug[:, a * CH:(a + 1) * CH], rows[:, a]).then_inc(loaded, 16)
            sp.dma_start(ugs[:], t["ug_all"][SEQ:SEQ + SMP, 0:D_SSM].rearrange("(n c) e -> n c e", c=CH)).then_inc(loaded, 16)
            sp.dma_start(rho[:], t["ones"]).then_inc(loaded, 16)
            rows = t["ug_all"][0:SEQ, D_SSM:].rearrange("(a k c) e -> k a c e", k=P, c=CH)
            for a in range(KTILES):
                sp.dma_start(gb[:, a * CH:(a + 1) * CH], rows[:, a]).then_inc(gb_loaded, 16)
            sp.dma_start(gb[0:SMP, KTILES * CH], t["ug_all"][SEQ:SEQ + SMP, D_SSM:]).then_inc(gb_loaded, 16)
            sp.wait_ge(gb_loaded, 16 * (KTILES + 1))
            sp.wait_ge(last_done, 2)
            for half, (a, b) in enumerate((("ssm_re_p", "ssm_re_s"), ("ssm_im_p", "ssm_im_s"))):
                at = slice(STATE * half, STATE * half + STATE)
                sp.dma_start(t[a], xe[at]).then_inc(state_out, 16)
                sp.dma_start(t[b], x1[at]).then_inc(state_out, 16)
            sp.wait_ge(y_out, 2 * GROUPS)
            sp.dma_start(t["ys_mid"].rearrange("(n c) e -> n c e", c=CH), ybs[:]).then_inc(state_out, 16)
            sp.wait_ge(state_out, 80)

        @block.gpsimd
        def _(pool):
            nc.gpsimd.memset(xz[:], 0.0).then_inc(zeroed, 1)
            nc.gpsimd.memset(rz[:], 0.0).then_inc(zeroed, 1)
            nc.gpsimd.memset(h[:, :, 0:1], 0.0).then_inc(zeroed, 1)
            nc.gpsimd.tensor_tensor(rr[:, 1], over(bc[:, 3], CH + 1), powers(0, None), ALU.mult).then_inc(rr_step, 1)
            nc.gpsimd.tensor_tensor(tmp2, over(bc[:, 2], CH + 1), powers(1, None), ALU.mult).then_inc(rr_step, 1)
            pool.wait_ge(rr_step, 2)
            nc.gpsimd.tensor_tensor(rr[:, 1], rr[:, 1], tmp2, ALU.subtract).then_inc(rr_step, 1)
            pool.wait_ge(zeroed, 2)
            pool.wait_ge(loaded, LOADS)
            pool.wait_ge(pre, PRE)

            def body(g, first, last):
                if not first:
                    pool.wait_ge(u_turned, g)
                    pool.wait_ge(dm_done, g)
                nc.gpsimd.tensor_copy(us_g[:], ugs[:, :, ds(g * GC, GC)])
                nc.gpsimd.tensor_copy(xz[:, 112:128], x12[:, 0, g])
                nc.gpsimd.tensor_copy(rz[:, 112:240].rearrange("p (c e) -> p c e", c=CH), rr[:, 0, g, 0:CH]).then_inc(copied, 1)
                shape = [P, TA, TBL]
                A = lambda x: ta[:, x, g].rearrange("p (a o) -> p a o", o=1).broadcast_to(shape)
                B = lambda x: tb[:, x, g].rearrange("p (o b) -> p o b", o=1).broadcast_to(shape)
                if not first:
                    pool.wait_ge(rot_done, 2 * g)
                for k, (x, y) in enumerate(((0, 0), (1, 0), (1, 1), (0, 1))):
                    nc.gpsimd.tensor_tensor(rot[:, k], A(x), B(y), ALU.mult).then_inc(pool_s, 1)
                pool.wait_ge(pool_s, 4 * g + 4)
                if not first:
                    pool.wait_ge(h_done, g)
                nc.gpsimd.tensor_tensor(cs[:, 0], rot[:, 0], rot[:, 2], ALU.subtract).then_inc(rot_done, 1)
                nc.gpsimd.tensor_tensor(cs[:, 1], rot[:, 1], rot[:, 3], ALU.add).then_inc(rot_done, 1)
            peeled(pool, GROUPS, body)

        @block.tensor
        def _(pe):
            pe.wait_ge(loaded, LOADS)
            pe.matmul(vs_ps[:, 0:GROUPS * NS], turn_i[:], x0[:], start=True, stop=True).then_inc(xi_done, 1)

            def turn(g, first):
                pe.wait_ge(copied, g + 1)
                pe.wait_ge(staged, g + 1)
                if not first:
                    pe.wait_ge(us_done, g)
                    pe.wait_ge(uT_out, g)
                for a in range(KTILES):
                    pe.transpose(u_ps[:, a * P:(a + 1) * P], u_g[:, a].rearrange("p c e -> p (c e)"), keep["ident"][:])
                pe.transpose(us_ps[:, 0:NS], us_g.rearrange("n c e -> n (c e)"), keep["ident"][0:NS, 0:NS]).then_inc(u_turned, 1)
                if not first:
                    pe.wait_ge(dm_out, g)
                for x in range(2):
                    w = pe.transpose(small_ps[:, x * P:(x + 1) * P], wv_g[:, x], keep["ident"][:])
                w.then_inc(w_turned, 1)
                pe.wait_ge(lhs_out, g + 1)
                for c in range(CH):
                    at = slice(112 - GC * c, 240 - GC * c)
                    m = pe.matmul(small_ps[:, 2 * P:3 * P], xz[:, at], rz[:, at], start=(c == 0), stop=(c == CH - 1))
                m.then_inc(dm_done, 1)

            def into_state(g, first):
                pe.wait_ge(uT_out, g + 1)
                pe.wait_ge(us_done, g + 1)
                if not first:
                    pe.wait_ge(z_step, NZ * (g - 1) + 2)
                for x in range(2):
                    pe.matmul(v_ps[:, x], lhs[:, x], uT[:, 0:KC], start=True, stop=True).then_inc(v_done, 1)

            def within(g, first):
                if first:
                    pe.wait_ge(last_done, 1)
                else:
                    pe.wait_ge(z_step, NZ * g)
                pe.matmul(vs_ps[:, 0:NS], lhs[:, 0], uT[:, KC:], start=True, stop=True).then_inc(v_done, 1)
                pe.wait_ge(dm_out, g + 1)
                if not first:
                    pe.wait_ge(y_out, 2 * g)
                for a in range(KTILES):
                    at = slice(a * P, (a + 1) * P)
                    pe.matmul(y_ps[:, at], uT[:, at], dm[:], start=(a == 0), stop=False, skip_group_check=True)
                pe.matmul(ys_ps[0:NS, 0:P], uT[:, KC:], dm[:], start=True, stop=False,
                          skip_group_check=True).then_inc(within_done, 1)

            def body(g, first, last):
                if not last:
                    turn(g + 1, False)
                    into_state(g + 1, False)
                pe.wait_ge(x0_copied, g + 1)
                hold(pe, keep, h_done, g + 1)
                for a in range(KTILES):
                    at = slice(a * P, (a + 1) * P)
                    for x in range(2):
                        m = pe.matmul(y_ps[:, at], h[:, x, at], rr[:, x, g, 1:].rearrange("p c e -> p (c e)"),
                                      start=False, stop=(x == 1), skip_group_check=True)
                m.then_inc(y_done, 1)
                pe.matmul(ys_ps[0:NS, 0:P], x0_g[:], rr[:, 0, g, 1:].rearrange("p c e -> p (c e)"),
                          start=False, stop=True, skip_group_check=True).then_inc(y_done, 1)
                if not last:
                    within(g + 1, False)
            pe.wait_ge(rr_step, 3)
            turn(0, True)
            into_state(0, True)
            within(0, True)
            peeled(pe, GROUPS, body)
            pe.wait_ge(last_h, GROUPS)
            pe.matmul(small_ps[:, 0:GROUPS], keep["ident"][:], h_last[:, 0], start=True, stop=False)
            pe.matmul(small_ps[:, 0:GROUPS], turn_i[:], h_last[:, 1], start=False, stop=True).then_inc(v_done, 1)

        @block.scalar
        def _(act):
            act.wait_ge(loaded, LOADS)
            def copy_lhs(g, first):
                act.wait_ge(w_turned, g + 1)
                if not first:
                    act.wait_ge(v_done, 3 * g)
                act.activation(lhs[:], small_ps[:, 0:2 * P].rearrange("p (x s) -> p x s", x=2), ACT.Copy).then_inc(lhs_out, 1)

            def copy_u(g, first):
                act.wait_ge(u_turned, g + 1)
                if not first:
                    act.wait_ge(within_done, g)
                act.activation(uT[:, 0:KC], u_ps[:], ACT.Copy).then_inc(uT_out, 1)
                act.activation(uT[:, KC:], us_ps[:, 0:NS], ACT.Copy).then_inc(us_done, 1)

            def body(g, first, last):
                if not last:
                    copy_lhs(g + 1, False)
                    copy_u(g + 1, False)
                if not (isinstance(g, int) and g + 2 >= GROUPS):
                    stage(g + 2, False)
                act.wait_ge(y_done, 2 * g + 2)
                act.activation(yb[:, 0:KTILES * CH].rearrange("p (a c) e -> p a c e", c=CH)[:, :, :, ds(g * GC, GC)], y_ps.rearrange("p (a c e) -> p a c e", a=KTILES, c=CH),
                               ACT.Copy).then_inc(y_out, 1)
                act.activation(ybs[:, :, ds(g * GC, GC)], ys_ps[0:NS, 0:P].rearrange("p (c e) -> p c e", c=CH),
                               ACT.Copy).then_inc(y_out, 1)
                if not last:
                    act.activation(x0_g[:], x0[:, g + 1], ACT.Copy).then_inc(x0_copied, 1)
            def stage(g, first):
                if not first:
                    act.wait_ge(u_turned, g)
                    act.wait_ge(w_turned, g)
                act.activation(u_g[:], ug[:, 0:KTILES * CH].rearrange("p (a c) e -> p a c e", c=CH)[:, :, :, ds(g * GC, GC)], ACT.Copy)
                act.activation(wv_g.rearrange("p x (c e) -> p x c e", c=CH), wv[:, :, g], ACT.Copy).then_inc(staged, 1)
            act.wait_ge(pre, PRE)
            stage(0, True)
            copy_lhs(0, True)
            copy_u(0, True)
            act.activation(x0_g[:], x0[:, 0], ACT.Copy).then_inc(x0_copied, 1)
            stage(1, False)
            peeled(act, GROUPS, body, tail=2)

        @block.vector
        def _(v):
            count = [0]

            def step(op):
                count[0] += 1
                op.then_inc(pre, 1)
                v.wait_ge(pre, count[0])

            def tt(out, a, b, op=ALU.mult):
                step(v.tensor_tensor(out, a, b, op))

            for c in range(CH):
                n = slice(CH - 1 - c, CH - c)
                pr, pi = powers(0, n), powers(1, n)
                X1, X2 = over(x12[:, 0], 1), over(x12[:, 1], 1)
                w0, w1, one = wv[:, 0, :, c:c + 1], wv[:, 1, :, c:c + 1], tmp[:, :, 0:1]
                tt(w0, X1, pr)
                tt(one, X2, pi)
                tt(w0, w0, one, ALU.add)
                tt(w1, X1, pi)
                tt(one, X2, pr)
                tt(w1, w1, one, ALU.subtract)
            D1, D2 = over(bc[:, 2], CH + 1), over(bc[:, 3], CH + 1)
            pr, pi = powers(0, None), powers(1, None)
            tt(rr[:, 0], D1, pr)
            tt(tmp, D2, pi)
            tt(rr[:, 0], rr[:, 0], tmp, ALU.add)
            v.wait_ge(loaded, LOADS)
            v.wait_ge(xi_done, 1)
            step(v.tensor_copy(x0i[:], vs_ps[:, 0:GROUPS * NS].rearrange("p (g n) -> p g n", g=GROUPS)))
            states = lambda x: x.rearrange("p (g o) -> p g o", o=1).broadcast_to([P, GROUPS, NS])
            tt(x1[:], x0[:], states(pw[:, 0, CH]))
            tt(x0i[:], x0i[:], states(pw[:, 1, CH]))
            tt(x1[:], x1[:], x0i[:], ALU.add)
            v.tensor_copy(xe[:], mag[:, CH]).then_inc(last_done, 1)
            assert count[0] == PRE, count[0]

            def body(g, first, last):
                rate = mag[:, CH, ds(g, 1)]
                cos, sin = cs[:, 0].rearrange("p a b -> p (a b)"), cs[:, 1].rearrange("p a b -> p (a b)")
                v.wait_ge(dm_done, g + 1)
                if not first:
                    v.wait_ge(within_done, g)
                v.scalar_tensor_tensor(dm[:], keep["ident"][:], dcol[:, ds(g, 1)], small_ps[:, 2 * P:3 * P],
                                       ALU.mult, ALU.add).then_inc(dm_out, 1)
                v.wait_ge(rot_done, 2 * g + 2)
                v.wait_ge(v_done, 3 * g + 1)
                v.tensor_tensor(z1[:], v_ps[:, 0], cos, ALU.mult).then_inc(z_step, 1)
                v.wait_ge(v_done, 3 * g + 2)
                v.tensor_tensor(z2[:], v_ps[:, 1], sin, ALU.mult).then_inc(z_step, 1)
                v.wait_ge(z_step, NZ * g + 2)
                v.tensor_tensor(z1[:], z1[:], z2[:], ALU.add).then_inc(z_step, 1)
                v.wait_ge(z_step, NZ * g + 3)
                v.tensor_scalar(z2[:], rho[:], rate, None, ALU.mult).then_inc(z_step, 1)
                v.wait_ge(z_step, NZ * g + 4)
                v.tensor_tensor_scan(z1[:], z2[:], z1[:], 0.0, ALU.mult, ALU.add).then_inc(z_step, 1)
                v.wait_ge(z_step, NZ * g + 5)
                if first:
                    v.wait_ge(zeroed, 3)
                else:
                    v.wait_ge(y_done, 2 * g)
                v.tensor_tensor(h[:, 0, 1:], z1[:], cos, ALU.mult).then_inc(z_step, 1)
                v.tensor_tensor(h[:, 1, 1:], z1[:], sin, ALU.mult).then_inc(h_done, 1)
                v.wait_ge(z_step, NZ * g + 6)
                v.wait_ge(h_done, g + 1)
                v.tensor_copy(h_last[:, :, ds(g, 1)], h[:, :, KC:]).then_inc(last_h, 1)
                v.wait_ge(v_done, 3 * g + 3)
                v.tensor_tensor(x1[:, g], x1[:, g], vs_ps[:, 0:NS], ALU.add).then_inc(z_step, 2)
            peeled(v, GROUPS, body)
            v.wait_ge(last_done, 1)
            v.wait_ge(v_done, 3 * GROUPS + 1)
            v.tensor_copy(xe[:], small_ps[:, 0:GROUPS]).then_inc(last_done, 1)

        inner.close()
        ssm_gate(nc, f, t, keep, yb, gb, rr.rearrange("p x g c e -> p (x g c e)"),
                 wv.rearrange("p x g c e -> p (x g c e)"), v_ps, small_ps, u_ps)


def ssm_gate(nc, f, t, keep, yb, gb, spare, weights, v_ps, small_ps, u_ps):
    nt = SEQ // P
    NP = nt // 2
    wide = weights[:, 0:4 * D_SSM].rearrange("p (x j e) -> p x j e", x=2, j=2)
    w = weights[:, 4 * D_SSM:6 * D_SSM].rearrange("p (a e) -> p a e", a=2)
    share = 2 * 2 * D_SSM
    gl, glT, z, sg = (spare[:, n * share:(n + 1) * share] for n in range(4))
    gl, glT = (x.rearrange("p (j n a e) -> p j n a e", j=2, n=2, a=2) for x in (gl, glT))
    z, sg = (x.rearrange("p (j n e) -> p j n e", j=2, n=2) for x in (z, sg))
    sq = f.sb("g_sq", [P, D_SSM])
    ss = f.sb("g_ss", [P, nt + 1])
    rs = f.sb("g_rs", [P, nt + 1])
    eps = f.sb("g_eps", [P, 1])
    loaded, gelu_done, copied, turned = f.sem("g_loaded"), f.sem("g_gelu"), f.sem("g_copied"), f.sem("g_turned")
    glT_out, z_done, z_biased, z_sig = f.sem("g_glT_out"), f.sem("g_z_done"), f.sem("g_z_biased"), f.sem("g_z_sig")
    gb_sig, step, y_done, squared = f.sem("g_gb_sig"), f.sem("g_step"), f.sem("g_y_done"), f.sem("g_squared")
    set_up, rooted, inv, normed, stored = f.sem("g_set_up"), f.sem("g_rooted"), f.sem("g_inv"), f.sem("g_normed"), f.sem("g_stored")
    turn_ps = [small_ps, u_ps]
    with nc.Block() as block:
        def early(m, until):
            return isinstance(m, int) and m < until

        def size(m):
            if not isinstance(m, int) or m < NP:
                return P, 2
            return SMP, 1

        def exists(m):
            return not isinstance(m, int) or m <= NP

        def at(x, m):
            rows, tiles = size(m)
            return x[0:rows, ds(2 * m, tiles)]

        @block.sync
        def _(sp):
            for twice in range(2):
                sp.dma_start(wide[:, :, twice], t["ssm_wide"].rearrange("(o n) e -> o n e", o=1).broadcast_to([P, 2, D_SSM])).then_inc(loaded, 16)
            sp.dma_start(w, t["glu_w"].rearrange("(a p) e -> p a e", p=P)).then_inc(loaded, 16)
            sp.dma_start(yb[0:SMP, nt], t["ys_mid"]).then_inc(loaded, 16)
            out = t["yb_all"][0:SEQ, :].rearrange("(a k c) e -> k a c e", k=P, c=CH)
            for a in range(KTILES):
                sp.wait_ge(normed, CH * (a + 1))
                sp.dma_start(out[:, a], yb[:, a * CH:(a + 1) * CH]).then_inc(stored, 16)
            sp.wait_ge(normed, nt + 1)
            sp.dma_start(t["yb_all"][SEQ:SEQ + SMP, :], yb[0:SMP, nt]).then_inc(stored, 16)
            sp.wait_ge(stored, 16 * (KTILES + 1))

        def steps(eng, visit):
            def body(i, first, last):
                for j in range(2):
                    visit(2 * i + j, j)
            peeled(eng, NP // 2, body)
            visit(NP, 0)

        @block.gpsimd
        def _(pool):
            nc.gpsimd.memset(eps[:], EPS).then_inc(set_up, 1)
            pool.wait_ge(gelu_done, 1)

            def visit(m, j):
                rows, tiles = size(m)
                if not early(m, 2):
                    pool.wait_ge(turned, m - 1)
                    pool.wait_ge(gelu_done, KTILES + 1)
                nc.gpsimd.tensor_copy(gl[0:rows, j, 0:tiles].rearrange("p n a e -> p n (a e)"), at(yb, m)).then_inc(copied, 1)
            steps(pool, visit)

        @block.tensor
        def _(pe):
            pe.wait_ge(loaded, 16 * 4)

            def turn(m, j):
                rows, tiles = size(m)
                pe.wait_ge(copied, m + 1)
                if not early(m, 2):
                    pe.wait_ge(glT_out, m - 1)
                for n in range(tiles):
                    for a in range(2):
                        c = (2 * n + a) * P
                        last = pe.transpose(turn_ps[j][:, c:c + rows], gl[0:rows, j, n, a], keep["ident"][0:rows, 0:rows])
                last.then_inc(turned, 1)

            def visit(m, j):
                rows, tiles = size(m)
                if exists(m + 1):
                    turn(m + 1, (j + 1) % 2)
                pe.wait_ge(glT_out, m + 1)
                if not early(m, 2):
                    pe.wait_ge(z_biased, m - 1)
                for n in range(tiles):
                    for a in range(2):
                        last = pe.matmul(v_ps[0:rows, j, n * D_SSM:(n + 1) * D_SSM], glT[:, j, n, a, 0:rows], w[:, a],
                                       start=(a == 0), stop=(a == 1), skip_group_check=True)
                last.then_inc(z_done, 1)
            turn(0, 0)
            steps(pe, visit)

        @block.scalar
        def _(act):
            act.wait_ge(loaded, 16 * 4)
            act.wait_ge(set_up, 2)
            for a in range(KTILES):
                part = yb[:, a * CH:(a + 1) * CH]
                act.activation(part, part, ACT.Gelu_apprx_tanh).then_inc(gelu_done, 1)
            act.activation(yb[0:SMP, nt], yb[0:SMP, nt], ACT.Gelu_apprx_tanh).then_inc(gelu_done, 1)

            def copy_out(m, j):
                rows, tiles = size(m)
                act.wait_ge(turned, m + 1)
                if not early(m, 2):
                    act.wait_ge(z_done, m - 1)
                act.activation(glT[:, j, 0:tiles, :, 0:rows],
                               turn_ps[j][:, 0:2 * P * tiles].rearrange("p (n a t) -> p n a t", n=tiles, a=2)[:, :, :, 0:rows],
                               ACT.Copy).then_inc(glT_out, 1)

            def squares(m):
                rows, tiles = size(m)
                act.wait_ge(y_done, m + 1)
                for n in range(tiles):
                    if not (isinstance(m, int) and m == 0 and n == 0):
                        act.wait_ge(squared, 2 * m + n)
                    act.activation(sq[0:rows], yb[0:rows, ds(2 * m + n, 1)].rearrange("p o e -> p (o e)"), ACT.Square,
                                   accum_out=ss[0:rows, ds(2 * m + n, 1)]).then_inc(squared, 1)
            copy_out(0, 0)

            def visit(m, j):
                rows, tiles = size(m)
                if exists(m + 1):
                    copy_out(m + 1, (j + 1) % 2)
                act.wait_ge(z_biased, m + 1)
                act.activation(z[0:rows, j, 0:tiles], z[0:rows, j, 0:tiles], ACT.Sigmoid).then_inc(z_sig, 1)
                if not early(m, 2):
                    act.wait_ge(y_done, m - 1)
                act.activation(sg[0:rows, j, 0:tiles], at(gb, m), ACT.Sigmoid).then_inc(gb_sig, 1)
                if not early(m, 1):
                    squares(m - 1)
            steps(act, visit)
            squares(NP)
            act.wait_ge(squared, nt + 1)
            act.activation(rs[:], ss[:], ACT.Sqrt, scale=1.0 / D_SSM, bias=eps[:]).then_inc(rooted, 1)

        @block.vector
        def _(v):
            v.memset(ss[:], 1.0).then_inc(set_up, 1)
            v.wait_ge(loaded, 16 * 4)
            v.wait_ge(gelu_done, KTILES + 1)

            def finish(m, j):
                rows, tiles = size(m)
                v.wait_ge(z_sig, m + 1)
                v.wait_ge(copied, m + 1)
                v.tensor_tensor(at(yb, m), at(yb, m), z[0:rows, j, 0:tiles], ALU.mult).then_inc(step, 1)
                v.wait_ge(step, 2 * m + 2)
                v.tensor_tensor(at(yb, m), at(yb, m), sg[0:rows, j, 0:tiles], ALU.mult).then_inc(y_done, 1)

            def visit(m, j):
                rows, tiles = size(m)
                v.wait_ge(z_done, m + 1)
                v.tensor_tensor(z[0:rows, j, 0:tiles], v_ps[0:rows, j, 0:tiles * D_SSM].rearrange("p (n e) -> p n e", n=tiles),
                                wide[0:rows, 0, 0:tiles], ALU.add).then_inc(z_biased, 1)
                if not early(m, 1):
                    finish(m - 1, (j + 1) % 2)
                v.wait_ge(gb_sig, m + 1)
                v.tensor_tensor(sg[0:rows, j, 0:tiles], sg[0:rows, j, 0:tiles], at(gb, m), ALU.mult).then_inc(step, 1)
            steps(v, visit)
            finish(NP, 0)
            v.wait_ge(rooted, 1)
            v.reciprocal(rs[:], rs[:]).then_inc(inv, 1)
            v.wait_ge(inv, 1)
            for n in range(nt + 1):
                rows = P if n < nt else SMP
                v.scalar_tensor_tensor(yb[0:rows, n], yb[0:rows, n], rs[0:rows, n:n + 1], wide[0:rows, 1, 0],
                                       ALU.mult, ALU.mult).then_inc(normed, 1)


KTS = 13
SAMPLE_TILES = [(0, slice(0, 8, 1))] + [(1, slice(c, 8, 4)) for c in range(4)] + [(2, slice(c, c + 1, 1)) for c in range(8)]
SEG = P + TS


def sample_attend(nc, t, keep):
    L = len(LEVELS)
    ROWS = 2 * TS
    with ExitStack() as ctx:
        f = Frame(nc, ctx)
        k = f.sb("c_k", [P, 2, KTS, PAIRS, P])
        v = f.sb("c_v", [P, 2, KTS, D_ATT])
        qk = f.sb("c_qk", [P, 2 * PAIRS, SMP])
        vn = f.sb("c_vn", [TS, 2, D_ATT])
        bias = f.sb("c_bias", [ROWS, PAIRS, L * SEG])
        q_mask = f.sb("c_q_mask", [P, KTS, 2, TS])
        w_mask = f.sb("c_w_mask", [P, KTS, TS])
        q_m = f.sb("c_q_m", [P, 2, KTS, PAIRS, ROWS])
        w = f.sb("c_w", [ROWS, PAIRS, L * SEG])
        low = f.sb("c_low", [ROWS, PAIRS])
        den = f.sb("c_den", [ROWS, PAIRS])
        wn = f.sb("c_wn", [ROWS, PAIRS, TS])
        w_m = f.sb("c_w_m", [P, KTS, HEADS, TS])
        wnT = f.sb("c_wnT", [TS, HEADS * TS])
        o = f.sb("c_o", [TS, 2, D_ATT])
        s_ps = f.ps("c_s_ps", [P, 2, PAIRS, 512])
        t_ps = f.ps("c_t_ps", [P, 512])
        o_ps = f.ps("c_o_ps", [P, 512])
        loaded, q_masked = f.sem("c_loaded"), f.sem("c_q_masked")
        k_loaded = [f.sem(f"c_k_loaded{j}") for j in range(2)]
        v_loaded = [f.sem(f"c_v_loaded{j}") for j in range(2)]
        stored = [f.sem(f"c_stored{j}") for j in range(2)]
        s_done, biased, low_done, exp_done = f.sem("c_s_done"), f.sem("c_biased"), f.sem("c_low_done"), f.sem("c_exp_done")
        den_inv, scaled, new_step, turned = f.sem("c_den_inv"), f.sem("c_scaled"), f.sem("c_new_step"), f.sem("c_turned")
        w_masked, wnT_out, o_done, o_out = f.sem("c_w_masked"), f.sem("c_wnT_out"), f.sem("c_o_done"), f.sem("c_o_out")
        block = ctx.enter_context(nc.Block())

        def sequences(eng, visit):
            def body(i, first, last):
                for j in range(2):
                    visit(2 * i + j, j, i)
            peeled(eng, NS // 2, body)

        def early(n, until):
            return isinstance(n, int) and n < until

        @block.sync
        def _(sp):
            sp.dma_start(qk[:], t["qkT_all"][:, :, SEQ:]).then_inc(loaded, 16)
            sp.dma_start(q_mask[:], t["q_mask"]).then_inc(loaded, 16)
            sp.dma_start(w_mask[:], t["w_mask"]).then_inc(loaded, 16)
            sp.dma_start(bias[:], t["bias_s"]).then_inc(loaded, 16)

            def load_k(n, j, i):
                if not early(n, 2):
                    hold(sp, keep, s_done, n - 1)
                sp.dma_start(k[:, j], t["cache_kT"][ds(n, 1)].rearrange("o p a -> (o p) a")).then_inc(k_loaded[j], 16)

            def load_v(n, j, i):
                if not early(n, 2):
                    hold(sp, keep, o_done, n - 1)
                sp.dma_start(v[:, j], t["cache_v"][ds(n, 1)].rearrange("o p a -> (o p) a")).then_inc(v_loaded[j], 16)
                sp.dma_start(vn[:, j], t["v_all"][ds(SEQ + n * TS, TS), :]).then_inc(v_loaded[j], 16)

            def visit(n, j, i):
                if not (isinstance(n, int) and n + 2 >= NS):
                    load_k(n + 2, j, i + 1)
                if not (isinstance(n, int) and n + 1 >= NS):
                    load_v(n + 1, (j + 1) % 2, i + j)
                hold(sp, keep, o_out, n + 1)
                sp.dma_start(t["os_all"][ds(n * TS, TS), :], o[:, j]).then_inc(stored[j], 16)
            load_k(0, 0, 0)
            load_k(1, 1, 0)
            load_v(0, 0, 0)
            sequences(sp, visit)
            for j in range(2):
                sp.wait_ge(stored[j], 16 * (NS // 2))

        @block.gpsimd
        def _(pool):
            pool.wait_ge(loaded, 64)

            def mask_q(n, j, i):
                if not early(n, 2):
                    pool.wait_ge(s_done, n - 1)
                for x in range(PAIRS):
                    q = qk[:, x, ds(n * TS, TS)].rearrange("p (a e t) -> p a e t", a=1, e=1).broadcast_to([P, KTS, 2, TS])
                    m = nc.gpsimd.tensor_tensor(q_m[:, j, :, x].rearrange("p a (e t) -> p a e t", e=2), q, q_mask[:], ALU.mult)
                m.then_inc(q_masked, 1)
            sequences(pool, mask_q)

        @block.tensor
        def _(pe):
            pe.wait_ge(loaded, 64)

            def scores(n, j, i):
                pe.wait_ge(q_masked, n + 1)
                pe.wait_ge(k_loaded[j], 16 * (i + 1))
                if not early(n, 2):
                    pe.wait_ge(biased, n - 1)
                for x in range(PAIRS):
                    out = s_ps[0:ROWS, j, x]
                    for a, (level, _) in enumerate(SAMPLE_TILES):
                        new = a == 0 or SAMPLE_TILES[a - 1][0] != level
                        end = a == KTS - 1 or SAMPLE_TILES[a + 1][0] != level
                        pe.matmul(out[:, level * SEG:level * SEG + P], q_m[:, j, a, x], k[:, j, a, x], start=new, stop=end,
                                  skip_group_check=True)
                    for level in range(L):
                        m = pe.matmul(out[:, level * SEG + P:(level + 1) * SEG], q_m[:, j, 0, x],
                                      qk[:, PAIRS + x, ds(n * TS, TS)], start=True, stop=True, skip_group_check=True)
                m.then_inc(s_done, 1)

            def weighted(n, j, i):
                if not early(n, 1):
                    pe.wait_ge(w_masked, n)
                    pe.wait_ge(wnT_out, n)
                pe.wait_ge(scaled, n + 1)
                hold(pe, keep, new_step, 2 * n + 2)
                for l in range(L):
                    for x in range(PAIRS):
                        at = (l * PAIRS + x) * ROWS
                        pe.transpose(t_ps[:, at:at + ROWS], w[:, x, l * SEG:l * SEG + P], keep["ident"][0:ROWS, 0:ROWS])
                for x in range(PAIRS):
                    at = (L * PAIRS + x) * ROWS
                    m = pe.transpose(t_ps[0:TS, at:at + ROWS], wn[:, x], keep["ident"][0:ROWS, 0:ROWS])
                m.then_inc(turned, 1)
                pe.wait_ge(w_masked, n + 1)
                pe.wait_ge(wnT_out, n + 1)
                pe.wait_ge(v_loaded[j], 32 * (i + 1))
                if not early(n, 1):
                    pe.wait_ge(o_out, n)
                for h in range(HEADS):
                    out = o_ps[0:TS, h * DH:(h + 1) * DH]
                    for a in range(KTS):
                        pe.matmul(out, w_m[:, a, h], v[:, j, a, h * DH:(h + 1) * DH], start=(a == 0), stop=False,
                                  skip_group_check=True)
                    m = pe.matmul(out, wnT[:, h * TS:(h + 1) * TS], vn[:, j, h * DH:(h + 1) * DH],
                                  start=False, stop=True, skip_group_check=True)
                m.then_inc(o_done, 1)

            def visit(n, j, i):
                if not (isinstance(n, int) and n + 1 >= NS):
                    scores(n + 1, (j + 1) % 2, i + j)
                weighted(n, j, i)
            scores(0, 0, 0)
            sequences(pe, visit)

        @block.scalar
        def _(act):
            act.wait_ge(loaded, 64)

            def weights(n):
                act.wait_ge(low_done, n + 1)
                for x in range(PAIRS):
                    act.activation(w[:, x], w[:, x], ACT.Exp, scale=-1.0, bias=low[:, x:x + 1],
                                   accum_out=den[:, x:x + 1]).then_inc(exp_done, 1)

            def visit(n, j, i):
                if not (isinstance(n, int) and n + 1 >= NS):
                    weights(n + 1)
                act.wait_ge(o_done, n + 1)
                if not early(n, 2):
                    act.wait_ge(stored[j], 16 * i)
                act.activation(o[:, j], o_ps[0:TS, 0:D_ATT], ACT.Copy).then_inc(o_out, 1)
            weights(0)
            sequences(act, visit)

        @block.vector
        def _(dve):
            dve.wait_ge(loaded, 64)

            def visit(n, j, i):
                dve.wait_ge(s_done, n + 1)
                if not early(n, 1):
                    dve.wait_ge(turned, n)
                dve.tensor_tensor(w[:], s_ps[0:ROWS, j, :, 0:L * SEG], bias[:], ALU.add).then_inc(biased, 1)
                dve.wait_ge(biased, n + 1)
                dve.tensor_reduce(low[:], w[:], AX.X, ALU.min).then_inc(low_done, 1)
                dve.wait_ge(exp_done, PAIRS * (n + 1))
                dve.reciprocal(den[:], den[:]).then_inc(den_inv, 1)
                dve.wait_ge(den_inv, n + 1)
                for x in range(PAIRS):
                    m = dve.tensor_scalar(w[:, x], w[:, x], den[:, x:x + 1], None, ALU.mult)
                m.then_inc(scaled, 1)
                dve.wait_ge(scaled, n + 1)
                new = w.rearrange("r x (l k) -> r x l k", l=L)[:, :, :, P:]
                dve.tensor_tensor(wn[:], new[:, :, 0], new[:, :, 1], ALU.add).then_inc(new_step, 1)
                dve.wait_ge(new_step, 2 * n + 1)
                dve.tensor_tensor(wn[:], wn[:], new[:, :, 2], ALU.add).then_inc(new_step, 1)
                dve.wait_ge(turned, n + 1)
                if not early(n, 1):
                    dve.wait_ge(o_done, n)
                dve.tensor_copy(wnT[:], t_ps[0:TS, L * PAIRS * ROWS:(L + 1) * PAIRS * ROWS]).then_inc(wnT_out, 1)
                for l in range(L):
                    tiles = [a for a, (level, _) in enumerate(SAMPLE_TILES) if level == l]
                    at, shape = slice(tiles[0], tiles[-1] + 1), [P, len(tiles), HEADS, TS]
                    src = t_ps[:, l * PAIRS * ROWS:(l + 1) * PAIRS * ROWS].rearrange("p (o h t) -> p o h t", o=1, h=HEADS)
                    mask = w_mask[:, at].rearrange("p a (o t) -> p a o t", o=1)
                    m = dve.tensor_tensor(w_m[:, at], src.broadcast_to(shape), mask.broadcast_to(shape), ALU.mult)
                m.then_inc(w_masked, 1)
            sequences(dve, visit)


def project_out(nc, t, keep):
    nt = SEQ // P
    L = len(LEVELS)
    TC = (D_SSM + D_ATT) // P
    with ExitStack() as ctx:
        f = Frame(nc, ctx)
        w_raw = f.sb("wo_raw", [P, STAGES, D])
        w_hi = f.sb("wo_hi", [P, KT, D], F32R)
        w_lo = f.sb("wo_lo", [P, KT, D], F32R)
        o = f.sb("o_in", [P, 2, L, O_ROW])
        gc = f.sb("gc_in", [P, 2, D_ATT])
        ya = f.sb("ya_in", [P, 2, LT, P])
        yb = f.sb("yb_in", [P, 2, D_SSM])
        yc = f.sb("yc", [P, 2, D_ATT])
        x = f.sb("x_in", [P, 2, D])
        y_out = f.sb("y_out", [P, 2, D])
        y_hi = f.sb("y_hi", [P, 2, KT, P], F32R)
        y_lo = f.sb("y_lo", [P, 2, KT, P], F32R)
        low = f.sb("low", [P, HEADS])
        wt = f.sb("weights", [P, L, HEADS])
        wd = f.sb("weighted_den", [P, L, HEADS])
        gate = f.sb("gc_gate", [P, D_ATT])
        sq = f.sb("yc_sq", [P, D_ATT])
        ms = f.sb("yc_ms", [P, 2])
        gain = f.sb("yc_gain", [P, D_ATT])
        eps = f.sb("eps_o", [P, 1])
        out_ps = f.ps("out_ps", [P, 2, 2, 512])
        t_ps = f.ps("yT_ps", [P, 2, 1024])
        w_loaded = [f.sem(f"wo_loaded{j}") for j in range(STAGES)]
        o_loaded = [f.sem(f"o_in_loaded{j}") for j in range(2)]
        ab_loaded = [f.sem(f"ab_in_loaded{j}") for j in range(2)]
        x_loaded = [f.sem(f"x_in_loaded{j}") for j in range(2)]
        y_stored = [f.sem(f"y_stored{j}") for j in range(2)]
        set_up, rooted = f.sem("o_set_up"), f.sem("yc_rooted")
        w_hi_done, w_split, gain_loaded = f.sem("wo_hi_done"), f.sem("wo_split"), f.sem("yc_gain_loaded")
        low_done, exp_done, step = f.sem("low_done"), f.sem("exp_done"), f.sem("yc_step")
        gate_exp, gate_den, gate_inv, gate_done = f.sem("gate_exp"), f.sem("gate_den"), f.sem("gate_inv"), f.sem("gate_done")
        gated, squared, inv, normed = f.sem("yc_gated"), f.sem("yc_squared"), f.sem("yc_inv"), f.sem("yc_normed")
        turned, hi_done, split, projected, added = f.sem("y_turned"), f.sem("y_hi_done"), f.sem("y_split"), f.sem("projected"), f.sem("added")
        block = ctx.enter_context(nc.Block())
        NSTEP = 10

        def height(n):
            if not isinstance(n, int) or n < nt:
                return P
            return SMP if n == nt else 0

        def tokens(n):
            return slice(SEQ, SEQ + SMP) if height(n) == SMP else ds(n * P, P)

        def steps(eng, visit, tail=1):
            def body(i, first, last):
                for j in range(2):
                    visit(2 * i + j, j, i)
            peeled(eng, nt // 2, body, tail=tail)
            visit(nt, 0, nt // 2)

        def early(n, until):
            return isinstance(n, int) and n < until

        @block.sync
        def _(sp):
            def load_o(n, j):
                if not height(n):
                    return
                if not early(n, 2):
                    hold(sp, keep, normed, n - 1)
                if height(n) == SMP:
                    sp.wait_ge(split, nt - 1)
                    sp.dma_start(yc[0:SMP, j], t["os_all"]).then_inc(o_loaded[j], 16)
                else:
                    sp.dma_start(o[:, j], t["o_all"][:, tokens(n), :].rearrange("l p e -> p l e")).then_inc(o_loaded[j], 16)
                sp.dma_start(gc[0:height(n), j], t["gc_all"][tokens(n), :]).then_inc(o_loaded[j], 16)

            def load_ab(n, j):
                if not height(n):
                    return
                if not early(n, 2):
                    hold(sp, keep, split, n - 1)
                sp.dma_start(ya[:, j, :, 0:height(n)], t["yaT_all"][:, :, tokens(n)]).then_inc(ab_loaded[j], 16)
                sp.dma_start(yb[0:height(n), j], t["yb_all"][tokens(n), :]).then_inc(ab_loaded[j], 16)

            def load_x(n, j):
                if not height(n):
                    return
                if not early(n, 2):
                    hold(sp, keep, added, n - 1)
                sp.dma_start(x[0:height(n), j], t["x_s"] if height(n) == SMP else t["x_p"][ds(n * P, P), :]).then_inc(x_loaded[j], 16)

            sp.dma_start(gain[:], t["yc_gain"].rearrange("(o d) -> o d", o=1).broadcast_to([P, D_ATT])).then_inc(gain_loaded, 16)
            for k in range(KT):
                if k == 1:
                    load_o(0, 0)
                if k == STAGES:
                    load_o(1, 1)
                    load_ab(0, 0)
                if k >= STAGES:
                    sp.wait_ge(w_split, k - STAGES + 1)
                sp.dma_start(w_raw[:, k % STAGES], t["w_out"][:, k]).then_inc(w_loaded[k % STAGES], 16)
            load_ab(1, 1)
            load_o(2, 0)
            load_x(0, 0)

            def visit(n, j, nth):
                load_o(n + 3, (j + 1) % 2)
                load_ab(n + 2, j)
                load_x(n + 1, (j + 1) % 2)
                hold(sp, keep, added, n + 1)
                sp.dma_start(t["y_s"] if height(n) == SMP else t["y_p"][ds(n * P, P), :],
                             y_out[0:height(n), j]).then_inc(y_stored[j], 16)
            steps(sp, visit, tail=2)
            sp.wait_ge(y_stored[0], 16 * (nt // 2 + 1))
            sp.wait_ge(y_stored[1], 16 * (nt // 2))

        @block.gpsimd
        def _(pool):
            def make_gate(n, j):
                rows = height(n)
                pool.wait_ge(gate_inv, n + 1)
                nc.gpsimd.tensor_tensor(gate[0:rows], gate[0:rows], gc[0:rows, j], ALU.mult).then_inc(gate_done, 1)
            nc.gpsimd.memset(eps[:], EPS).then_inc(set_up, 1)
            make_gate(0, 0)
            make_gate(1, 1)

            def visit(n, j, nth):
                if height(n + 2):
                    make_gate(n + 2, j)
            steps(pool, visit)

        @block.tensor
        def _(pe):
            def turn(n, j, nth):
                rows = height(n)
                pe.wait_ge(ab_loaded[j], 32 * (nth + 1))
                pe.wait_ge(normed, n + 1)
                if not early(n, 2):
                    pe.wait_ge(split, n - 1)
                for c in range(TC):
                    src = yb[0:rows, j, c * P:(c + 1) * P] if c < 2 else yc[0:rows, j, (c - 2) * P:(c - 1) * P]
                    m = pe.transpose(t_ps[:, j, c * P:c * P + rows], src, keep["ident"][0:rows, 0:rows])
                m.then_inc(turned, 1)

            def project(n, j, half):
                rows = height(n)
                for k in range(KT):
                    out, cols = out_ps[0:rows, j, half], slice(half * 512, half * 512 + 512)
                    yh = y_hi[:, j, k, 0:rows]
                    pe.matmul(out, yh, w_hi[:, k, cols], start=(k == 0), stop=False)
                    pe.matmul(out, yh, w_lo[:, k, cols], start=False, stop=False)
                    m = pe.matmul(out, y_lo[:, j, k, 0:rows], w_hi[:, k, cols], start=False, stop=(k == KT - 1))
                m.then_inc(projected, 1)
            turn(0, 0, 0)
            pe.wait_ge(w_split, KT)

            def visit(n, j, nth):
                pe.wait_ge(split, n + 1)
                if not early(n, 2):
                    pe.wait_ge(added, n - 1)
                project(n, j, 0)
                if height(n + 1):
                    turn(n + 1, (j + 1) % 2, nth + j)
                project(n, j, 1)
            steps(pe, visit)

        @block.scalar
        def _(act):
            def start_gate(n, j, nth):
                act.wait_ge(o_loaded[j], 32 * (nth + 1))
                if not early(n, 1):
                    act.wait_ge(gated, n)
                act.activation(gate[0:height(n)], gc[0:height(n), j], ACT.Exp, scale=-1.0).then_inc(gate_exp, 1)
                act.wait_ge(gate_exp, n + 1)
                act.activation(gate[0:height(n)], gate[0:height(n)], ACT.Copy, bias=1.0).then_inc(gate_den, 1)
                if height(n) == P:
                    act.wait_ge(low_done, n + 1)
                    act.activation(wt[:], wt[:], ACT.Exp).then_inc(exp_done, 1)

            def mean_square(n, j):
                rows = height(n)
                act.wait_ge(gated, n + 1)
                if not early(n, 1):
                    act.wait_ge(squared, n)
                act.activation(sq[0:rows], yc[0:rows, j], ACT.Square, scale=D_ATT ** -0.5,
                               accum_out=ms[0:rows, j:j + 1]).then_inc(squared, 1)
                act.wait_ge(squared, n + 1)
                act.activation(ms[0:rows, j:j + 1], ms[0:rows, j:j + 1], ACT.Sqrt, bias=eps[0:rows]).then_inc(rooted, 1)

            def highs(n, j, nth):
                rows = height(n)
                act.wait_ge(ab_loaded[j], 32 * (nth + 1))
                if not early(n, 2):
                    act.wait_ge(projected, 2 * n - 2)
                act.activation(y_hi[:, j, 0:LT, 0:rows], ya[:, j, :, 0:rows], ACT.Copy).then_inc(hi_done, 1)
                act.wait_ge(turned, n + 1)
                act.activation(y_hi[:, j, LT:, 0:rows], t_ps[:, j, 0:TC * P].rearrange("p (c t) -> p c t", c=TC)[:, :, 0:rows],
                               ACT.Copy).then_inc(hi_done, 1)
            def weight_highs(k):
                act.wait_ge(w_loaded[k % STAGES], 16 * (k // STAGES + 1))
                act.activation(w_hi[:, k], w_raw[:, k % STAGES], ACT.Copy).then_inc(w_hi_done, 1)
            act.wait_ge(set_up, 1)
            for k in range(2):
                weight_highs(k)
            start_gate(0, 0, 0)
            for k in range(2, 5):
                weight_highs(k)
            mean_square(0, 0)
            for k in range(5, KT):
                weight_highs(k)
            highs(0, 0, 0)
            start_gate(1, 1, 0)
            mean_square(1, 1)

            def visit(n, j, nth):
                if height(n + 2):
                    start_gate(n + 2, j, nth + 1)
                if height(n + 1):
                    highs(n + 1, (j + 1) % 2, nth + j)
                if height(n + 2):
                    mean_square(n + 2, j)
            steps(act, visit)

        @block.vector
        def _(v):
            v.wait_ge(gain_loaded, 16)

            def join(n, j, nth):
                rows = height(n)
                v.wait_ge(o_loaded[j], 32 * (nth + 1))
                Y = yc[0:rows, j]
                base = NSTEP * n
                if rows == P:
                    mins, dens = o[:, j, :, D_ATT:D_ATT + HEADS], o[:, j, :, D_ATT + HEADS:]
                    v.tensor_tensor(low[:], mins[:, 0], mins[:, 1], ALU.min).then_inc(step, 1)
                    v.wait_ge(step, base + 1)
                    v.tensor_tensor(low[:], low[:], mins[:, 2], ALU.min).then_inc(step, 1)
                    v.wait_ge(step, base + 2)
                    v.tensor_tensor(wt[:], low.rearrange("p (o h) -> p o h", o=1).broadcast_to([P, L, HEADS]), mins,
                                    ALU.subtract).then_inc(low_done, 1)
                v.wait_ge(gate_den, n + 1)
                v.reciprocal(gate[0:rows], gate[0:rows]).then_inc(gate_inv, 1)
                if rows == P:
                    v.wait_ge(exp_done, n + 1)
                    v.tensor_tensor(wd[:], wt[:], dens, ALU.mult).then_inc(step, 1)
                    v.wait_ge(step, base + 3)
                    v.tensor_tensor(low[:], wd[:, 0], wd[:, 1], ALU.add).then_inc(step, 1)
                    v.wait_ge(step, base + 4)
                    v.tensor_tensor(low[:], low[:], wd[:, 2], ALU.add).then_inc(step, 1)
                    v.wait_ge(step, base + 5)
                    v.reciprocal(low[:], low[:]).then_inc(step, 1)
                    v.wait_ge(step, base + 6)
                    v.tensor_tensor(wt[:], wt[:], low.rearrange("p (o h) -> p o h", o=1).broadcast_to([P, L, HEADS]),
                                    ALU.mult).then_inc(step, 1)
                    v.wait_ge(step, base + 7)
                    rows_o = o[:, j, :, 0:D_ATT].rearrange("p l (h d) -> p l h d", d=DH)
                    for l in range(L):
                        m = v.tensor_tensor(rows_o[:, l], rows_o[:, l],
                                            wt[:, l].rearrange("p (h o) -> p h o", o=1).broadcast_to([P, HEADS, DH]), ALU.mult)
                    m.then_inc(step, 1)
                    v.wait_ge(step, base + 8)
                    v.tensor_tensor(Y, o[:, j, 0, 0:D_ATT], o[:, j, 1, 0:D_ATT], ALU.add).then_inc(step, 1)
                    v.wait_ge(step, base + 9)
                    v.tensor_tensor(Y, Y, o[:, j, 2, 0:D_ATT], ALU.add).then_inc(step, 1)
                    v.wait_ge(step, base + 10)
                v.wait_ge(gate_done, n + 1)
                v.tensor_tensor(Y, Y, gate[0:rows], ALU.mult).then_inc(gated, 1)

            def norm(n, j):
                rows = height(n)
                v.wait_ge(rooted, n + 1)
                v.reciprocal(ms[0:rows, j:j + 1], ms[0:rows, j:j + 1]).then_inc(inv, 1)
                v.wait_ge(inv, n + 1)
                v.scalar_tensor_tensor(yc[0:rows, j], yc[0:rows, j], ms[0:rows, j:j + 1], gain[0:rows],
                                       ALU.mult, ALU.mult).then_inc(normed, 1)

            def lows(n, j):
                rows = height(n)
                v.wait_ge(hi_done, 2 * n + 1)
                v.tensor_tensor(y_lo[:, j, 0:LT, 0:rows], ya[:, j, :, 0:rows], y_hi[:, j, 0:LT, 0:rows].bitcast(F32), ALU.subtract)
                v.wait_ge(hi_done, 2 * n + 2)
                v.tensor_tensor(y_lo[:, j, LT:, 0:rows], t_ps[:, j, 0:TC * P].rearrange("p (c t) -> p c t", c=TC)[:, :, 0:rows],
                                y_hi[:, j, LT:, 0:rows].bitcast(F32), ALU.subtract).then_inc(split, 1)

            def add(n, j, half):
                cols = slice(half * 512, half * 512 + 512)
                v.wait_ge(projected, 2 * n + half + 1)
                return v.tensor_tensor(y_out[0:height(n), j, cols], out_ps[0:height(n), j, half], x[0:height(n), j, cols], ALU.add)
            def weight_lows(k):
                v.wait_ge(w_hi_done, k + 1)
                v.tensor_tensor(w_lo[:, k], w_raw[:, k % STAGES], w_hi[:, k].bitcast(F32), ALU.subtract).then_inc(w_split, 1)
            for k in range(2):
                weight_lows(k)
            join(0, 0, 0)
            for k in range(2, 5):
                weight_lows(k)
            norm(0, 0)
            for k in range(5, KT):
                weight_lows(k)
            lows(0, 0)
            join(1, 1, 0)
            norm(1, 1)

            def visit(n, j, nth):
                if height(n + 2):
                    join(n + 2, j, nth + 1)
                if height(n + 1):
                    lows(n + 1, (j + 1) % 2)
                v.wait_ge(x_loaded[j], 16 * (nth + 1))
                if not early(n, 2):
                    v.wait_ge(y_stored[j], 16 * nth)
                add(n, j, 0)
                if height(n + 2):
                    norm(n + 2, j)
                add(n, j, 1).then_inc(added, 1)
            steps(v, visit)


def constants(nc, top, t):
    keep = {
        "ident": top.sb("ident", [P, P]),
        "qk_gain": top.sb("qk_gain", [P, 2 * D_ATT]),
        "rs": top.sb("rs_keep", [P, SEQ // P + 1]),
        "tables": table_buffers(top),
    }
    loaded = top.sem("constants_loaded")
    gained = top.sem("q_gain_scaled")
    with nc.Block() as block:
        @block.sync
        def _(sp):
            sp.dma_start(keep["ident"][:], t["identity"]).then_inc(loaded, 16)
            for name, half in (("q_norm_g", 0), ("k_norm_g", 1)):
                for h in range(HEADS):
                    at = half * D_ATT + h * DH
                    sp.dma_start(keep["qk_gain"][:, at:at + DH],
                                 t[name].rearrange("(o d) -> o d", o=1).broadcast_to([P, DH])).then_inc(loaded, 16)
            sp.wait_ge(loaded, 16 * (1 + 2 * HEADS))

        @block.vector
        def _(v):
            v.wait_ge(loaded, 16 * (1 + 2 * HEADS))
            v.tensor_scalar(keep["qk_gain"][:, 0:D_ATT], keep["qk_gain"][:, 0:D_ATT], -(DH ** -0.5), None, ALU.mult).then_inc(gained, 1)
    keep["loaded"] = loaded
    return keep


def program(nc, t):
    with ExitStack() as ctx:
        top = Frame(nc, ctx)
        keep = constants(nc, top, t)
        project_attention(nc, t, keep)
        project_recurrent(nc, t, keep)
        attend(nc, t, keep)
        ssm(nc, t, keep)
        sample_attend(nc, t, keep)
        project_out(nc, t, keep)


OUTS = {
    "y_p": (SEQ, D), "y_s": (SMP, D), "conv_p": (P, LT, 3), "lru_p": (P, LT),
    "ssm_re_p": (STATE, GROUPS), "ssm_im_p": (STATE, GROUPS), "k_p": (KEEP, D_ATT), "v_p": (KEEP, D_ATT),
    "conv_s": (P, LT, NS, 3), "lru_s": (P, LT, NS), "ssm_re_s": (STATE, GROUPS, NS), "ssm_im_s": (STATE, GROUPS, NS),
    "k_s": (SMP, D_ATT), "v_s": (SMP, D_ATT),
}
SCRATCH = {
    "v_all": (SEQ + SMP, D_ATT), "gc_all": (SEQ + SMP, D_ATT), "k_all": (SEQ + SMP, D_ATT),
    "ys_mid": (SMP, D_SSM), "yb_all": (SEQ + SMP, D_SSM), "os_all": (SMP, D_ATT),
    "o_all": (len(LEVELS), SEQ, O_ROW),
    "qkT_all": (P, 2 * PAIRS, SEQ + SMP), "ug_all": (SEQ + SMP, 2 * D_SSM), "yaT_all": (P, LT, SEQ + SMP),
}


def slopes():
    return np.exp2(-8.0 * np.arange(1, HEADS + 1) / HEADS).astype(np.float32)


def prompt_bias():
    delta = np.arange(P)[:, None] - np.arange(2 * P)[None] + P
    out = np.zeros((P, len(LEVELS), HEADS, 2 * P), np.float32)
    for n, (_, dil) in enumerate(LEVELS):
        for h, slope in enumerate(slopes()):
            out[:, n, h] = np.where((delta >= 0) & (delta <= P), slope * (delta * dil).astype(np.float32), -NEG)
    return out


def tiles_of(cache):
    n = PAST
    parts = [cache[:, n - P:]]
    parts += [cache[:, n - 4 * P + c::4] for c in range(4)]
    parts += [cache[:, n - 16 * P + c::16] for c in range(16 // 2)]
    return np.stack(parts, 1)


def sample_bias():
    out = np.full((2, TS, PAIRS, len(LEVELS), SEG), -NEG, np.float32)
    m = np.arange(P)
    for h, slope in enumerate(slopes()):
        for l, (_, dil) in enumerate(LEVELS):
            for step in range(TS):
                delta = P + step // dil - m
                row = out[h % 2, step, h // 2, l]
                row[:P] = np.where(delta <= P, slope * (delta * dil).astype(np.float32), -NEG)
                for back in range(0, step + 1, dil):
                    row[P + step - back] = slope * np.float32(back)
    return out.reshape(2 * TS, PAIRS, -1)


def sample_masks():
    serves = np.zeros((KTS, TS), np.float32)
    for a, (_, steps) in enumerate(SAMPLE_TILES):
        serves[a, steps] = 1.0
    heads = np.repeat(np.eye(2, dtype=np.float32), DH, 0)
    q_mask = heads[:, None, :, None] * serves[None, :, None, :]
    return np.ascontiguousarray(q_mask), np.ascontiguousarray(np.broadcast_to(serves, (P, KTS, TS)))


def lay_out(i):
    w = i["w_in"][0].reshape(KT, P, -1).transpose(1, 0, 2)
    twice = lambda x: np.concatenate([x, x])
    eye = np.eye(STATE, dtype=np.float32)
    br, bi = (i[n][0].transpose(1, 0, 2) for n in ("ssm_b_re", "ssm_b_im"))
    cr, ci = (i[n][0].transpose(2, 0, 1) for n in ("ssm_c_re", "ssm_c_im"))
    return {
        "xT_p": i["x_prompt"][0].T.reshape(KT, P, SEQ).transpose(1, 0, 2),
        "xT_s": i["x_sample"].reshape(SMP, D).T.reshape(KT, P, SMP).transpose(1, 0, 2),
        "x_p": i["x_prompt"][0],
        "x_s": i["x_sample"].reshape(SMP, D),
        "norm_g": i["norm_g"][0].reshape(KT, P).T,
        "w_att": w[:, :, D_R:],
        "w_rec": w[:, :, :D_R],
        "q_norm_g": i["q_norm_g"][0],
        "k_norm_g": i["k_norm_g"][0],
        "conv_w": i["conv_w"][0].reshape(CONV_W, LT, P).transpose(2, 1, 0),
        "lru_vec": np.stack([i[n][0][:D_LRU].reshape(LT, P).T for n in ("conv_b", "b_r", "b_i", "lru_lambda", "out_norm_g")], 1),
        "w_r": i["w_r"][0],
        "w_i": i["w_i"][0],
        "state_conv": i["state_conv"][0].transpose(2, 0, 1).reshape(LT, P, NS, 3).transpose(1, 0, 2, 3),
        "state_lru": i["state_lru"][0].T.reshape(LT, P, NS).transpose(1, 0, 2),
        "ssm_par": twice(np.stack([i[n][0].T for n in ("ssm_lambda_re", "ssm_lambda_im", "ssm_log_dt")], 1)),
        "ssm_bc": np.stack([np.concatenate(x) for x in ((br, bi), (bi, br), (cr, ci), (ci, cr))], 1),
        "ssm_sign": np.repeat(np.float32([[-1], [1]]), STATE, 0),
        "ssm_turn": np.block([[0 * eye, eye], [-eye, 0 * eye]]),
        "ssm_d": np.tile(i["ssm_d"][0].reshape(GROUPS, GC).T, (CH, 1)),
        "ssm_x0": np.concatenate([i[n][0].transpose(2, 1, 0) for n in ("state_ssm_re", "state_ssm_im")]),
        "ssm_wide": np.stack([i["glu_b"][0], i["out_norm_g"][0][D_LRU:D_LRU + D_SSM]]),
        "glu_w": i["glu_w"][0],
        "yc_gain": i["out_norm_g"][0][D_LRU + D_SSM:],
        "w_out": i["w_out"][0].reshape(KT, P, D).transpose(1, 0, 2),
        "ones": np.ones((P, KC), np.float32),
        "cache_kT": tiles_of(i["cache_k"][0]).reshape(NS, KTS, P, PAIRS, P).transpose(0, 4, 1, 3, 2).reshape(NS, P, -1),
        "cache_v": tiles_of(i["cache_v"][0]).reshape(NS, KTS, P, D_ATT).transpose(0, 2, 1, 3).reshape(NS, P, -1),
        "bias_s": sample_bias(),
        "q_mask": sample_masks()[0],
        "w_mask": sample_masks()[1],
        "bias_p": prompt_bias(),
        "identity": np.eye(P, dtype=np.float32),
    }


def kernel(**inputs):
    import concourse.bacc as bacc
    from concourse.bass_utils import run_bass_kernel_spmd

    nc = bacc.Bacc("TRN2", target_bir_lowering=False, num_devices=1)
    arrays = {f"in_{n}": np.ascontiguousarray(a) for n, a in lay_out({n: np.asarray(a) for n, a in inputs.items()}).items()}
    t = {n[3:]: nc.dram_tensor(n, a.shape, F32, kind="ExternalInput").ap() for n, a in arrays.items()}
    for n, s in OUTS.items():
        t[n] = nc.dram_tensor(f"out_{n}", s, F32, kind="ExternalOutput").ap()
    for n, s in SCRATCH.items():
        t[n] = nc.dram_tensor(f"mid_{n}", s, F32, kind="Internal").ap()
    program(nc, t)
    r = run_bass_kernel_spmd(nc, [arrays], core_ids=[0]).results[0]
    o = {n: r[f"out_{n}"] for n in OUTS}
    return (
        o["y_p"].reshape(1, SEQ, D), o["y_s"].reshape(NS, TS, D),
        o["conv_p"].transpose(2, 1, 0).reshape(1, 1, 3, D_LRU), o["lru_p"].T.reshape(1, 1, D_LRU),
        o["ssm_re_p"].T.reshape(1, 1, GROUPS, STATE), o["ssm_im_p"].T.reshape(1, 1, GROUPS, STATE),
        o["k_p"].reshape(1, 1, KEEP, HEADS, DH), o["v_p"].reshape(1, 1, KEEP, HEADS, DH),
        o["conv_s"].transpose(2, 3, 1, 0).reshape(1, NS, 3, D_LRU), o["lru_s"].transpose(2, 1, 0).reshape(1, NS, D_LRU),
        o["ssm_re_s"].transpose(2, 1, 0).reshape(1, NS, GROUPS, STATE),
        o["ssm_im_s"].transpose(2, 1, 0).reshape(1, NS, GROUPS, STATE),
        o["k_s"].reshape(1, NS, TS, HEADS, DH), o["v_s"].reshape(1, NS, TS, HEADS, DH),
    )
```
